# Optimizing a Trainium2 kernel written in Bass

```python
import jax, jax.numpy as jnp
from jax import lax
import numpy as np

D_MODEL = 1024
BATCH = 1
SEQ = 1024
DEPTH = 1

CTX_LEN = 256
GRID_W = 64
N_MOD = 6
EPS = 1e-6

GLA_HEADS = 4
GLA_DK = 64
GLA_DV = 128
GLA_LR = 16
GLA_TAU = 16.0
GLA_CHUNK = 64

ML_HEADS = 4
ML_DH = 128
ML_CHUNK = 64
CONV_K = 3

N_GROUPS = 4
EXP_PER_GROUP = 8
N_EXPERTS = N_GROUPS * EXP_PER_GROUP
TOP_K = 2
D_EXPERT = 512
MOE_BLOCK = 128

GLA_QK_W = GLA_HEADS * GLA_DK
GLA_V_W = GLA_HEADS * GLA_DV
ML_W = ML_HEADS * ML_DH
MIX_W = GLA_V_W + ML_W

IN_SPLITS = (GLA_QK_W, GLA_QK_W, GLA_V_W, GLA_V_W, 2 * GLA_LR, 2 * ML_W, ML_W, ML_W, 2 * ML_HEADS, 2 * ML_HEADS)
IN_W = sum(IN_SPLITS)


def rmsnorm(x, g):
    xf = x.astype(jnp.float32)
    y = xf * lax.rsqrt(jnp.mean(xf * xf, axis=-1, keepdims=True) + EPS)
    return (y * g.astype(jnp.float32)).astype(x.dtype)

def modulate(h, shift, scale):
    return h * (1 + scale) + shift

def to_heads(t, n_heads):
    b, l, w = t.shape
    return t.reshape(b, l, n_heads, w // n_heads).transpose(0, 2, 1, 3)

def from_heads(t):
    b, h, l, d = t.shape
    return t.transpose(0, 2, 1, 3).reshape(b, l, h * d)

def head_rmsnorm(t, g):
    y = t * lax.rsqrt(jnp.mean(t * t, axis=-1, keepdims=True) + EPS)
    return from_heads(y) * g.astype(jnp.float32)

def to_chunks(t, c):
    b, h, l = t.shape[:3]
    return jnp.moveaxis(t.reshape((b, h, l // c, c) + t.shape[3:]), 2, 0)

def from_chunks(t):
    n, b, h, c = t.shape[:4]
    return jnp.moveaxis(t, 0, 2).reshape((b, h, n * c) + t.shape[4:])

def flip_time(t):
    return jnp.flip(t, axis=2)

def gla_chunked(q, k, v, log_a, s0):
    mask = jnp.tril(jnp.ones((GLA_CHUNK, GLA_CHUNK), dtype=bool))

    def step(s, inp):
        qc, kc, vc, gc = inp
        b = jnp.cumsum(gc, axis=2)
        q_t = qc * jnp.exp(b)
        k_t = kc * jnp.exp(-b)
        att = jnp.where(mask, jnp.einsum('bhtd,bhsd->bhts', q_t, k_t), 0.0)
        o = jnp.einsum('bhts,bhsv->bhtv', att, vc) + jnp.einsum('bhtd,bhdv->bhtv', q_t, s)
        b_end = b[:, :, -1]
        s_new = jnp.exp(b_end)[..., None] * s + jnp.einsum(
            'bhsd,bhsv->bhdv', kc * jnp.exp(b_end[:, :, None] - b), vc)
        return s_new, o

    s_fin, o = lax.scan(step, s0, tuple(to_chunks(t, GLA_CHUNK) for t in (q, k, v, log_a)))
    return from_chunks(o), s_fin

def mlstm_chunked(q, k, v, ig, lf, state0):
    mask = jnp.tril(jnp.ones((ML_CHUNK, ML_CHUNK), dtype=bool))

    def step(state, inp):
        s, n, m = state
        qc, kc, vc, ic, fc = inp
        a = jnp.cumsum(fc, axis=-1)
        dmat = jnp.where(mask, a[..., :, None] - a[..., None, :] + ic[..., None, :], -jnp.inf)
        inter = a + m[..., None]
        m_t = jnp.maximum(inter, jnp.max(dmat, axis=-1))
        w_inter = jnp.exp(inter - m_t)
        qk = jnp.einsum('bhtd,bhsd->bhts', qc, kc) * jnp.exp(dmat - m_t[..., None])
        num = jnp.einsum('bhts,bhsv->bhtv', qk, vc) + w_inter[..., None] * jnp.einsum('bhtd,bhdv->bhtv', qc, s)
        den = jnp.sum(qk, axis=-1) + w_inter * jnp.einsum('bhtd,bhd->bht', qc, n)
        h = num / jnp.maximum(jnp.abs(den), jnp.exp(-m_t))[..., None]
        a_end = a[..., -1]
        g = a_end[..., None] - a + ic
        m_new = jnp.maximum(a_end + m, jnp.max(g, axis=-1))
        decay = jnp.exp(a_end + m - m_new)
        kw = kc * jnp.exp(g - m_new[..., None])[..., None]
        s_new = decay[..., None, None] * s + jnp.einsum('bhsd,bhsv->bhdv', kw, vc)
        n_new = decay[..., None] * n + jnp.sum(kw, axis=2)
        return (s_new, n_new, m_new), h

    state_fin, h = lax.scan(step, state0, tuple(to_chunks(t, ML_CHUNK) for t in (q, k, v, ig, lf)))
    return from_chunks(h), state_fin

def bidir(scan_fn, ctx_dirs, lat_dirs, init):
    outs_c, outs_l = [], []
    for direction in range(2):
        fl = flip_time if direction == 1 else (lambda t: t)
        oc, st = scan_fn(*[fl(t) for t in ctx_dirs[direction]], init)
        ol, _ = scan_fn(*[fl(t) for t in lat_dirs[direction]], st)
        outs_c.append(fl(oc))
        outs_l.append(fl(ol))
    return outs_c[0] + outs_c[1], outs_l[0] + outs_l[1]

def grid_conv(t, w, b, grid_w):
    bsz, l, ch = t.shape
    rows = l // grid_w
    img = t.reshape(bsz, rows, grid_w, ch)
    y = lax.conv_general_dilated(img, w.astype(t.dtype), (1, 1), 'SAME',
                                 dimension_numbers=('NHWC', 'HWIO', 'NHWC'), feature_group_count=ch)
    return y.reshape(bsz, l, ch) + b

def prepare_stream(z, grid_w, gla_up_w, gla_up_b, conv_w, conv_b, ml_i_b, ml_f_b):
    bsz, l, _ = z.shape
    zf = z.astype(jnp.float32)
    idx = np.cumsum(IN_SPLITS)[:-1].tolist()
    gq, gk, gv, gg, glr, mqk, mv, mo, mi, mf = jnp.split(zf, idx, axis=-1)
    gla_q = to_heads(gq, GLA_HEADS) * (GLA_DK ** -0.5)
    gla_k = to_heads(gk, GLA_HEADS)
    gla_v = to_heads(gv, GLA_HEADS)
    gate_logits = jnp.einsum('blrk,rkn->blrn', glr.reshape(bsz, l, 2, GLA_LR), gla_up_w) + gla_up_b
    log_a = jax.nn.log_sigmoid(gate_logits) / GLA_TAU
    gla_dirs = tuple((gla_q, gla_k, gla_v, to_heads(log_a[:, :, d], GLA_HEADS)) for d in range(2))
    qk = jax.nn.silu(grid_conv(mqk, conv_w, conv_b, grid_w))
    mq, mk = jnp.split(qk, 2, axis=-1)
    ml_q = to_heads(mq, ML_HEADS)
    ml_k = to_heads(mk, ML_HEADS) * (ML_DH ** -0.5)
    ml_v = to_heads(mv, ML_HEADS)
    ig = (mi.reshape(bsz, l, 2, ML_HEADS) + ml_i_b).transpose(2, 0, 3, 1)
    lf = jax.nn.log_sigmoid(mf.reshape(bsz, l, 2, ML_HEADS) + ml_f_b).transpose(2, 0, 3, 1)
    ml_dirs = tuple((ml_q, ml_k, ml_v, ig[d], lf[d]) for d in range(2))
    return gla_dirs, ml_dirs, gg, mo

def mixer_output(gla_h, ml_h, gg, mo, gla_norm_g, ml_norm_g, w_out, dtype):
    gla_o = head_rmsnorm(gla_h, gla_norm_g) * jax.nn.silu(gg)
    ml_o = jax.nn.sigmoid(mo) * head_rmsnorm(ml_h, ml_norm_g)
    return jnp.concatenate([gla_o, ml_o], axis=-1).astype(dtype) @ w_out

def hier_moe(h, rg_w, rg_b, re_w, re_b, e_w_in, e_w_out):
    bsz, l, d = h.shape
    t = bsz * l
    tok = h.reshape(t, d)
    g_logits = (tok @ rg_w + rg_b).astype(jnp.float32)
    p_group = jax.nn.softmax(g_logits, axis=-1)
    g_idx = jnp.argmax(g_logits, axis=-1)
    g_w = jnp.take_along_axis(p_group, g_idx[:, None], axis=-1)
    e_logits = (tok @ re_w + re_b).astype(jnp.float32).reshape(t, N_GROUPS, EXP_PER_GROUP)
    e_in_group = jnp.take_along_axis(e_logits, g_idx[:, None, None], axis=1)[:, 0]
    top_v, top_i = lax.top_k(e_in_group, TOP_K)
    weights = g_w * jax.nn.softmax(top_v, axis=-1)
    expert_ids = (g_idx[:, None] * EXP_PER_GROUP + top_i).reshape(-1)
    n_assign = t * TOP_K
    order = jnp.argsort(expert_ids)
    sorted_e = expert_ids[order]
    token_of = order // TOP_K
    counts = jnp.bincount(expert_ids, length=N_EXPERTS)
    padded = (counts + MOE_BLOCK - 1) // MOE_BLOCK * MOE_BLOCK
    pad_end = jnp.cumsum(padded)
    pad_start = pad_end - padded
    start = jnp.cumsum(counts) - counts
    dest = pad_start[sorted_e] + jnp.arange(n_assign) - start[sorted_e]
    n_blocks = (n_assign + MOE_BLOCK - 1) // MOE_BLOCK + N_EXPERTS
    buf = jnp.zeros((n_blocks * MOE_BLOCK, d), tok.dtype).at[dest].set(tok[token_of])
    block_e = jnp.minimum(jnp.searchsorted(pad_end, jnp.arange(n_blocks) * MOE_BLOCK, side='right'), N_EXPERTS - 1)

    def expert_block(args):
        xb, e = args
        gate, up = jnp.split(xb @ e_w_in[e], 2, axis=-1)
        return (jax.nn.silu(gate) * up) @ e_w_out[e]

    yb = lax.map(expert_block, (buf.reshape(n_blocks, MOE_BLOCK, d), block_e)).reshape(-1, d)
    y = yb[dest] * weights.reshape(-1)[order][:, None].astype(yb.dtype)
    out = jax.ops.segment_sum(y, token_of, num_segments=t)
    return out.reshape(bsz, l, d)

def hybrid_layer(x, ctx, c, c_ctx, ada_w, ada_b, norm1_g, w_in, gla_up_w, gla_up_b, gla_norm_g,
                 ml_conv_w, ml_conv_b, ml_i_b, ml_f_b, ml_norm_g, w_out, norm2_g,
                 rg_w, rg_b, re_w, re_b, e_w_in, e_w_out, update_ctx):
    bsz = x.shape[0]
    mod_x = (jax.nn.silu(c) @ ada_w + ada_b)[:, None, :]
    mod_c = (jax.nn.silu(c_ctx) @ ada_w + ada_b)[None, None, :]
    sh1x, sc1x, g1x, sh2x, sc2x, g2x = jnp.split(mod_x, N_MOD, axis=-1)
    sh1c, sc1c, g1c, sh2c, sc2c, g2c = jnp.split(mod_c, N_MOD, axis=-1)

    zx = modulate(rmsnorm(x, norm1_g), sh1x, sc1x) @ w_in
    zc = modulate(rmsnorm(ctx, norm1_g), sh1c, sc1c) @ w_in
    gla_c, ml_c, gg_c, mo_c = prepare_stream(zc, zc.shape[1], gla_up_w, gla_up_b, ml_conv_w, ml_conv_b, ml_i_b, ml_f_b)
    gla_x, ml_x, gg_x, mo_x = prepare_stream(zx, GRID_W, gla_up_w, gla_up_b, ml_conv_w, ml_conv_b, ml_i_b, ml_f_b)
    gla_init = jnp.zeros((bsz, GLA_HEADS, GLA_DK, GLA_DV), jnp.float32)
    ml_init = (jnp.zeros((bsz, ML_HEADS, ML_DH, ML_DH), jnp.float32),
               jnp.zeros((bsz, ML_HEADS, ML_DH), jnp.float32),
               jnp.zeros((bsz, ML_HEADS), jnp.float32))
    gla_hc, gla_hx = bidir(gla_chunked, gla_c, gla_x, gla_init)
    ml_hc, ml_hx = bidir(mlstm_chunked, ml_c, ml_x, ml_init)
    x = x + g1x * mixer_output(gla_hx, ml_hx, gg_x, mo_x, gla_norm_g, ml_norm_g, w_out, x.dtype)

    x = x + g2x * hier_moe(modulate(rmsnorm(x, norm2_g), sh2x, sc2x), rg_w, rg_b, re_w, re_b, e_w_in, e_w_out)

    if update_ctx:
        ctx = ctx + g1c * mixer_output(gla_hc, ml_hc, gg_c, mo_c, gla_norm_g, ml_norm_g, w_out, ctx.dtype)
        ctx = ctx + g2c * hier_moe(modulate(rmsnorm(ctx, norm2_g), sh2c, sc2c), rg_w, rg_b, re_w, re_b, e_w_in, e_w_out)
    return x, ctx

def first_inputs(seed: int = 0) -> dict:
    key = jax.random.key(seed)
    ks = jax.random.split(key, 26)
    nrm = lambda k, shape, s: jax.random.normal(k, shape, jnp.float32) * s
    L = DEPTH
    return {
        "x": nrm(ks[0], (BATCH, SEQ, D_MODEL), 1.0),
        "c": nrm(ks[1], (BATCH, D_MODEL), 1.0),
        "ctx": nrm(ks[2], (BATCH, CTX_LEN, D_MODEL), 1.0),
        "c_ctx": nrm(ks[3], (D_MODEL,), 1.0),
        "ada_w": nrm(ks[4], (L, D_MODEL, N_MOD * D_MODEL), D_MODEL ** -0.5),
        "ada_b": nrm(ks[5], (L, N_MOD * D_MODEL), 0.02),
        "norm1_g": 1.0 + nrm(ks[6], (L, D_MODEL), 0.02),
        "w_in": nrm(ks[7], (L, D_MODEL, IN_W), D_MODEL ** -0.5),
        "gla_up_w": nrm(ks[8], (L, 2, GLA_LR, GLA_QK_W), GLA_LR ** -0.5),
        "gla_up_b": nrm(ks[9], (L, 2, GLA_QK_W), 0.1),
        "gla_norm_g": 1.0 + nrm(ks[10], (L, GLA_V_W), 0.02),
        "ml_conv_w": nrm(ks[11], (L, CONV_K, CONV_K, 1, 2 * ML_W), 1.0 / CONV_K),
        "ml_conv_b": nrm(ks[12], (L, 2 * ML_W), 0.02),
        "ml_i_b": nrm(ks[13], (L, 2, ML_HEADS), 0.1),
        "ml_f_b": 3.0 + nrm(ks[14], (L, 2, ML_HEADS), 0.5),
        "ml_norm_g": 1.0 + nrm(ks[15], (L, ML_W), 0.02),
        "w_out": nrm(ks[16], (L, MIX_W, D_MODEL), MIX_W ** -0.5),
        "norm2_g": 1.0 + nrm(ks[17], (L, D_MODEL), 0.02),
        "router_group_w": nrm(ks[18], (L, D_MODEL, N_GROUPS), D_MODEL ** -0.5),
        "router_group_b": nrm(ks[19], (L, N_GROUPS), 0.01),
        "router_expert_w": nrm(ks[20], (L, D_MODEL, N_EXPERTS), D_MODEL ** -0.5),
        "router_expert_b": nrm(ks[21], (L, N_EXPERTS), 0.01),
        "expert_w_in": nrm(ks[22], (L, N_EXPERTS, D_MODEL, 2 * D_EXPERT), D_MODEL ** -0.5),
        "expert_w_out": nrm(ks[23], (L, N_EXPERTS, D_EXPERT, D_MODEL), D_EXPERT ** -0.5),
        "final_norm_g": 1.0 + nrm(ks[24], (D_MODEL,), 0.02),
    }

def first_block(x, c, ctx, c_ctx, ada_w, ada_b, norm1_g, w_in, gla_up_w, gla_up_b, gla_norm_g,
              ml_conv_w, ml_conv_b, ml_i_b, ml_f_b, ml_norm_g, w_out, norm2_g,
              router_group_w, router_group_b, router_expert_w, router_expert_b,
              expert_w_in, expert_w_out, final_norm_g):
    for layer in range(DEPTH):
        x, ctx = hybrid_layer(
            x, ctx, c, c_ctx, ada_w[layer], ada_b[layer], norm1_g[layer], w_in[layer],
            gla_up_w[layer], gla_up_b[layer], gla_norm_g[layer],
            ml_conv_w[layer], ml_conv_b[layer], ml_i_b[layer], ml_f_b[layer], ml_norm_g[layer],
            w_out[layer], norm2_g[layer],
            router_group_w[layer], router_group_b[layer], router_expert_w[layer], router_expert_b[layer],
            expert_w_in[layer], expert_w_out[layer], update_ctx=(layer < DEPTH - 1))
    return rmsnorm(x, final_norm_g)


MIX_WIDTH = 512
N_BRANCH = 4
MLA_HEADS = 8
QK_NOPE = 64
QK_ROPE = 32
V_HEAD = 64
Q_LORA = 384
KV_LORA = 256
ROPE_THETA = 10000.0
Q_BLOCK = 128
POOL_WINDOWS = (2, 4, 8, 16)
POOL_GROUP = MIX_WIDTH // 4
SSD_HEADS = 8
SSD_HEADDIM = 64
SSD_GROUPS = 2
SSD_STATE = 64
SSD_CHUNK = 128
CONV_WIDTH = 4
SSD_XBC = SSD_HEADS * SSD_HEADDIM + 2 * SSD_GROUPS * SSD_STATE
LRU_BLOCKS = 8
LRU_BLOCK = MIX_WIDTH // LRU_BLOCKS
LRU_C = 8.0
D_FF = 4 * D_MODEL
PLE_DIM = 256

SPLIT_SIZES = (Q_LORA, KV_LORA, QK_ROPE,
               MIX_WIDTH,
               MIX_WIDTH, SSD_XBC, SSD_HEADS,
               MIX_WIDTH, MIX_WIDTH,
               N_BRANCH * D_MODEL)
IN_COLS = sum(SPLIT_SIZES)


def _split_points():
    pts, acc = [], 0
    for s in SPLIT_SIZES[:-1]:
        acc += s
        pts.append(acc)
    return pts

def rmsnorm_2(x, g):
    x32 = x.astype(jnp.float32)
    y = x32 * lax.rsqrt(jnp.mean(x32 * x32, axis=-1, keepdims=True) + EPS)
    return (y * g.astype(jnp.float32)).astype(x.dtype)

def causal_dwconv(x, w, b):
    c = x.shape[-1]
    y = lax.conv_general_dilated(x, w[:, None, :].astype(x.dtype), window_strides=(1,),
                                 padding=[(CONV_WIDTH - 1, 0)],
                                 dimension_numbers=('NWC', 'WIO', 'NWC'),
                                 feature_group_count=c)
    return y + b.astype(x.dtype)

def rope_tables(positions):
    inv = 1.0 / (ROPE_THETA ** (jnp.arange(0, QK_ROPE, 2, dtype=jnp.float32) / QK_ROPE))
    ang = positions.astype(jnp.float32)[..., None] * inv
    return jnp.cos(ang), jnp.sin(ang)

def apply_rope(x, cos, sin):
    x32 = x.astype(jnp.float32)
    x1, x2 = jnp.split(x32, 2, axis=-1)
    out = jnp.concatenate([x1 * cos - x2 * sin, x2 * cos + x1 * sin], axis=-1)
    return out.astype(x.dtype)

def mla_mixer(c_q, c_kv, k_r, cos, sin, q_norm, w_uq, kv_norm, w_ukv):
    b, s, _ = c_q.shape
    q = (rmsnorm_2(c_q, q_norm) @ w_uq).reshape(b, s, MLA_HEADS, QK_NOPE + QK_ROPE)
    q_nope = q[..., :QK_NOPE]
    q_rope = apply_rope(q[..., QK_NOPE:], cos[:, :, None], sin[:, :, None])
    kv = (rmsnorm_2(c_kv, kv_norm) @ w_ukv).reshape(b, s, MLA_HEADS, QK_NOPE + V_HEAD)
    k_nope, v = kv[..., :QK_NOPE], kv[..., QK_NOPE:]
    k_rope = apply_rope(k_r, cos, sin)
    scale = (QK_NOPE + QK_ROPE) ** -0.5
    outs = []
    for blk in range(s // Q_BLOCK):
        q0, kend = blk * Q_BLOCK, (blk + 1) * Q_BLOCK
        sc = (jnp.einsum('bqhd,bkhd->bhqk', q_nope[:, q0:kend], k_nope[:, :kend])
              + jnp.einsum('bqhd,bkd->bhqk', q_rope[:, q0:kend], k_rope[:, :kend]))
        sc = sc.astype(jnp.float32) * scale
        qi = q0 + jnp.arange(Q_BLOCK)[:, None]
        ki = jnp.arange(kend)[None, :]
        sc = jnp.where(ki <= qi, sc, -jnp.inf)
        pr = jax.nn.softmax(sc, axis=-1).astype(v.dtype)
        outs.append(jnp.einsum('bhqk,bkhd->bqhd', pr, v[:, :kend]))
    o = jnp.concatenate(outs, axis=1)
    return o.reshape(b, s, MLA_HEADS * V_HEAD)

def pool_mixer(u, w_pool, pool_scale):
    b, s, _ = u.shape
    u32 = u.astype(jnp.float32)
    maxw = max(POOL_WINDOWS)
    cs = jnp.pad(jnp.cumsum(u32, axis=1), ((0, 0), (maxw, 0), (0, 0)))
    t = jnp.arange(s)
    groups = []
    for g, w in enumerate(POOL_WINDOWS):
        sl = slice(g * POOL_GROUP, (g + 1) * POOL_GROUP)
        win_sum = cs[:, maxw:, sl] - cs[:, maxw - w:maxw - w + s, sl]
        count = jnp.minimum(t + 1, w).astype(jnp.float32)[None, :, None]
        groups.append(win_sum / count - u32[..., sl])
    d = jnp.stack(groups, axis=2).astype(u.dtype)
    y = jnp.einsum('bsgc,gcd->bsgd', d, w_pool).reshape(b, s, MIX_WIDTH)
    return y * pool_scale

def segsum(a):
    t = a.shape[-1]
    cs = jnp.cumsum(a, axis=-1)
    diff = cs[..., :, None] - cs[..., None, :]
    mask = jnp.tril(jnp.ones((t, t), dtype=bool))
    return jnp.where(mask, diff, -jnp.inf)

def ssd_mixer(z, xbc, dt, conv_w, conv_b, dt_bias, a_log, d_skip, norm_g):
    b, s, _ = z.shape
    nc, lc, g, r, n, hp = s // SSD_CHUNK, SSD_CHUNK, SSD_GROUPS, SSD_HEADS // SSD_GROUPS, SSD_STATE, SSD_HEADDIM
    xbc = jax.nn.silu(causal_dwconv(xbc, conv_w, conv_b)).astype(jnp.float32)
    xs = xbc[..., :MIX_WIDTH]
    bm = xbc[..., MIX_WIDTH:MIX_WIDTH + g * n].reshape(b, nc, lc, g, n)
    cm = xbc[..., MIX_WIDTH + g * n:].reshape(b, nc, lc, g, n)
    dt = jax.nn.softplus(dt.astype(jnp.float32) + dt_bias.astype(jnp.float32))
    a_head = -jnp.exp(a_log.astype(jnp.float32))
    x = xs.reshape(b, nc, lc, g, r, hp)
    xdt = x * dt.reshape(b, nc, lc, g, r)[..., None]
    a = (dt * a_head).reshape(b, nc, lc, g, r).transpose(0, 3, 4, 1, 2)
    a_cs = jnp.cumsum(a, axis=-1)
    lmat = jnp.exp(segsum(a))
    cb = jnp.einsum('bclgn,bcsgn->bgcls', cm, bm)
    y_diag = jnp.einsum('bgrcls,bcsgrp->bclgrp', cb[:, :, None] * lmat, xdt)
    decay_states = jnp.exp(a_cs[..., -1:] - a_cs)
    states = jnp.einsum('bclgn,bgrcl,bclgrp->bcgrpn', bm, decay_states, xdt)
    states = jnp.concatenate([jnp.zeros_like(states[:, :1]), states], axis=1)
    chunk_a = jnp.pad(a_cs[..., -1], ((0, 0), (0, 0), (0, 0), (1, 0)))
    decay_chunk = jnp.exp(segsum(chunk_a))
    states = jnp.einsum('bgrzc,bcgrpn->bzgrpn', decay_chunk, states)[:, :-1]
    y_off = jnp.einsum('bclgn,bcgrpn,bgrcl->bclgrp', cm, states, jnp.exp(a_cs))
    y = (y_diag + y_off).reshape(b, s, SSD_HEADS, hp) \
        + xs.reshape(b, s, SSD_HEADS, hp) * d_skip.astype(jnp.float32)[:, None]
    y = y.reshape(b, s, MIX_WIDTH) * jax.nn.silu(z.astype(jnp.float32))
    return rmsnorm_2(y, norm_g).astype(z.dtype)

def rglru_mixer(gate_in, x_in, conv_w, conv_b, w_a, b_a, w_i, b_i, lam):
    b, s, _ = x_in.shape
    gate = jax.nn.gelu(gate_in)
    xc = causal_dwconv(x_in, conv_w, conv_b)
    xb = xc.reshape(b, s, LRU_BLOCKS, LRU_BLOCK)
    r_t = jax.nn.sigmoid((jnp.einsum('bshi,hij->bshj', xb, w_a).reshape(b, s, MIX_WIDTH) + b_a).astype(jnp.float32))
    i_t = jax.nn.sigmoid((jnp.einsum('bshi,hij->bshj', xb, w_i).reshape(b, s, MIX_WIDTH) + b_i).astype(jnp.float32))
    log_a = -LRU_C * r_t * jax.nn.softplus(-lam.astype(jnp.float32))
    a_t = jnp.exp(log_a)
    mult = jnp.sqrt(-jnp.expm1(2.0 * log_a))
    u = xc.astype(jnp.float32) * i_t * mult

    def combine(lhs, rhs):
        a1, b1 = lhs
        a2, b2 = rhs
        return a1 * a2, a2 * b1 + b2

    _, h = lax.associative_scan(combine, (a_t, u), axis=1)
    return h.astype(x_in.dtype) * gate

def second_inputs(seed: int = 0) -> dict:
    key = jax.random.key(seed)
    ks = iter(jax.random.split(key, 48))
    f32 = jnp.float32

    def nrm(shape, fan_in):
        return jax.random.normal(next(ks), shape, f32) * (fan_in ** -0.5)

    def gain(shape):
        return 1.0 + 0.05 * jax.random.normal(next(ks), shape, f32)

    def small(shape):
        return 0.01 * jax.random.normal(next(ks), shape, f32)

    L = DEPTH
    x = jax.random.normal(next(ks), (BATCH, SEQ, D_MODEL), f32)
    p = jax.random.normal(next(ks), (DEPTH, BATCH, SEQ, PLE_DIM), f32)
    offs = jax.random.randint(next(ks), (BATCH, 1), 0, 1024, dtype=jnp.int32)
    positions = (offs + jnp.arange(SEQ, dtype=jnp.int32)[None, :]).astype(jnp.int32)
    dt0 = jnp.exp(jax.random.uniform(next(ks), (L, SSD_HEADS), f32, np.log(1e-3), np.log(1e-1)))
    dt_bias = dt0 + jnp.log(-jnp.expm1(-dt0))
    a_log = jnp.log(jax.random.uniform(next(ks), (L, SSD_HEADS), f32, 1.0, 16.0))
    a_pow = jax.random.uniform(next(ks), (L, MIX_WIDTH), f32, 0.9, 0.999) ** (1.0 / LRU_C)
    lam = jnp.log(a_pow) - jnp.log1p(-a_pow)
    return {
        "x": x,
        "p": p,
        "positions": positions,
        "g_mix": gain((L, D_MODEL)),
        "w_in": nrm((L, D_MODEL, IN_COLS), D_MODEL),
        "q_norm": gain((L, Q_LORA)),
        "w_uq": nrm((L, Q_LORA, MLA_HEADS * (QK_NOPE + QK_ROPE)), Q_LORA),
        "kv_norm": gain((L, KV_LORA)),
        "w_ukv": nrm((L, KV_LORA, MLA_HEADS * (QK_NOPE + V_HEAD)), KV_LORA),
        "w_pool": nrm((L, 4, POOL_GROUP, POOL_GROUP), POOL_GROUP),
        "pool_scale": 1.0 + 0.1 * jax.random.normal(next(ks), (L, MIX_WIDTH), f32),
        "ssd_conv_w": nrm((L, CONV_WIDTH, SSD_XBC), CONV_WIDTH),
        "ssd_conv_b": small((L, SSD_XBC)),
        "ssd_dt_bias": dt_bias,
        "ssd_a_log": a_log,
        "ssd_d": gain((L, SSD_HEADS)),
        "ssd_norm": gain((L, MIX_WIDTH)),
        "lru_conv_w": nrm((L, CONV_WIDTH, MIX_WIDTH), CONV_WIDTH),
        "lru_conv_b": small((L, MIX_WIDTH)),
        "lru_w_a": nrm((L, LRU_BLOCKS, LRU_BLOCK, LRU_BLOCK), LRU_BLOCK),
        "lru_b_a": small((L, MIX_WIDTH)),
        "lru_w_i": nrm((L, LRU_BLOCKS, LRU_BLOCK, LRU_BLOCK), LRU_BLOCK),
        "lru_b_i": small((L, MIX_WIDTH)),
        "lru_lambda": lam,
        "w_branch": nrm((L, N_BRANCH, MIX_WIDTH, D_MODEL), MIX_WIDTH),
        "w_out": nrm((L, D_MODEL, D_MODEL), D_MODEL),
        "g_mlp": gain((L, D_MODEL)),
        "w_ff1": nrm((L, D_MODEL, D_FF), D_MODEL),
        "w_ff2": nrm((L, D_FF, D_MODEL), D_FF),
        "g_ple": gain((L, D_MODEL)),
        "w_ple_gate": nrm((L, D_MODEL, D_MODEL), D_MODEL),
        "w_ple": nrm((L, PLE_DIM, D_MODEL), PLE_DIM),
        "g_final": gain((D_MODEL,)),
    }

def second_block(x, p, positions, g_mix, w_in, q_norm, w_uq, kv_norm, w_ukv, w_pool, pool_scale,
              ssd_conv_w, ssd_conv_b, ssd_dt_bias, ssd_a_log, ssd_d, ssd_norm,
              lru_conv_w, lru_conv_b, lru_w_a, lru_b_a, lru_w_i, lru_b_i, lru_lambda,
              w_branch, w_out, g_mlp, w_ff1, w_ff2, g_ple, w_ple_gate, w_ple, g_final):
    b, s, _ = x.shape
    cos, sin = rope_tables(positions)
    pts = _split_points()
    for l in range(DEPTH):
        h = rmsnorm_2(x, g_mix[l])
        u = h @ w_in[l]
        c_q, c_kv, k_r, u_pool, z, xbc, dt, lru_g, lru_x, gates = jnp.split(u, pts, axis=-1)
        y_a = mla_mixer(c_q, c_kv, k_r, cos, sin, q_norm[l], w_uq[l], kv_norm[l], w_ukv[l])
        y_b = pool_mixer(u_pool, w_pool[l], pool_scale[l])
        y_c = ssd_mixer(z, xbc, dt, ssd_conv_w[l], ssd_conv_b[l], ssd_dt_bias[l], ssd_a_log[l],
                        ssd_d[l], ssd_norm[l])
        y_d = rglru_mixer(lru_g, lru_x, lru_conv_w[l], lru_conv_b[l], lru_w_a[l], lru_b_a[l],
                          lru_w_i[l], lru_b_i[l], lru_lambda[l])
        gates = jax.nn.sigmoid(gates.reshape(b, s, N_BRANCH, D_MODEL))
        merged = (gates[:, :, 0] * (y_a @ w_branch[l, 0])
                  + gates[:, :, 1] * (y_b @ w_branch[l, 1])
                  + gates[:, :, 2] * (y_c @ w_branch[l, 2])
                  + gates[:, :, 3] * (y_d @ w_branch[l, 3]))
        x = x + merged @ w_out[l]
        h2 = rmsnorm_2(x, g_mlp[l])
        x = x + jnp.square(jax.nn.relu(h2 @ w_ff1[l])) @ w_ff2[l]
        ple_gate = jax.nn.sigmoid(rmsnorm_2(x, g_ple[l]) @ w_ple_gate[l])
        x = x + (p[l] @ w_ple[l]) * ple_gate
    return rmsnorm_2(x, g_final)


def setup_inputs(seed=0):
    out = dict(first_inputs(seed))
    for name, value in second_inputs(seed + 1).items():
        if name != "x":
            out[name + "_2"] = value
    return out


def reference(
    x, c, ctx, c_ctx, ada_w, ada_b, norm1_g, w_in, gla_up_w, gla_up_b, gla_norm_g, ml_conv_w,
    ml_conv_b, ml_i_b, ml_f_b, ml_norm_g, w_out, norm2_g, router_group_w, router_group_b,
    router_expert_w, router_expert_b, expert_w_in, expert_w_out, final_norm_g, p_2, positions_2,
    g_mix_2, w_in_2, q_norm_2, w_uq_2, kv_norm_2, w_ukv_2, w_pool_2, pool_scale_2, ssd_conv_w_2,
    ssd_conv_b_2, ssd_dt_bias_2, ssd_a_log_2, ssd_d_2, ssd_norm_2, lru_conv_w_2, lru_conv_b_2,
    lru_w_a_2, lru_b_a_2, lru_w_i_2, lru_b_i_2, lru_lambda_2, w_branch_2, w_out_2, g_mlp_2,
    w_ff1_2, w_ff2_2, g_ple_2, w_ple_gate_2, w_ple_2, g_final_2,
):
    x = first_block(
        x, c, ctx, c_ctx, ada_w, ada_b, norm1_g, w_in, gla_up_w, gla_up_b, gla_norm_g,
        ml_conv_w, ml_conv_b, ml_i_b, ml_f_b, ml_norm_g, w_out, norm2_g, router_group_w,
        router_group_b, router_expert_w, router_expert_b, expert_w_in, expert_w_out,
        final_norm_g,
    )
    return second_block(
        x, p_2, positions_2, g_mix_2, w_in_2, q_norm_2, w_uq_2, kv_norm_2, w_ukv_2, w_pool_2,
        pool_scale_2, ssd_conv_w_2, ssd_conv_b_2, ssd_dt_bias_2, ssd_a_log_2, ssd_d_2,
        ssd_norm_2, lru_conv_w_2, lru_conv_b_2, lru_w_a_2, lru_b_a_2, lru_w_i_2, lru_b_i_2,
        lru_lambda_2, w_branch_2, w_out_2, g_mlp_2, w_ff1_2, w_ff2_2, g_ple_2, w_ple_gate_2,
        w_ple_2, g_final_2,
    )


_drawn_inputs = setup_inputs


def setup_inputs(seed=0):
    import zlib

    import numpy as np

    out = dict(_drawn_inputs(seed))
    spreads = {}
    factors = {'ml_conv_b': 8.0,
     'ml_i_b': 8.0,
     'ml_norm_g': 3.014,
     'router_group_b': 3.49,
     'router_expert_b': 4.253,
     'q_norm_2': 8.0,
     'kv_norm_2': 8.0,
     'ssd_conv_b_2': 48.168,
     'ssd_d_2': 39.336,
     'lru_conv_b_2': 12.986,
     'lru_b_a_2': 200.0,
     'lru_b_i_2': 64.0,
     'g_ple_2': 200.0,
     'pool_scale_2': 5.961,
     'ssd_dt_bias_2': 64.0,
     'ssd_a_log_2': 8.0,
     'ssd_norm_2': 8.0,
     'lru_w_a_2': 2.925,
     'g_mlp_2': 3.628}
    for name, (base, spread) in spreads.items():
        noise = np.random.default_rng([zlib.crc32(name.encode()), seed]).standard_normal(out[name].shape)
        drawn = base * np.exp(spread * noise) if base else spread * noise
        out[name] = __import__('jax').numpy.asarray(drawn.astype(out[name].dtype))
    for name, factor in factors.items():
        out[name] = (out[name] * factor).astype(out[name].dtype)
    return out
```

```python
import math
from contextlib import ExitStack

import numpy as np

import concourse.bass as bass
from concourse import mybir

F32 = mybir.dt.float32
I32 = mybir.dt.int32
F32R = mybir.dt.float32r
U32 = mybir.dt.uint32
ALU = mybir.AluOpType
ACT = mybir.ActivationFunctionType
AX = mybir.AxisListType

P = 128
D = 1024
KD = D // P
SEQ, CTX = 1024, 256
TOT = CTX + SEQ
EPS = 1e-6
CH = 128
NCC, NCX = CTX // CH, SEQ // CH
NCH = NCC + NCX
GRID_W = 64
NEG = -1e30
BANK = 512
NE, NG, EG, DE = 32, 4, 8, 512
SLOT = 128
NBLK = SEQ * 2 // SLOT + NE


class Stage:

    def __init__(self, nc, name):
        self.nc, self.name, self.stack, self.used = nc, name, ExitStack(), []

    def __enter__(self):
        return self

    def __exit__(self, *a):
        if self.used and a[0] is None:
            self.nc.clear_and_free_semaphores(self.used)
            self.nc.all_engine_barrier()
        return self.stack.__exit__(*a)

    def sb(self, name, shape, dt=F32):
        return self.stack.enter_context(self.nc.sbuf_tensor(f"{self.name}_{name}", shape, dt))

    def ps(self, name, shape=(P, BANK)):
        return self.stack.enter_context(self.nc.psum_tensor(f"{self.name}_{name}", list(shape), F32))

    def sem(self, name):
        self.used.append(self.nc.alloc_semaphore(f"{self.name}_{name}"))
        return self.used[-1]

    def sems(self, name, n):
        return [self.sem(f"{name}{i}") for i in range(n)]


class Steps:

    def __init__(self, eng, sem, n=0):
        self.eng, self.sem, self.n = eng, sem, n

    def then(self, ins):
        ins.then_inc(self.sem, 1)
        self.n = self.n + 1
        self.eng.wait_ge(self.sem, self.n)


def chunks_of(total, step=BANK):
    return [(a, min(step, total - a)) for a in range(0, total, step)]


def load(nc, name, pairs):
    with Stage(nc, name) as s:
        loaded = s.sem("loaded")
        with nc.Block() as block:
            @block.sync
            def _(sp):
                for dst, src in pairs:
                    sp.dma_start(dst, src).then_inc(loaded, 16)
                sp.wait_ge(loaded, 16 * len(pairs))


def product3(nc, out, w, x, first, last):
    nc.tensor.matmul(out, w[0], x[0], start=first, stop=False)
    nc.tensor.matmul(out, w[0], x[1], start=False, stop=False)
    return nc.tensor.matmul(out, w[1], x[0], start=False, stop=last)


def split(nc, name, t, high, rest, n):
    with Stage(nc, name) as s:
        rounded, left = s.sem("rounded"), s.sem("left")
        with nc.Block() as block:
            @block.scalar
            def _(act):
                for k in range(n):
                    nc.scalar.activation(high[:, k], t[:, k], ACT.Copy).then_inc(rounded, 1)

            @block.vector
            def _(dve):
                for k in range(n):
                    dve.wait_ge(rounded, k + 1)
                    nc.vector.tensor_tensor(rest[:, k], t[:, k], high[:, k].bitcast(F32), ALU.subtract).then_inc(left, 1)
                dve.wait_ge(left, n)


class Weights:

    def __init__(self, nc, s, w, size, turns):
        self.nc, self.w, self.turns = nc, w, turns
        self.raw = [s.sb(f"raw{j}", [P, size]) for j in range(2)]
        self.high = [s.sb(f"high{j}", [P, size], F32R) for j in range(2)]
        self.one, self.filled = s.sb("one", [P, 1]), s.sem("filled")
        self.low = [s.sb(f"low{j}", [P, size], F32R) for j in range(2)]
        self.w_in, self.rounded, self.split, self.used = s.sems("w_in", 2), s.sem("rounded"), s.sems("split", 2), s.sems("used", 2)

    def load(self, sp):
        with sp.Fori(0, self.turns // 2) as i:
            for j in range(2):
                sp.wait_ge(self.split[j], i)
                sp.dma_start(self.raw[j][:], self.w[i * 2 + j]).then_inc(self.w_in[j], 16)

    def halve(self, pool):
        g = self.nc.gpsimd
        g.memset(self.one[:], 1.0).then_inc(self.filled, 1)
        pool.wait_ge(self.filled, 1)
        with pool.Fori(0, self.turns // 2) as i:
            for j in range(2):
                pool.wait_ge(self.w_in[j], i * 16 + 16)
                pool.wait_ge(self.used[j], i)
                g.tensor_tensor(self.high[j][:], self.raw[j][:], self.one[:].broadcast_to(self.raw[j].shape), ALU.mult).then_inc(self.rounded, 1)
                pool.wait_ge(self.rounded, i * 2 + j + 1)
                g.tensor_tensor(self.low[j][:], self.raw[j][:], self.high[j][:].bitcast(F32), ALU.subtract).then_inc(self.split[j], 1)

    def tile(self, j, k):
        return self.high[j][:, k * P:(k + 1) * P], self.low[j][:, k * P:(k + 1) * P]


def gemm(nc, name, w, kt, nt, rhs, total, evac, evac_on="scalar", out_dram=None, side_dram=None):
    cs = chunks_of(total)
    nb = len(cs)
    with Stage(nc, name) as s:
        W = Weights(nc, s, w, kt * P, nt)
        ob = [s.sb(f"o{j}", [P, total]) for j in range(2)] if out_dram is not None else None
        xb = [s.sb(f"x{j}", [P, total]) for j in range(2)] if side_dram is not None else None
        ps = [[s.ps(f"p{j}_{c}") for c in range(nb)] for j in range(2)]
        summed, out_taken, stored, x_in = s.sems("summed", 2), s.sems("taken", 2), s.sems("stored", 2), s.sems("x_in", 2)
        with nc.Block() as block:
            @block.sync
            def _(sp):
                W.load(sp)

            @block.gpsimd
            def _(pool):
                W.halve(pool)

            @block.tensor
            def _(pe):
                with pe.Fori(0, nt // 2) as i:
                    for j in range(2):
                        pe.wait_ge(W.split[j], i + 1)
                        pe.wait_ge(out_taken[j], i * nb)
                        for c, (a, m) in enumerate(cs):
                            for k in range(kt):
                                mm = product3(nc, ps[j][c][:, 0:m], W.tile(j, k), rhs(k, a, m), k == 0, k == kt - 1)
                            mm.then_inc(summed[j] if c < nb - 1 else W.used[j], 1)

            def take(eng, ns, i):
                for j in range(2):
                    if ob:
                        eng.wait_ge(stored[j], i * 16)
                    if xb:
                        eng.wait_ge(x_in[j], i * 16 + 16)
                    for c, (a, m) in enumerate(cs):
                        if c < nb - 1:
                            eng.wait_ge(summed[j], i * (nb - 1) + c + 1)
                        else:
                            eng.wait_ge(W.used[j], i + 1)
                        evac(ns, ob[j][:, a:a + m] if ob else None, ps[j][c][:, 0:m], i * 2 + j, a, m,
                             xb[j][:, a:a + m] if xb else None).then_inc(out_taken[j], 1)

            if evac_on == "vector":
                @block.vector
                def _(dve):
                    with dve.Fori(0, nt // 2) as i:
                        take(dve, nc.vector, i)

            @block.scalar
            def _(act):
                if evac_on == "scalar" or ob or xb:
                    with act.Fori(0, nt // 2) as i:
                        if xb:
                            for j in range(2):
                                act.wait_ge(out_taken[j], i * nb)
                                act.dma_start(xb[j][:], side_dram[i * 2 + j]).then_inc(x_in[j], 16)
                        if evac_on == "scalar":
                            take(act, nc.scalar, i)
                        if ob:
                            for j in range(2):
                                act.wait_ge(out_taken[j], i * nb + nb)
                                act.dma_start(out_dram[i * 2 + j], ob[j][:]).then_inc(stored[j], 16)
                if ob:
                    for j in range(2):
                        act.wait_ge(stored[j], nt // 2 * 16)


def gemm_tokens(nc, name, w, groups, width, h, hl, t0, nt, out_dram):
    nj = 2 if groups % 2 == 0 else 1
    per, turns, half = nj * nt, groups // nj, KD * width // 2
    with Stage(nc, name) as s:
        wb = [s.sb(f"w{j}", [P, KD * width]) for j in range(nj)]
        wh = [s.sb(f"h{j}", [P, KD * width], F32R) for j in range(nj)]
        wl = [s.sb(f"l{j}", [P, KD * width], F32R) for j in range(nj)]
        ob = [s.sb(f"o{b}", [P, width]) for b in range(4)]
        ps = [s.ps(f"p{b}") for b in range(4)]
        w_in, summed, taken, stored = s.sems("w_in", nj), s.sems("summed", nj), s.sem("taken"), s.sems("stored", 4)
        rounded, parted = s.sem("rounded"), s.sem("parted")
        with nc.Block() as block:
            @block.sync
            def _(sp):
                with sp.Fori(0, turns) as i:
                    for j in range(nj):
                        sp.wait_ge(summed[j], i * nt)
                        for x in range(2):
                            sp.dma_start(wb[j][:, x * half:(x + 1) * half], w[i * nj + j][:, x * half:(x + 1) * half]).then_inc(w_in[j], 16)

            @block.gpsimd
            def _(pool):
                with pool.Fori(0, turns) as i:
                    for j in range(nj):
                        pool.wait_ge(w_in[j], i * 32 + 32)
                        for x in range(2):
                            part = slice(x * half, (x + 1) * half)
                            n = (i * nj + j) * 2 + x + 1
                            pool.wait_ge(rounded, n)
                            nc.gpsimd.tensor_tensor(wl[j][:, part], wb[j][:, part], wh[j][:, part].bitcast(F32), ALU.subtract).then_inc(parted, 1)

            @block.tensor
            def _(pe):
                with pe.Fori(0, turns) as i:
                    pe.wait_ge(taken, i * per)
                    for j in range(nj):
                        for t in range(nt):
                            n = j * nt + t
                            if n >= 4:
                                pe.wait_ge(taken, i * per + n - 3)
                            for k in range(KD):
                                if t == 0 and k % (KD // 2) == 0:
                                    pe.wait_ge(parted, (i * nj + j) * 2 + k // (KD // 2) + 1)
                                part, rows = slice(k * width, (k + 1) * width), slice(t0 + t * P, t0 + (t + 1) * P)
                                mm = product3(nc, ps[n % 4][:, 0:width], (h[:, k, rows], hl[:, k, rows]),
                                              (wh[j][:, part], wl[j][:, part]), k == 0, k == KD - 1)
                            mm.then_inc(summed[j], 1)

            @block.vector
            def _(dve):
                with dve.Fori(0, turns) as i:
                    for j in range(nj):
                        for t in range(nt):
                            n = j * nt + t
                            of = -(-(per - n % 4) // 4)
                            dve.wait_ge(stored[n % 4], (i * of + n // 4) * 16)
                            dve.wait_ge(summed[j], i * nt + t + 1)
                            nc.vector.tensor_copy(ob[n % 4][:], ps[n % 4][:, 0:width]).then_inc(taken, 1)

            @block.scalar
            def _(act):
                with act.Fori(0, turns) as i:
                    for j in range(nj):
                        act.wait_ge(w_in[j], i * 32 + 32)
                        for x in range(2):
                            nc.scalar.activation(wh[j][:, x * half:(x + 1) * half], wb[j][:, x * half:(x + 1) * half], ACT.Copy).then_inc(rounded, 1)
                    for j in range(nj):
                        for t in range(nt):
                            n = j * nt + t
                            act.wait_ge(taken, i * per + n + 1)
                            act.dma_start(out_dram[i * nj + j][t * P:(t + 1) * P, :], ob[n % 4][:]).then_inc(stored[n % 4], 16)
                for b in range(4):
                    act.wait_ge(stored[b], turns * -(-(per - b) // 4) * 16)


def gemm_small(nc, name, w, kt, nt, rhs, total, evac, evac_on="scalar", out_dram=None, side=None, side_dram=None, unroll=2):
    cs = chunks_of(total)
    nb = len(cs)
    with Stage(nc, name) as s:
        wb = [s.sb(f"w{j}", [P, kt * P]) for j in range(unroll)]
        ob = [s.sb(f"o{j}", [P, total]) for j in range(unroll)] if out_dram is not None else None
        xb = [s.sb(f"x{j}", [P, total]) for j in range(unroll)] if side_dram is not None else None
        ps = [[s.ps(f"p{j}_{c}") for c in range(nb)] for j in range(unroll)]
        w_in, summed, out_taken = s.sems("w_in", unroll), s.sems("summed", unroll), s.sems("taken", unroll)
        stored, x_in = s.sems("stored", unroll), s.sems("x_in", unroll)
        with nc.Block() as block:
            @block.sync
            def _(sp):
                with sp.Fori(0, nt // unroll) as i:
                    for j in range(unroll):
                        sp.wait_ge(summed[j], i * nb)
                        sp.dma_start(wb[j][:], w[i * unroll + j]).then_inc(w_in[j], 16)
                        if xb:
                            sp.wait_ge(out_taken[j], i * nb)
                            sp.dma_start(xb[j][:], side_dram[i * unroll + j]).then_inc(x_in[j], 16)

            @block.tensor
            def _(pe):
                with pe.Fori(0, nt // unroll) as i:
                    for j in range(unroll):
                        pe.wait_ge(w_in[j], i * 16 + 16)
                        pe.wait_ge(out_taken[j], i * nb)
                        for c, (a, m) in enumerate(cs):
                            for k in range(kt):
                                mm = nc.tensor.matmul(ps[j][c][:, 0:m], wb[j][:, k * P:(k + 1) * P], rhs(k, a, m),
                                                      start=(k == 0), stop=(k == kt - 1))
                            mm.then_inc(summed[j], 1)

            def take(eng, ns, i):
                for j in range(unroll):
                    if ob:
                        eng.wait_ge(stored[j], i * 16)
                    if xb:
                        eng.wait_ge(x_in[j], i * 16 + 16)
                    for c, (a, m) in enumerate(cs):
                        eng.wait_ge(summed[j], i * nb + c + 1)
                        evac(ns, ob[j][:, a:a + m] if ob else None, ps[j][c][:, 0:m], i * unroll + j, a, m,
                             xb[j][:, a:a + m] if xb else None).then_inc(out_taken[j], 1)

            if evac_on == "vector":
                @block.vector
                def _(dve):
                    with dve.Fori(0, nt // unroll) as i:
                        take(dve, nc.vector, i)

            @block.scalar
            def _(act):
                if evac_on == "scalar" or ob:
                    with act.Fori(0, nt // unroll) as i:
                        if evac_on == "scalar":
                            take(act, nc.scalar, i)
                        if ob:
                            for j in range(unroll):
                                act.wait_ge(out_taken[j], i * nb + nb)
                                act.dma_start(out_dram[i * unroll + j], ob[j][:]).then_inc(stored[j], 16)
                if ob:
                    for j in range(unroll):
                        act.wait_ge(stored[j], nt // unroll * 16)


def norm_channels(nc, name, src, total, dst, gain, shift, ones, width=D):
    kt = width // P
    cs = chunks_of(total)
    with Stage(nc, name) as s:
        sq = [s.sb(f"sq{j}", [P, BANK]) for j in range(2)]
        rs = s.sb("rs", [P, total])
        ps = [s.ps(f"p{c}") for c in range(len(cs))]
        squared, used, summed = s.sem("squared"), s.sem("used"), s.sem("summed")
        meant, rooted, scaled, own = s.sem("meant"), s.sem("rooted"), s.sem("scaled"), s.sem("own")
        with nc.Block() as block:
            @block.scalar
            def _(act):
                n = 0
                for a, m in cs:
                    for k in range(kt):
                        if n >= 2:
                            act.wait_ge(used, n - 1)
                        nc.scalar.activation(sq[n % 2][:, 0:m], src[:, k, a:a + m], ACT.Square).then_inc(squared, 1)
                        n += 1
                for c, (a, m) in enumerate(cs):
                    act.wait_ge(meant, c + 1)
                    nc.scalar.activation(rs[:, a:a + m], rs[:, a:a + m], ACT.Sqrt).then_inc(rooted, 1)
                for k in range(kt):
                    act.wait_ge(scaled, k + 1)
                    nc.scalar.activation(dst[:, k, 0:total], dst[:, k, 0:total], ACT.Identity,
                                         bias=shift(k) if shift else 0.0, scale=gain(k)).then_inc(own, 1)

            @block.tensor
            def _(pe):
                n = 0
                for c, (a, m) in enumerate(cs):
                    for k in range(kt):
                        pe.wait_ge(squared, n + 1)
                        mm = nc.tensor.matmul(ps[c][:, 0:m], ones[:, 0:P], sq[n % 2][:, 0:m], start=(k == 0), stop=(k == kt - 1))
                        mm.then_inc(used, 1)
                        n += 1

            @block.vector
            def _(dve):
                for c, (a, m) in enumerate(cs):
                    dve.wait_ge(used, kt * (c + 1))
                    nc.vector.tensor_scalar(rs[:, a:a + m], ps[c][:, 0:m], 1.0 / width, EPS, ALU.mult, ALU.add).then_inc(meant, 1)
                for c, (a, m) in enumerate(cs):
                    dve.wait_ge(rooted, c + 1)
                    nc.vector.reciprocal(rs[:, a:a + m], rs[:, a:a + m]).then_inc(summed, 1)
                dve.wait_ge(summed, len(cs))
                for k in range(kt):
                    nc.vector.tensor_tensor(dst[:, k, 0:total], src[:, k, 0:total], rs[:], ALU.mult).then_inc(scaled, 1)


def norm_split(nc, name, src, total, high, rest, gain, shift, ones):
    cs = chunks_of(total)
    with Stage(nc, name) as s:
        sq = [s.sb(f"sq{j}", [P, BANK]) for j in range(2)]
        rs = s.sb("rs", [P, total])
        t, y = [s.sb(f"t{j}", [P, total]) for j in range(2)], [s.sb(f"y{j}", [P, total]) for j in range(2)]
        ps = [s.ps(f"p{c}") for c in range(len(cs))]
        squared, used, inverted = s.sem("squared"), s.sem("used"), s.sem("inverted")
        meant, rooted, scaled, gained, left = s.sem("meant"), s.sem("rooted"), s.sem("scaled"), s.sem("gained"), s.sem("left")
        with nc.Block() as block:
            @block.scalar
            def _(act):
                n = 0
                for a, m in cs:
                    for k in range(KD):
                        if n >= 2:
                            act.wait_ge(used, n - 1)
                        nc.scalar.activation(sq[n % 2][:, 0:m], src[:, k, a:a + m], ACT.Square).then_inc(squared, 1)
                        n += 1
                for c, (a, m) in enumerate(cs):
                    act.wait_ge(meant, c + 1)
                    nc.scalar.activation(rs[:, a:a + m], rs[:, a:a + m], ACT.Sqrt).then_inc(rooted, 1)
                for k in range(KD):
                    act.wait_ge(scaled, k + 1)
                    if k >= 2:
                        act.wait_ge(left, k - 1)
                    for out in (y[k % 2][:], high[:, k, 0:total]):
                        nc.scalar.activation(out, t[k % 2][:], ACT.Identity, bias=shift(k) if shift else 0.0, scale=gain(k)).then_inc(gained, 1)

            @block.tensor
            def _(pe):
                n = 0
                for c, (a, m) in enumerate(cs):
                    for k in range(KD):
                        pe.wait_ge(squared, n + 1)
                        nc.tensor.matmul(ps[c][:, 0:m], ones[:, 0:P], sq[n % 2][:, 0:m], start=(k == 0), stop=(k == KD - 1)).then_inc(used, 1)
                        n += 1

            @block.vector
            def _(dve):
                for c, (a, m) in enumerate(cs):
                    dve.wait_ge(used, KD * (c + 1))
                    nc.vector.tensor_scalar(rs[:, a:a + m], ps[c][:, 0:m], 1.0 / D, EPS, ALU.mult, ALU.add).then_inc(meant, 1)
                for c, (a, m) in enumerate(cs):
                    dve.wait_ge(rooted, c + 1)
                    nc.vector.reciprocal(rs[:, a:a + m], rs[:, a:a + m]).then_inc(inverted, 1)
                dve.wait_ge(inverted, len(cs))
                for k in range(KD + 1):
                    if k < KD:
                        if k >= 2:
                            dve.wait_ge(gained, 2 * (k - 1))
                        nc.vector.tensor_tensor(t[k % 2][:], src[:, k, 0:total], rs[:], ALU.mult).then_inc(scaled, 1)
                    if k:
                        dve.wait_ge(gained, 2 * k)
                        nc.vector.tensor_tensor(rest[:, k - 1, 0:total], y[(k - 1) % 2][:], high[:, k - 1, 0:total].bitcast(F32), ALU.subtract).then_inc(left, 1)
                dve.wait_ge(left, KD)


def modulation(nc, A, mod):
    nt, per = 6 * KD, 4
    with Stage(nc, "ada") as s:
        c2, cs = s.sb("c2", [P, KD, 2]), s.sb("cs", [P, KD, 2])
        bias = s.sb("bias", [P, nt])
        wb = [s.sb(f"w{j}", [P, per * KD * P]) for j in range(2)]
        ps = [s.ps(f"p{j}") for j in range(2)]
        c_in, silu, w_in, used, taken = s.sem("c_in"), s.sem("silu"), s.sems("w_in", 2), s.sems("used", 2), s.sems("taken", 2)
        own = s.sem("own")
        with nc.Block() as block:
            @block.sync
            def _(sp):
                sp.dma_start(c2[:], A["c2"]).then_inc(c_in, 16)
                sp.dma_start(bias[:], A["ada_b"]).then_inc(c_in, 16)
                with sp.Fori(0, nt // per // 2) as i:
                    for j in range(2):
                        sp.wait_ge(used[j], i)
                        sp.dma_start(wb[j][:], A["ada_w"][i * 2 + j]).then_inc(w_in[j], 16)

            @block.scalar
            def _(act):
                act.wait_ge(c_in, 32)
                nc.scalar.activation(cs[:], c2[:], ACT.Silu).then_inc(silu, 1)

            @block.tensor
            def _(pe):
                pe.wait_ge(silu, 1)
                with pe.Fori(0, nt // per // 2) as i:
                    for j in range(2):
                        pe.wait_ge(w_in[j], i * 16 + 16)
                        pe.wait_ge(taken[j], i)
                        for n in range(per):
                            for k in range(KD):
                                mm = nc.tensor.matmul(ps[j][:, 2 * n:2 * n + 2], wb[j][:, (n * KD + k) * P:(n * KD + k + 1) * P],
                                                      cs[:, k, :], start=(k == 0), stop=(k == KD - 1))
                        mm.then_inc(used[j], 1)

            @block.vector
            def _(dve):
                with dve.Fori(0, nt // per // 2) as i:
                    for j in range(2):
                        dve.wait_ge(used[j], i + 1)
                        nc.vector.tensor_copy(mod[:, bass.ds((i * 2 + j) * per, per), :], ps[j][:, 0:2 * per].rearrange("p (n s) -> p n s", s=2)).then_inc(taken[j], 1)
                for j in range(2):
                    dve.wait_ge(taken[j], nt // per // 2)
                dve.wait_ge(c_in, 32)
                st = Steps(dve, own)
                for x in range(2):
                    st.then(nc.vector.tensor_tensor(mod[:, :, x], mod[:, :, x], bias[:], ALU.add))


GLA_H, GLA_DK, GLA_DV, LR = 4, 64, 128, 16
ML_H, ML_D = 4, 128
CM1 = 14


def first_projection(nc, A, R, mod, ones):
    with Stage(nc, "zin") as s:
        hh, hl = s.sb("hh", [P, KD, TOT], F32R), s.sb("hl", [P, KD, TOT], F32R)
        with Stage(nc, "znorm") as z:
            h, gain, shift = z.sb("h", [P, KD, TOT]), z.sb("gain", [P, 2, KD]), z.sb("shift", [P, 2, KD])
            own = z.sem("own")
            load(nc, "zld", [(h[:, :, 0:CTX], A["ctxT"]), (h[:, :, CTX:TOT], A["xT"]), (gain[:, 0, :], A["norm1_g"])])
            with nc.Block() as block:
                @block.vector
                def _(dve):
                    st = Steps(dve, own)
                    st.then(nc.vector.tensor_copy(gain[:, 1, :], gain[:, 0, :]))
                    st.then(nc.vector.tensor_scalar(shift[:], mod[:, KD:2 * KD, :].rearrange("p k s -> p s k"), 1.0, None, ALU.add))
                    st.then(nc.vector.tensor_tensor(gain[:], gain[:], shift[:], ALU.mult))
                    st.then(nc.vector.tensor_copy(shift[:], mod[:, 0:KD, :].rearrange("p k s -> p s k")))
            for name, n, at in (("nc", 1, slice(0, CTX)), ("nx", 0, slice(CTX, TOT))):
                norm_split(nc, name, h[:, :, at], at.stop - at.start, hh[:, :, at], hl[:, :, at],
                           lambda k: gain[:, n, k:k + 1], lambda k: shift[:, n, k:k + 1], ones)
        rhs = lambda k, a, m: (hh[:, k, a:a + m], hl[:, k, a:a + m])
        copy = lambda ns, out, ps, n, a, m, side: ns.activation(out, ps, ACT.Copy)
        gemm(nc, "z1", A["w_in_cm"], KD, CM1, rhs, TOT, copy, out_dram=R["z_cm"])
        gemm_tokens(nc, "z3", A["w_in_v"], 2, 512, hh, hl, 0, NCH, R["z_v"])
        gemm_tokens(nc, "z4", A["w_in_g"], 2, 512, hh, hl, CTX, NCX, R["z_g"])


def grid_conv(nc, A, R):
    n_t, rows = 8, SEQ // GRID_W
    pw = GRID_W + 2
    with Stage(nc, "conv") as s:
        w, b = s.sb("w", [P, n_t, 9]), s.sb("b", [P, n_t])
        post = s.sb("post", [P, n_t])
        pad = [s.sb(f"pad{j}", [P, rows + 2, pw]) for j in range(2)]
        padc = [s.sb(f"padc{j}", [P, CTX + 2]) for j in range(2)]
        raw = [s.sb(f"raw{j}", [P, TOT]) for j in range(2)]
        out = [s.sb(f"out{j}", [P, TOT]) for j in range(2)]
        consts, x_in, zeroed, taken = s.sem("consts"), s.sems("x_in", 2), s.sem("zeroed"), s.sems("taken", 2)
        summed, gated, done, stored, own = s.sems("summed", 2), s.sems("gated", 2), s.sems("done", 2), s.sems("stored", 2), s.sem("own")
        n_own = 2 * (2 + 8 + 2)
        with nc.Block() as block:
            @block.sync
            def _(sp):
                sp.dma_start(w[:], A["conv_w"]).then_inc(consts, 16)
                sp.dma_start(b[:], A["conv_b"]).then_inc(consts, 16)
                sp.dma_start(post[:], A["conv_post"]).then_inc(consts, 16)
                with sp.Fori(0, n_t // 2) as i:
                    for j in range(2):
                        sp.wait_ge(taken[j], i)
                        sp.dma_start(raw[j][:], R["z_cm"][i * 2 + 4 + j]).then_inc(x_in[j], 16)

            @block.gpsimd
            def _(pool):
                for j in range(2):
                    nc.gpsimd.memset(pad[j][:], 0.0).then_inc(zeroed, 1)
                    nc.gpsimd.memset(padc[j][:], 0.0).then_inc(zeroed, 1)

            @block.vector
            def _(dve):
                dve.wait_ge(consts, 48)
                dve.wait_ge(zeroed, 4)
                with dve.Fori(0, n_t // 2) as i:
                    st = Steps(dve, own, i * n_own)
                    for j in range(2):
                        dve.wait_ge(x_in[j], i * 16 + 16)
                        dve.wait_ge(stored[j], i * 16)
                        st.then(nc.vector.tensor_copy(padc[j][:, 1:CTX + 1], raw[j][:, 0:CTX]))
                        st.then(nc.vector.tensor_copy(pad[j][:, 1:rows + 1, 1:GRID_W + 1],
                                                      raw[j][:, CTX:TOT].rearrange("p (r c) -> p r c", c=GRID_W)))
                        oc, ox = out[j][:, 0:CTX], out[j][:, CTX:TOT].rearrange("p (r c) -> p r c", c=GRID_W)
                        tap = lambda q: w[:, bass.ds(i * 2 + j, 1), q]
                        nc.vector.tensor_scalar(oc, padc[j][:, 0:CTX], tap(3), None, ALU.mult).then_inc(taken[j], 1)
                        nc.vector.tensor_scalar(ox, pad[j][:, 0:rows, 0:GRID_W], tap(0), None, ALU.mult).then_inc(own, 1)
                        st.n = st.n + 1
                        dve.wait_ge(taken[j], i + 1)
                        dve.wait_ge(own, st.n)
                        for q in (1, 2):
                            st.then(nc.vector.scalar_tensor_tensor(oc, padc[j][:, q:q + CTX], tap(3 + q), oc, ALU.mult, ALU.add))
                        for q in range(1, 8):
                            st.then(nc.vector.scalar_tensor_tensor(ox, pad[j][:, q // 3:q // 3 + rows, q % 3:q % 3 + GRID_W],
                                                                   tap(q), ox, ALU.mult, ALU.add))
                        nc.vector.scalar_tensor_tensor(ox, pad[j][:, 2:2 + rows, 2:2 + GRID_W],
                                                       tap(8), ox, ALU.mult, ALU.add).then_inc(summed[j], 1)
                        dve.wait_ge(gated[j], i + 1)
                        nc.vector.tensor_scalar(out[j][:], out[j][:], post[:, bass.ds(i * 2 + j, 1)], None, ALU.mult).then_inc(done[j], 1)

            @block.scalar
            def _(act):
                with act.Fori(0, n_t // 2) as i:
                    for j in range(2):
                        act.wait_ge(summed[j], i + 1)
                        nc.scalar.activation(out[j][:], out[j][:], ACT.Silu, bias=b[:, bass.ds(i * 2 + j, 1)]).then_inc(gated[j], 1)
                        act.wait_ge(done[j], i + 1)
                        act.dma_start(R["mqk"][i * 2 + j], out[j][:]).then_inc(stored[j], 16)
                for j in range(2):
                    act.wait_ge(stored[j], 16 * (n_t // 2))


ORDER = [list(range(NCH)), list(range(NCC - 1, -1, -1)) + list(range(NCH - 1, NCC - 1, -1))]


def gla_gates(nc, A, R, qk, fac, room, room2):
    cs = chunks_of(TOT)
    with Stage(nc, "gg") as s:
        lr, up = s.sb("lr", [P, TOT]), s.sb("up", [P, 2, P])
        upb = s.sb("upb", [P, 4])
        room = room.rearrange("p a b -> p (a b)")
        raw = room[:, 0:4 * TOT].rearrange("p (n t) -> p n t", t=TOT)
        mask = room[:, 4 * TOT:6 * TOT].rearrange("p (n t) -> p n t", t=TOT)
        room2 = room2.rearrange("p a b -> p (a b)")
        g, u, t, e = (room2[:, n * TOT:(n + 1) * TOT] for n in range(4))
        f = s.sb("f", [P, 3, NCH])
        ps = [s.ps(f"p{c}") for c in range(len(cs))]
        got, summed, exped, own, zeroed = s.sem("got"), s.sem("summed"), s.sem("exped"), s.sem("own"), s.sem("zeroed")
        per = len(cs) + 13
        with nc.Block() as block:
            @block.sync
            def _(sp):
                for dst, src in ((lr[:], R["z_cm"][12]), (up[:], A["gla_up_w"]), (upb[:], A["gla_up_b"]),
                                 (raw, R["z_cm"][0:4].rearrange("n p t -> p n t")),
                                 (mask[:, 0, :], A["scan_mask"][0:1, :].broadcast_to([P, TOT])),
                                 (mask[:, 1, :], A["scan_mask"][1:2, :].broadcast_to([P, TOT]))):
                    sp.dma_start(dst, src).then_inc(got, 16)

            @block.tensor
            def _(pe):
                pe.wait_ge(got, 96)
                for n in range(4):
                    d, ti = n // 2, n % 2
                    if n:
                        pe.wait_ge(own, per * (n - 1) + len(cs))
                    for c, (a, m) in enumerate(cs):
                        nc.tensor.matmul(ps[c][:, 0:m], up[32 * d:32 * d + LR, ti, :], lr[32 * d:32 * d + LR, a:a + m],
                                         start=True, stop=True).then_inc(summed, 1)

            @block.gpsimd
            def _(pool):
                for x in range(2):
                    for d in range(2):
                        nc.gpsimd.memset(qk[64 - 64 * x:128 - 64 * x, d, :, :, x, :], 0.0).then_inc(zeroed, 1)
                pool.wait_ge(zeroed, 4)

            @block.vector
            def _(dve):
                dve.wait_ge(got, 96)
                st = Steps(dve, own)
                for n in range(4):
                    d, ti = n // 2, n % 2
                    dve.wait_ge(summed, len(cs) * (n + 1))
                    for c, (a, m) in enumerate(cs):
                        st.then(nc.vector.tensor_scalar(g[:, a:a + m], ps[c][:, 0:m], upb[:, n:n + 1], None, ALU.add))
                    st.then(nc.vector.scalar_tensor_tensor(u[:], g[:], -1.0, g[:], ALU.mult, ALU.min))
                    dve.wait_ge(exped, 5 * n + 2)
                    st.then(nc.vector.scalar_tensor_tensor(g[:], g[:], 0.0, u[:], ALU.min, ALU.subtract))
                    st.then(nc.vector.tensor_scalar(g[:], g[:], 1.0 / 16.0, None, ALU.mult))
                    r = slice(None) if d == 0 else slice(None, None, -1)
                    st.then(nc.vector.tensor_tensor_scan(out=t[:, r], data0=mask[:, d, r], data1=g[:, r], initial=0.0,
                                                         op0=ALU.mult, op1=ALU.add))
                    tc = t[:].rearrange("p (c t) -> p c t", t=CH)
                    mid = tc[:, :, CH // 2 - 1 if d == 0 else CH // 2]
                    end = tc[:, :, CH - 1 if d == 0 else 0]
                    st.then(nc.vector.tensor_copy(f[:, 0, :], mid))
                    st.then(nc.vector.tensor_copy(f[:, 1, :], end))
                    st.then(nc.vector.tensor_tensor(f[:, 2, :], f[:, 1, :], f[:, 0, :], ALU.subtract))
                    st.then(nc.vector.tensor_tensor(u[:].rearrange("p (c t) -> p c t", t=CH), tc,
                                                    f[:, 0, :].unsqueeze(2).broadcast_to([P, NCH, CH]), ALU.subtract))
                    dve.wait_ge(exped, 5 * n + 5)
                    first, rest = (slice(0, NCC), slice(NCC, NCH)) if d == 0 else (slice(NCC - 1, None, -1), slice(NCH - 1, NCC - 1, -1))
                    st.then(nc.vector.tensor_copy(fac[:, 0:NCC, d, ti, :].rearrange("p n f -> p f n"), f[:, :, first]))
                    st.then(nc.vector.tensor_copy(fac[:, NCC:NCH, d, ti, :].rearrange("p n f -> p f n"), f[:, :, rest]))
                    ch = lambda x: x.rearrange("p (c t) -> p c t", t=CH)
                    for x in range(2):
                        rows = slice(64 * x, 64 * x + 64)
                        st.then(nc.vector.scalar_tensor_tensor(qk[rows, d, :, ti, x, :], ch(e[:])[rows], GLA_DK ** -0.5,
                                                               ch(raw[:, ti, :])[rows], ALU.mult, ALU.mult))
                    st.then(nc.vector.tensor_tensor(qk[:, d, :, ti, 2, :], ch(u[:]), ch(raw[:, 2 + ti, :]), ALU.mult))

            @block.scalar
            def _(act):
                for n in range(4):
                    start = per * n
                    act.wait_ge(own, start + len(cs) + 1)
                    nc.scalar.activation(u[:], u[:], ACT.Exp).then_inc(exped, 1)
                    act.wait_ge(exped, 5 * n + 1)
                    nc.scalar.activation(u[:], u[:], ACT.Ln, bias=1.0).then_inc(exped, 1)
                    act.wait_ge(own, start + len(cs) + 8)
                    nc.scalar.activation(e[:], u[:], ACT.Exp).then_inc(exped, 1)
                    act.wait_ge(exped, 5 * n + 3)
                    nc.scalar.activation(u[:], u[:], ACT.Exp, scale=-1.0).then_inc(exped, 1)
                    nc.scalar.activation(f[:], f[:], ACT.Exp).then_inc(exped, 1)


def gla_scan(nc, A, R, qk, fac, v, out, C):
    with Stage(nc, "gs") as s:
        cur = s.sb("cur", [P, 2, 2, 3, CH])
        att, kt = s.sb("att", [P, 2, GLA_H, CH]), s.sb("kt", [P, 4, CH])
        seen = s.sb("seen", [P, 1])
        state, mid, add = s.sb("state", [P, 4, GLA_DV]), s.sb("mid", [P, 4, GLA_DV]), s.sb("add", [P, 4, GLA_DV])
        pa = s.ps("pa", [P, 2, BANK])
        pk, po = s.ps("pk"), [s.ps(f"po{d}") for d in range(2)]
        pst = s.ps("pst", [P, 4, 2 * GLA_DV])
        cut, att_done, kt_done, masked, kt_taken, mid_done, o_done, stepped, o_taken, own = (
            s.sem(x) for x in ("cut", "att_done", "kt_done", "masked", "kt_taken", "mid_done", "o_done", "stepped", "o_taken", "own"))
        factor = lambda n, f, rows=slice(0, P): fac[rows, bass.ds(n, 1), :, :, f].rearrange("p n d t -> p (n d t)").unsqueeze(2)

        def steps(emit, eng):
            for n in range(NCC):
                emit(n, [ORDER[0][n], ORDER[1][n]], None)
            with eng.Fori(0, NCX) as i:
                emit(i + NCC, [i + NCC, i * -1 + NCH - 1], i)

        with nc.Block() as block:
            @block.vector
            def _(dve):
                st = Steps(dve, own)
                st.then(nc.vector.memset(att[:], 0.0))
                st.then(nc.vector.memset(state[:], 0.0))
                n_own = 4

                def emit(n, c, i):
                    st = Steps(dve, own, n * n_own + 2)
                    dve.wait_ge(stepped, n)
                    for d in range(2):
                        ins = nc.vector.tensor_copy(cur[:, d], qk[:, d, bass.ds(c[d], 1)].rearrange("p a t q c -> p (a t) q c"))
                        ins.then_inc(cut, 1)
                    if i is not None:
                        nc.vector.tensor_tensor(mid[:], state[:], factor(n, 0).broadcast_to([P, 4, GLA_DV]), ALU.mult).then_inc(mid_done, 1)
                        dve.wait_ge(att_done, i + 1)
                        nc.vector.memset(seen[:], 0.0)
                        for d in range(2):
                            nc.vector.copy_predicated(att[:, d], C["keep"][:, d].unsqueeze(1).broadcast_to([P, GLA_H, CH]),
                                                      pa[:, d].rearrange("p (h t) -> p h t", t=CH)).then_inc(masked, 1)
                    dve.wait_ge(stepped, n + 1)
                    for half in range(2):
                        rows = slice(64 * half, 64 * half + 64)
                        st.then(nc.vector.tensor_tensor(add[rows], pst[rows, :, half * GLA_DV:(half + 1) * GLA_DV],
                                                        factor(n, 2, rows).broadcast_to([64, 4, GLA_DV]), ALU.mult))
                    if i is not None:
                        dve.wait_ge(mid_done, i + 1)
                    st.then(nc.vector.tensor_tensor(state[:], state[:], factor(n, 1).broadcast_to([P, 4, GLA_DV]), ALU.mult))
                    st.then(nc.vector.tensor_tensor(state[:], state[:], add[:], ALU.add))

                steps(emit, dve)

            @block.tensor
            def _(pe):
                def emit(n, c, i):
                    pe.wait_ge(cut, n * 2 + 2)
                    if i is not None:
                        for d in range(2):
                            for h in range(GLA_H):
                                mm = nc.tensor.matmul(pa[:, d, h * CH:(h + 1) * CH], cur[:, d, h // 2, 2, :], cur[:, d, h // 2, h % 2, :],
                                                      start=True, stop=True)
                        mm.then_inc(att_done, 1)
                    for q in range(4):
                        mm = nc.tensor.transpose(pk[:, q * CH:(q + 1) * CH], cur[:, q // 2, q % 2, 2, :], C["ident"][:])
                    mm.then_inc(kt_done, 1)
                    if i is not None:
                        pe.wait_ge(masked, i * 2 + 2)
                        pe.wait_ge(mid_done, i + 1)
                        pe.wait_ge(o_taken, i * 2)
                        for d in range(2):
                            for h in range(GLA_H):
                                o = po[d][:, h * GLA_DV:(h + 1) * GLA_DV]
                                nc.tensor.matmul(o, att[:, d, h, :], v[:, bass.ds(c[d], 1), h * GLA_DV:(h + 1) * GLA_DV], start=True, stop=False)
                                mm = nc.tensor.matmul(o, cur[:, d, h // 2, h % 2, :], mid[:, 2 * d + h // 2, :], start=False, stop=True)
                        mm.then_inc(o_done, 1)
                    pe.wait_ge(kt_taken, n + 1)
                    for q in range(4):
                        t = q % 2
                        mm = nc.tensor.matmul(pst[:, q, :], kt[:, q, :], v[:, bass.ds(c[q // 2], 1), t * 256:t * 256 + 256], start=True, stop=True)
                    mm.then_inc(stepped, 1)

                steps(emit, pe)

            @block.scalar
            def _(act):
                def emit(n, c, i):
                    act.wait_ge(kt_done, n + 1)
                    act.wait_ge(stepped, n)
                    nc.scalar.activation(kt[:], pk[:], ACT.Copy).then_inc(kt_taken, 1)
                    if i is not None:
                        act.wait_ge(o_done, i + 1)
                        for d in range(2):
                            nc.scalar.activation(out[:, d, bass.ds(c[d] - NCC, 1), :], po[d][:], ACT.Copy).then_inc(o_taken, 1)

                steps(emit, act)


def mlstm_gates(nc, A, R, negm, cols, C):
    R64 = 64
    with Stage(nc, "mg") as s:
        ig, fg, t, zero = s.sb("ig", [R64, TOT]), s.sb("fg", [R64, TOT]), s.sb("t", [R64, TOT]), s.sb("zero", [R64, TOT])
        ib, fb = s.sb("ib", [R64, 1]), s.sb("fb", [R64, 1])
        ps = [s.ps(f"p{b}") for b in range(3)]
        zeroed, got, exped, rows, turned, own = (s.sem(x) for x in ("zeroed", "got", "exped", "rows", "turned", "own"))
        with nc.Block() as block:
            @block.sync
            def _(sp):
                sp.wait_ge(zeroed, 2)
                for d in range(2):
                    r = slice(32 * d, 32 * d + 4)
                    sp.dma_start(ig[r, :], R["z_cm"][12, 64 + 4 * d:68 + 4 * d, :]).then_inc(got, 16)
                    sp.dma_start(fg[r, :], R["z_cm"][12, 96 + 4 * d:100 + 4 * d, :]).then_inc(got, 16)
                sp.dma_start(ib[:], A["ml_i_b"]).then_inc(got, 16)
                sp.dma_start(fb[:], A["ml_f_b"]).then_inc(got, 16)

            @block.vector
            def _(dve):
                nc.vector.memset(ig[:], 0.0).then_inc(zeroed, 1)
                nc.vector.memset(fg[:], 0.0).then_inc(zeroed, 1)
                st = Steps(dve, own)
                V = nc.vector
                st.then(V.memset(zero[:], 1.0))
                dve.wait_ge(got, 96)
                st.then(V.tensor_scalar(fg[:], fg[:], fb[:], None, ALU.add))
                st.then(V.scalar_tensor_tensor(t[:], fg[:], -1.0, fg[:], ALU.mult, ALU.min))
                dve.wait_ge(exped, 2)
                st.then(V.scalar_tensor_tensor(fg[:], fg[:], 0.0, t[:], ALU.min, ALU.subtract))
                seg = [[(slice(0, 4), slice(0, TOT), None)],
                       [(slice(32, 36), slice(CTX - 1, None, -1), None), (slice(32, 36), slice(TOT - 1, CTX - 1, -1), 0)]]
                st.then(V.memset(t[:], 0.0))
                for d in range(2):
                    for r, c, first in seg[d]:
                        st.then(V.tensor_tensor_scan(out=t[r, c], data0=zero[r, c], data1=fg[r, c],
                                                     initial=0.0 if first is None else t[r, 0:1], op0=ALU.mult, op1=ALU.add))
                st.then(V.tensor_scalar(ig[:], ig[:], ib[:], None, ALU.add))
                st.then(V.tensor_tensor(ig[:], ig[:], t[:], ALU.subtract))
                st.then(V.memset(fg[:], 0.0))
                for d in range(2):
                    for r, c, first in seg[d]:
                        st.then(V.tensor_tensor_scan(out=fg[r, c], data0=ig[r, c], data1=ig[r, c],
                                                     initial=0.0 if first is None else fg[r, 0:1], op0=ALU.max, op1=ALU.max))
                st.then(V.tensor_scalar(negm[:], fg[:], -1.0, None, ALU.mult))
                V.tensor_tensor(t[:], negm[:], t[:], ALU.subtract).then_inc(rows, 1)
                for b in range(3):
                    dve.wait_ge(turned, b + 1)
                    n = min(8, 2 * NCH - 8 * b)
                    st.then(V.tensor_copy(cols[:].rearrange("p a c r -> p (a c) r")[:, 8 * b:8 * b + n, :],
                                          ps[b][:, 0:n * R64].rearrange("p (c r) -> p c r", r=R64)))

            @block.scalar
            def _(act):
                act.wait_ge(own, 3)
                nc.scalar.activation(t[:], t[:], ACT.Exp).then_inc(exped, 1)
                act.wait_ge(exped, 1)
                nc.scalar.activation(t[:], t[:], ACT.Ln, bias=1.0).then_inc(exped, 1)
                act.wait_ge(own, 18)
                nc.scalar.activation(cols[:, 1], cols[:, 1], ACT.Exp).then_inc(exped, 1)

            @block.tensor
            def _(pe):
                pe.wait_ge(rows, 1)
                for b in range(3):
                    n = min(8, 2 * NCH - 8 * b)
                    for j in range(n):
                        a, c = (8 * b + j) // NCH, (8 * b + j) % NCH
                        mm = nc.tensor.transpose(ps[b][:, j * R64:(j + 1) * R64], (ig, t)[a][:, c * CH:(c + 1) * CH], C["ident"][0:R64, 0:R64])
                    mm.then_inc(turned, 1)


def mlstm_scan(nc, A, R, negm, cols, v, out, C):
    H = ML_H
    with Stage(nc, "ms") as s:
        q, k = s.sb("q", [P, H, TOT]), s.sb("k", [P, H, TOT])
        kcur, arg, inter, qw, pt, kw = (s.sb(x, [P, H, CH]) for x in ("kcur", "arg", "inter", "qw", "pt", "kw"))
        state, norm, mbefore = s.sb("state", [P, 2, H, ML_D]), s.sb("norm", [P, 2, H]), s.sb("mbefore", [P, 2, H])
        kd, den = s.sb("kd", [P, 2, H]), s.sb("den", [P, H])
        ones1, pick = s.sb("ones1", [P, 1]), s.sb("pick", [64, 2 * ML_H, P])
        pm, pqk, pk, pn, pst, pden, pnorm = (s.ps(x) for x in ("pm", "pqk", "pk", "pn", "pst", "pden", "pnorm"))
        got, k_cut, rows_up, args, exps, qk_done, kt_done, q_in, weighed, kw_done, o_done, stepped, own = (
            s.sem(x) for x in ("got", "k_cut", "rows_up", "args", "exps", "qk_done", "kt_done", "q_in", "weighed", "kw_done", "o_done", "stepped", "own"))
        heads = lambda x: x.rearrange("p (h t) -> p h t", h=H)
        wide = lambda x: x.unsqueeze(2).broadcast_to([P, H, CH])

        def steps(emit, eng):
            for n in range(NCC):
                for d in range(2):
                    emit(n * 2 + d, d, ORDER[d][n], None)
            with eng.Fori(0, NCX) as i:
                for d in range(2):
                    emit((i + NCC) * 2 + d, d, (i + NCC) if d == 0 else (i * -1 + NCH - 1), i * 2 + d)

        with nc.Block() as block:
            @block.sync
            def _(sp):
                sp.dma_start(q[:], R["mqk"][0:4].rearrange("n p t -> p n t")).then_inc(got, 16)
                sp.dma_start(k[:], R["mqk"][4:8].rearrange("n p t -> p n t")).then_inc(got, 16)
                sp.dma_start(pick[:], A["pick"]).then_inc(got, 16)

            @block.scalar
            def _(act):
                act.wait_ge(got, 48)

                def emit(n, d, c, i):
                    act.wait_ge(stepped, n)
                    nc.scalar.activation(kcur[:], k[:, :, bass.ds(c * CH, CH)], ACT.Copy).then_inc(k_cut, 1)
                    act.wait_ge(args, n + 1)
                    nc.scalar.activation(kd[:], kd[:], ACT.Exp).then_inc(exps, 1)
                    if i is not None:
                        nc.scalar.activation(inter[:], inter[:], ACT.Exp).then_inc(exps, 1)
                        nc.scalar.activation(arg[:], arg[:], ACT.Exp).then_inc(exps, 1)

                steps(emit, act)

            @block.vector
            def _(dve):
                V = nc.vector
                st = Steps(dve, own)
                for x in (state, norm, mbefore):
                    st.then(V.memset(x[:], 0.0))
                st.then(V.memset(ones1[:], 1.0))
                dve.wait_ge(got, 48)
                n_ctx, n_lat = 6, 14

                def emit(n, d, c, i):
                    st = Steps(dve, own, 4 + (n * n_ctx if i is None else 2 * NCC * n_ctx + i * n_lat))
                    last = CH - 1 if d == 0 else 0
                    bcol = cols[:, 0, bass.ds(c, 1), 32 * d:32 * d + H].rearrange("p a h -> p (a h)")
                    dve.wait_ge(rows_up, n + 1)
                    mend = heads(pm[:])[:, :, last]
                    st.then(V.tensor_tensor(kd[:, 0], bcol, mend, ALU.add))
                    st.then(V.tensor_tensor(kd[:, 1], mbefore[:, d], mend, ALU.add))
                    if i is not None:
                        st.then(V.tensor_tensor(inter[:], heads(pm[:]), wide(mbefore[:, d]), ALU.add))
                        st.then(V.tensor_tensor(arg[:], heads(pm[:]), wide(bcol), ALU.add))
                        st.then(V.tensor_tensor(arg[:], arg[:], C["cut"][:, d].unsqueeze(1).broadcast_to([P, H, CH]), ALU.min))
                    V.tensor_scalar(mbefore[:, d], mend, -1.0, None, ALU.mult).then_inc(args, 1)
                    e = n + 1 if i is None else 2 * NCC + i * 3 + 1
                    if i is not None:
                        dve.wait_ge(exps, e + 1)
                        V.tensor_tensor(qw[:], inter[:], q[:, :, bass.ds(c * CH, CH)], ALU.mult).then_inc(q_in, 1)
                        dve.wait_ge(exps, e + 2)
                        dve.wait_ge(qk_done, i + 1)
                        V.tensor_tensor(pt[:], arg[:], heads(pqk[:]), ALU.mult).then_inc(weighed, 1)
                    dve.wait_ge(exps, e)
                    dve.wait_ge(kt_done, n + 1)
                    V.tensor_tensor(kw[:], heads(pk[:]), wide(kd[:, 0]), ALU.mult).then_inc(kw_done, 1)
                    if i is not None:
                        dve.wait_ge(o_done, i + 1)
                        st.then(V.tensor_copy(den[:], pden[:, 0:H]))
                        st.then(V.scalar_tensor_tensor(den[:], den[:], -1.0, den[:], ALU.mult, ALU.max))
                        st.then(V.tensor_tensor(den[:], den[:], cols[:, 1, bass.ds(c, 1), 32 * d:32 * d + H].rearrange("p a h -> p (a h)"), ALU.max))
                        st.then(V.reciprocal(den[:], den[:]))
                        st.then(V.tensor_tensor(out[:, d, bass.ds(c - NCC, 1), :].rearrange("p a (h e) -> p (a h) e", h=H),
                                                heads(pn[:]), wide(den[:]), ALU.mult))
                    dve.wait_ge(stepped, n + 1)
                    st.then(V.tensor_tensor(state[:, d], state[:, d], wide(kd[:, 1]), ALU.mult))
                    st.then(V.tensor_tensor(state[:, d], state[:, d], heads(pst[:]), ALU.add))
                    st.then(V.tensor_tensor(norm[:, d], norm[:, d], kd[:, 1], ALU.mult))
                    st.then(V.tensor_tensor(norm[:, d], norm[:, d], pnorm[:, 0:H], ALU.add))

                steps(emit, dve)

            @block.tensor
            def _(pe):
                pe.wait_ge(got, 48)

                def emit(n, d, c, i):
                    pe.wait_ge(kw_done, n)
                    if i is not None:
                        pe.wait_ge(weighed, i)
                    for h in range(H):
                        mm = nc.tensor.matmul(pm[:, h * CH:(h + 1) * CH], pick[:, d * H + h, :], negm[:, bass.ds(c * CH, CH)], start=True, stop=True)
                    mm.then_inc(rows_up, 1)
                    pe.wait_ge(k_cut, n + 1)
                    for h in range(H):
                        mm = nc.tensor.transpose(pk[:, h * CH:(h + 1) * CH], kcur[:, h, :], C["ident"][:])
                    mm.then_inc(kt_done, 1)
                    if i is not None:
                        for h in range(H):
                            mm = nc.tensor.matmul(pqk[:, h * CH:(h + 1) * CH], kcur[:, h, :], q[:, h, bass.ds(c * CH, CH)], start=True, stop=True)
                        mm.then_inc(qk_done, 1)
                        pe.wait_ge(q_in, i + 1)
                        pe.wait_ge(weighed, i + 1)
                        for h in range(H):
                            nc.tensor.matmul(pn[:, h * CH:(h + 1) * CH], pt[:, h, :], v[:, bass.ds(c, 1), h * ML_D:(h + 1) * ML_D], start=True, stop=False)
                            nc.tensor.matmul(pn[:, h * CH:(h + 1) * CH], qw[:, h, :], state[:, d, h, :], start=False, stop=True)
                            nc.tensor.matmul(pden[:, h:h + 1], pt[:, h, :], ones1[:], start=True, stop=False)
                            mm = nc.tensor.matmul(pden[:, h:h + 1], qw[:, h, :], norm[:, d, h:h + 1], start=False, stop=True)
                        mm.then_inc(o_done, 1)
                    pe.wait_ge(kw_done, n + 1)
                    for h in range(H):
                        nc.tensor.matmul(pst[:, h * CH:(h + 1) * CH], kw[:, h, :], v[:, bass.ds(c, 1), h * ML_D:(h + 1) * ML_D], start=True, stop=True)
                        mm = nc.tensor.matmul(pnorm[:, h:h + 1], kw[:, h, :], ones1[:], start=True, stop=True)
                    mm.then_inc(stepped, 1)

                steps(emit, pe)


def mixer_norm(nc, A, R, out, mixT, C):
    H = 8
    with Stage(nc, "mn") as s:
        gate = s.sb("gate", [P, NCX, 2 * 512])
        sq = [s.sb(f"sq{j}", [P, D]) for j in range(2)]
        y = s.sb("y", [P, D])
        ss, gn = s.sb("ss", [P, NCX, H]), s.sb("gn", [P, KD])
        sig = s.sb("sig", [P, D])
        pt = [s.ps(f"pt{j}") for j in range(2)]
        got, rooted, meant, sig_done, sig_used, y_done, turned, moved, own = (
            s.sem(x) for x in ("got", "rooted", "meant", "sig_done", "sig_used", "y_done", "turned", "moved", "own"))
        with nc.Block() as block:
            @block.sync
            def _(sp):
                for x in range(2):
                    sp.dma_start(gate[:, :, x * 512:(x + 1) * 512], R["z_g"][x].rearrange("(c p) n -> p c n", p=P)).then_inc(got, 16)
                sp.dma_start(gn[:], A["mix_g"]).then_inc(got, 16)

            @block.vector
            def _(dve):
                V = nc.vector
                per = 3
                with dve.Fori(0, NCX) as c:
                    st = Steps(dve, own, c * per)
                    h = out[:, 0, bass.ds(c, 1), :].rearrange("p a n -> p (a n)")
                    st.then(V.tensor_tensor(h, h, out[:, 1, bass.ds(c, 1), :].rearrange("p a n -> p (a n)"), ALU.add))
                    st.then(V.tensor_tensor(sq[0][:], h, h, ALU.mult))
                    st.then(V.tensor_reduce(ss[:, bass.ds(c, 1), :].rearrange("p a h -> p (a h)"), sq[0][:].rearrange("p (h e) -> p h e", h=H), AX.X, ALU.add))
                V.tensor_scalar(ss[:], ss[:], 1.0 / CH, EPS, ALU.mult, ALU.add).then_inc(meant, 1)
                dve.wait_ge(rooted, 1)
                st = Steps(dve, own, NCX * per)
                st.then(V.reciprocal(ss[:], ss[:]))
                dve.wait_ge(got, 48)
                base, per2 = NCX * per + 1, 3
                with dve.Fori(0, NCX) as c:
                    st = Steps(dve, own, c * per2 + base)
                    h = out[:, 0, bass.ds(c, 1), :].rearrange("p a (h e) -> p (a h) e", h=H)
                    rs = ss[:, bass.ds(c, 1), :].rearrange("p a h -> p (a h)").unsqueeze(2).broadcast_to([P, H, CH])
                    st.then(V.tensor_tensor(sq[0][:].rearrange("p (h e) -> p h e", h=H), h, rs, ALU.mult))
                    g = gate[:, bass.ds(c, 1), 0:512].rearrange("p a n -> p (a n)")
                    st.then(V.tensor_tensor(sq[0][:, 0:512], sq[0][:, 0:512], g, ALU.mult))
                    dve.wait_ge(sig_done, c + 1)
                    dve.wait_ge(turned, c)
                    V.tensor_tensor(y[:], sq[0][:], sig[:], ALU.mult).then_inc(y_done, 1)
                    dve.wait_ge(y_done, c + 1)
                    V.memset(sq[1][:, 0:1], 0.0).then_inc(own, 1)

            @block.scalar
            def _(act):
                act.wait_ge(meant, 1)
                nc.scalar.activation(ss[:], ss[:], ACT.Sqrt).then_inc(rooted, 1)
                act.wait_ge(got, 48)
                with act.Fori(0, NCX) as c:
                    act.wait_ge(y_done, c)
                    nc.scalar.activation(sig[:], gate[:, bass.ds(c, 1), :].rearrange("p a n -> p (a n)"), ACT.Sigmoid).then_inc(sig_done, 1)
                    act.wait_ge(turned, c + 1)
                    for n in range(KD):
                        nc.scalar.activation(mixT[:, n, bass.ds(c * CH, CH)], pt[n // 4][:, n % 4 * CH:(n % 4 + 1) * CH], ACT.Copy,
                                             scale=gn[:, n:n + 1]).then_inc(moved, 1)

            @block.tensor
            def _(pe):
                with pe.Fori(0, NCX) as c:
                    pe.wait_ge(y_done, c + 1)
                    pe.wait_ge(moved, c * KD)
                    for n in range(KD):
                        mm = nc.tensor.transpose(pt[n // 4][:, n % 4 * CH:(n % 4 + 1) * CH], y[:, n * CH:(n + 1) * CH], C["ident"][:])
                    mm.then_inc(turned, 1)


def add_scaled(nc, gain):
    return lambda ns, out, ps, n, a, m, side: nc.vector.scalar_tensor_tensor(out, ps, gain(n), side, ALU.mult, ALU.add)


def router_logits(nc, A, R, h, L, C):
    with Stage(nc, "rl") as s:
        w, b = s.sb("w", [P, KD, NG + NE]), s.sb("b", [P, NG + NE])
        row = [s.sb(f"row{j}", [P, D]) for j in range(2)]
        pl, pt = [s.ps(f"pl{j}") for j in range(2)], [[s.ps(f"pt{j}{x}") for x in range(2)] for j in range(2)]
        got, logits, biased, turned, moved, stored = s.sem("got"), s.sem("logits"), s.sem("biased"), s.sem("turned"), s.sem("moved"), s.sems("stored", 2)
        with nc.Block() as block:
            @block.sync
            def _(sp):
                sp.dma_start(w[:], A["router_w"]).then_inc(got, 16)
                sp.dma_start(b[:], A["router_b"].broadcast_to([P, NG + NE])).then_inc(got, 16)
                for c in range(NCX):
                    sp.wait_ge(moved, 2 * c + 2)
                    sp.dma_start(R["h2rows"][c * P:(c + 1) * P, :], row[c % 2][:]).then_inc(stored[c % 2], 16)
                for j in range(2):
                    sp.wait_ge(stored[j], 16 * NCX // 2)

            @block.tensor
            def _(pe):
                pe.wait_ge(got, 32)
                for c in range(NCX):
                    if c >= 2:
                        pe.wait_ge(biased, c - 1)
                    for k in range(KD):
                        mm = nc.tensor.matmul(pl[c % 2][:, 0:NG + NE], h[:, k, c * P:(c + 1) * P], w[:, k, :], start=(k == 0), stop=(k == KD - 1))
                    mm.then_inc(logits, 1)
                    if c >= 2:
                        pe.wait_ge(moved, 2 * (c - 1))
                    for k in range(KD):
                        mm = nc.tensor.transpose(pt[c % 2][k // 4][:, k % 4 * P:(k % 4 + 1) * P], h[:, k, c * P:(c + 1) * P], C["ident"][:])
                    mm.then_inc(turned, 1)

            @block.vector
            def _(dve):
                dve.wait_ge(got, 32)
                for c in range(NCX):
                    dve.wait_ge(logits, c + 1)
                    nc.vector.tensor_tensor(L[:, c, :], pl[c % 2][:, 0:NG + NE], b[:], ALU.add).then_inc(biased, 1)

            @block.scalar
            def _(act):
                for c in range(NCX):
                    act.wait_ge(turned, c + 1)
                    if c >= 2:
                        act.wait_ge(stored[c % 2], 16 * (c // 2))
                    for x in range(2):
                        nc.scalar.activation(row[c % 2][:, x * BANK:(x + 1) * BANK], pt[c % 2][x][:], ACT.Copy).then_inc(moved, 1)


def route(nc, A, R, L, dest, wt, owner, pairs, C):
    G2 = [P, NCX, NG, EG]
    with Stage(nc, "rt") as s:
        oh, ohn = s.sb("oh", [P, NCX, NG]), s.sb("ohn", [P, NCX, NG])
        t8, gm, gs = s.sb("t8", [P, NCX]), s.sb("gm", [P, NCX]), s.sb("gs", [P, NCX])
        em, top, topi, topf = s.sb("em", [P, NCX, NE]), s.sb("top", [P, NCX, 8]), s.sb("topi", [P, NCX, 8], U32), s.sb("topf", [P, NCX, 2])
        hot, both, base = s.sb("hot", [P, NCX, 2, NE]), s.sb("both", [P, NCX, NE]), s.sb("base", [P, NCX, NE])
        cnt, nb, cum, one = s.sb("cnt", [P, NE]), s.sb("nb", [P, NE]), s.sb("cum", [P, NE]), s.sb("one", [P, NE])
        before = s.sb("before", [P, NE])
        destf, ids = s.sb("destf", [P, NCX, 2]), s.sb("ids", [P, NE])
        tok, zero = s.sb("tok", [P, NCX, 16], I32), s.sb("zero", [P, (NBLK + 1) * 16], I32)
        bids, evens, le = s.sb("bids", [P, NBLK + 2]), s.sb("evens", [P, NBLK + 2]), s.sb("le", [P, NBLK + 2, NE])
        pos, pc = s.ps("pos"), s.ps("pc")
        got, hots, counted, exps, placed, filled, noted, scattered, own = (
            s.sem(x) for x in ("got", "hots", "counted", "exps", "placed", "filled", "noted", "scattered", "own"))
        with nc.Block() as block:
            @block.sync
            def _(sp):
                sp.dma_start(ids[:], A["expert_ids"].broadcast_to([P, NE])).then_inc(got, 16)
                sp.dma_start(bids[:], A["block_ids"].broadcast_to([P, NBLK + 2])).then_inc(got, 16)
                sp.wait_ge(noted, 1)
                sp.dma_start(R["slots"].rearrange("(p a) n -> p (a n)", p=P), zero[:]).then_inc(filled, 16)

            @block.gpsimd
            def _(pool):
                nc.gpsimd.memset(zero[:], 0).then_inc(noted, 1)
                nc.gpsimd.iota(tok[:], pattern=[[P, NCX], [0, 16]], base=0, channel_multiplier=1).then_inc(noted, 1)
                pool.wait_ge(noted, 2)
                pool.wait_ge(placed, 1)
                pool.wait_ge(filled, 16)
                for c in range(NCX):
                    for k in range(2):
                        nc.gpsimd.indirect_dma_start(out=R["slots"], out_offset=bass.IndirectOffsetOnAxis(ap=dest[:, c, k:k + 1], axis=0),
                                                     in_=tok[:, c, :], in_offset=None).then_inc(scattered, 16)
                pool.wait_ge(scattered, 16 * 2 * NCX)

            @block.vector
            def _(dve):
                V = nc.vector
                st = Steps(dve, own)
                gl, el = L[:, :, 0:NG], L[:, :, NG:NG + NE]
                st.then(V.tensor_reduce(gm[:], gl, AX.X, ALU.max))
                gmw = gm[:].unsqueeze(2).broadcast_to([P, NCX, NG])
                st.then(V.tensor_tensor(oh[:], gl, gmw, ALU.is_equal))
                st.then(V.tensor_tensor(ohn[:], gl, gmw, ALU.subtract))
                dve.wait_ge(exps, 1)
                st.then(V.tensor_reduce(gs[:], ohn[:], AX.X, ALU.add))
                st.then(V.reciprocal(gs[:], gs[:]))
                st.then(V.tensor_copy(gm[:], oh[:, :, 0]))
                for g in range(1, NG):
                    st.then(V.tensor_scalar(t8[:], gm[:], -1.0, 1.0, ALU.mult, ALU.add))
                    st.then(V.tensor_tensor(oh[:, :, g], oh[:, :, g], t8[:], ALU.mult))
                    st.then(V.tensor_tensor(gm[:], gm[:], oh[:, :, g], ALU.add))
                st.then(V.tensor_scalar(ohn[:], oh[:], -NEG, NEG, ALU.mult, ALU.add))
                for g in range(NG):
                    part = em[:, :, g * EG:(g + 1) * EG]
                    w8 = lambda x: x[:, :, g:g + 1].broadcast_to([P, NCX, EG])
                    st.then(V.tensor_tensor(part, el[:, :, g * EG:(g + 1) * EG], w8(oh), ALU.mult))
                    st.then(V.tensor_tensor(part, part, w8(ohn), ALU.add))
                for c in range(NCX):
                    st.then(V.max(out=top[:, c, :], in_=em[:, c, :]))
                    st.then(V.max_index(out=topi[:, c, :], in_max=top[:, c, :], in_values=em[:, c, :]))
                st.then(V.tensor_copy(topf[:], topi[:, :, 0:2]))
                dve.wait_ge(got, 32)
                for k in range(2):
                    st.then(V.tensor_tensor(hot[:, :, k, :], ids[:].unsqueeze(1).broadcast_to([P, NCX, NE]),
                                            topf[:, :, k:k + 1].broadcast_to([P, NCX, NE]), ALU.is_equal))
                V.tensor_tensor(both[:], hot[:, :, 0, :], hot[:, :, 1, :], ALU.add).then_inc(hots, 1)
                st.then(V.tensor_tensor(t8[:], top[:, :, 1], top[:, :, 0], ALU.subtract))
                V.tensor_copy(gm[:], t8[:]).then_inc(hots, 1)
                dve.wait_ge(exps, 2)
                st.then(V.tensor_scalar(t8[:], gm[:], 1.0, None, ALU.add))
                st.then(V.reciprocal(t8[:], t8[:]))
                st.then(V.tensor_tensor(wt[:, :, 0], gs[:], t8[:], ALU.mult))
                st.then(V.tensor_tensor(wt[:, :, 1], wt[:, :, 0], gm[:], ALU.mult))
                dve.wait_ge(counted, 1)
                st.then(V.tensor_copy(cnt[:], pc[:, 0:NE]))
                st.then(V.memset(nb[:], 1.0))
                st.then(V.memset(one[:], 1.0))
                for j in range(1, SEQ // SLOT):
                    st.then(V.scalar_tensor_tensor(nb[:], cnt[:], float(SLOT * j), nb[:], ALU.is_gt, ALU.add))
                st.then(V.tensor_tensor_scan(out=cum[:], data0=one[:], data1=nb[:], initial=0.0, op0=ALU.mult, op1=ALU.add))
                st.then(V.tensor_tensor(before[:], cum[:], nb[:], ALU.subtract))
                st.then(V.scalar_tensor_tensor(evens[:], bids[:], 2.0, cum[:, NE - 1:NE].broadcast_to([P, NBLK + 2]), ALU.mult, ALU.is_lt))
                st.then(V.tensor_reduce(one[:, 0:1], evens[:], AX.X, ALU.add))
                st.then(V.tensor_copy(pairs[:], one[:, 0:1]))
                st.then(V.tensor_tensor(le[:], bids[:].unsqueeze(2).broadcast_to([P, NBLK + 2, NE]),
                                        cum[:].unsqueeze(1).broadcast_to([P, NBLK + 2, NE]), ALU.is_ge))
                st.then(V.tensor_reduce(bids[:], le[:], AX.X, ALU.add))
                st.then(V.tensor_scalar(bids[:], bids[:], float(NE - 1), None, ALU.min))
                st.then(V.tensor_copy(owner[:], bids[:]))
                st.then(V.tensor_scalar(before[:], before[:], float(SLOT), None, ALU.mult))
                st.then(V.tensor_tensor(base[:], pos[:, 0:NCX * NE].rearrange("p (c e) -> p c e", e=NE),
                                        before[:].unsqueeze(1).broadcast_to([P, NCX, NE]), ALU.add))
                for k in range(2):
                    st.then(V.tensor_tensor(hot[:, :, k, :], hot[:, :, k, :], base[:], ALU.mult))
                st.then(V.tensor_reduce(destf[:], hot[:], AX.X, ALU.add))
                V.tensor_copy(dest[:], destf[:]).then_inc(placed, 1)

            @block.scalar
            def _(act):
                act.wait_ge(own, 3)
                nc.scalar.activation(ohn[:], ohn[:], ACT.Exp).then_inc(exps, 1)
                act.wait_ge(hots, 2)
                nc.scalar.activation(gm[:], gm[:], ACT.Exp).then_inc(exps, 1)

            @block.tensor
            def _(pe):
                pe.wait_ge(hots, 1)
                for c in range(NCX):
                    for j in range(c):
                        nc.tensor.matmul(pos[:, c * NE:(c + 1) * NE], C["ones"][:], both[:, j, :], start=(j == 0), stop=False)
                    nc.tensor.matmul(pos[:, c * NE:(c + 1) * NE], C["earlier"][:], both[:, c, :], start=(c == 0), stop=True)
                for c in range(NCX):
                    mm = nc.tensor.matmul(pc[:, 0:NE], C["ones"][:], both[:, c, :], start=(c == 0), stop=(c == NCX - 1))
                mm.then_inc(counted, 1)


def experts(nc, A, R, owner, pairs, C):
    with Stage(nc, "ex") as s:
        raw = [s.sb(f"raw{c}", [P, D]) for c in range(4)]
        gh, gl, uh, ul = ([s.sb(f"{n}{j}", [P, KD, DE], F32R) for j in range(2)] for n in ("gh", "gl", "uh", "ul"))
        oh, ol = s.sb("oh", [P, DE // P, D], F32R), s.sb("ol", [P, DE // P, D], F32R)
        idx, x, y = s.sb("idx", [P, 16], I32), s.sb("x", [P, D]), s.sb("y", [P, D])
        xh, xl = s.sb("xh", [P, KD, P], F32R), s.sb("xl", [P, KD, P], F32R)
        hid, hh, hl = s.sb("hid", [P, DE]), s.sb("hh", [P, DE // P, P], F32R), s.sb("hl", [P, DE // P, P], F32R)
        px, ph, py = ([s.ps(f"{n}{j}") for j in range(2)] for n in ("px", "ph", "py"))
        pt, carry = s.ps("pt"), s.sb("carry", [P, 1])
        raw_in = s.sems("raw_in", 4)
        (zeroed, cleared, carried, rounded, left, idx_in, x_in, turned, xh_done, xl_done, g_done, u_done, silu, hid_done,
         h_turned, hh_done, hl_done, summed, taken, stored) = (s.sem(n) for n in (
             "zeroed", "cleared", "carried", "rounded", "left", "idx_in", "x_in", "turned", "xh_done", "xl_done", "g_done",
             "u_done", "silu", "hid_done", "h_turned", "hh_done", "hl_done", "summed", "taken", "stored"))
        chunk = lambda t, c: t[:].rearrange("p k n -> p (k n)")[:, c * D:(c + 1) * D]
        turn = lambda t: t[:].rearrange("p (k t) -> p k t", t=P)
        with nc.Block() as block:
            def count(eng):
                return eng.value_load(pairs[0:1, 0:1], min_val=NE // 2, max_val=NBLK // 2)

            @block.sync
            def _(sp):
                def unit(m, e, part):
                    for c in range(4):
                        if not isinstance(m, int) or m:
                            sp.wait_ge(left, m * 4 + c - 3)
                        sp.dma_start(raw[c][:], A["expert_w"][e * 12 + (part * 4 + c)]).then_inc(raw_in[c], 16)

                unit(0, 0, 0)
                unit(1, 0, 1)
                unit(2, 0, 2)
                sp.wait_ge(zeroed, 1)
                sp.dma_start(R["yrows"][NE * SLOT:NBLK * SLOT, :].rearrange("(b p) n -> p b n", p=P),
                             y[:].unsqueeze(1).broadcast_to([P, NBLK - NE, D])).then_inc(cleared, 16)
                n = count(sp)
                with sp.Fori(0, n) as i:
                    for j in range(2):
                        b = i * 2 + j
                        after = sp.value_load(owner[0:1, bass.ds(b + 1, 1)], min_val=0, max_val=NE - 1)
                        unit(b * 3 + 3, after, 0)
                        unit(b * 3 + 4, after, 1)
                        unit(b * 3 + 5, after, 2)
                        sp.wait_ge(taken, b * 2 + 2)
                        sp.dma_start(R["yrows"][bass.ds(b * SLOT, SLOT), :], y[:]).then_inc(stored, 16)

            @block.gpsimd
            def _(pool):
                n = count(pool)
                with pool.Fori(0, n * 2 + 1) as b:
                    pool.wait_ge(carried, b)
                    pool.wait_ge(x_in, b * 16)
                    pool.dma_start(idx[:], R["slots"][bass.ds(b * SLOT, SLOT), :]).then_inc(idx_in, 16)
                    pool.wait_ge(idx_in, b * 16 + 16)
                    pool.wait_ge(turned, b * 2)
                    nc.gpsimd.tensor_tensor(carry[:], C["ones"][:, 0:1], C["ones"][:, 0:1], ALU.add).then_inc(carried, 1)
                    nc.gpsimd.indirect_dma_start(out=x[:], out_offset=None, in_=R["h2rows"],
                                                 in_offset=bass.IndirectOffsetOnAxis(ap=idx[:, 0:1], axis=0)).then_inc(x_in, 16)

            @block.tensor
            def _(pe):
                def rows_turned(b):
                    pe.wait_ge(x_in, b * 16 + 16)
                    for k in range(KD):
                        mm = nc.tensor.transpose(px[k // 4][:, k % 4 * P:(k % 4 + 1) * P], x[:, k * P:(k + 1) * P], C["ident"][:])
                        if k % 4 == 3:
                            mm.then_inc(turned, 1)

                def up(b, wh, wl, out, unit, done):
                    pe.wait_ge(left, b * 12 + 4 * unit + 4)
                    for k in range(KD):
                        mm = product3(nc, out[:], (xh[:, k, :], xl[:, k, :]), (wh[:, k, :], wl[:, k, :]), k == 0, k == KD - 1)
                    mm.then_inc(done, 1)

                rows_turned(0)
                n = count(pe)
                with pe.Fori(0, n) as i:
                    for j in range(2):
                        b = i * 2 + j
                        pe.wait_ge(xl_done, b * 2 + 2)
                        pe.wait_ge(hid_done, b)
                        up(b, gh[j], gl[j], ph[0], 0, g_done)
                        up(b, uh[j], ul[j], ph[1], 1, u_done)
                        rows_turned(b + 1)
                        pe.wait_ge(hid_done, b + 1)
                        for k in range(DE // P):
                            mm = nc.tensor.transpose(pt[:, k * P:(k + 1) * P], hid[:, k * P:(k + 1) * P], C["ident"][:])
                        mm.then_inc(h_turned, 1)
                        pe.wait_ge(left, b * 12 + 12)
                        pe.wait_ge(hl_done, b + 1)
                        pe.wait_ge(taken, b * 2)
                        for g in range(2):
                            cut = slice(g * BANK, (g + 1) * BANK)
                            for k in range(DE // P):
                                mm = product3(nc, py[g][:], (hh[:, k, :], hl[:, k, :]), (oh[:, k, cut], ol[:, k, cut]), k == 0, k == DE // P - 1)
                            mm.then_inc(summed, 1)

            @block.scalar
            def _(act):
                S = nc.scalar

                def high(m, dst, cs=range(4)):
                    for c in cs:
                        act.wait_ge(raw_in[c], m * 16 + 16)
                        S.activation(chunk(dst, c), raw[c][:], ACT.Copy).then_inc(rounded, 1)

                def rows_high(b):
                    for g in range(2):
                        act.wait_ge(turned, b * 2 + g + 1)
                        S.activation(xh[:, 4 * g:4 * g + 4, :], turn(px[g]), ACT.Copy).then_inc(xh_done, 1)

                rows_high(0)
                high(0, gh[0])
                high(1, uh[0])
                n = count(act)
                with act.Fori(0, n) as i:
                    for j in range(2):
                        b = i * 2 + j
                        high(b * 3 + 2, oh)
                        act.wait_ge(g_done, b + 1)
                        S.activation(hid[:], ph[0][:], ACT.Silu).then_inc(silu, 1)
                        high(b * 3 + 3, gh[1 - j], range(2))
                        rows_high(b + 1)
                        act.wait_ge(h_turned, b + 1)
                        S.activation(hh[:], turn(pt), ACT.Copy).then_inc(hh_done, 1)
                        high(b * 3 + 3, gh[1 - j], range(2, 4))
                        high(b * 3 + 4, uh[1 - j])
                        act.wait_ge(cleared, 16)
                        act.wait_ge(summed, b * 2 + 2)
                        act.wait_ge(stored, b * 16)
                        S.activation(y[:, 0:BANK], py[0][:], ACT.Copy).then_inc(taken, 1)
                act.wait_ge(stored, n * 32)
                S.activation(hid[:, 0:1], hid[:, 0:1], ACT.Copy)

            @block.vector
            def _(dve):
                V = nc.vector

                def rest(m, dst, dst_high, cs=range(4)):
                    for c in cs:
                        dve.wait_ge(rounded, m * 4 + c + 1)
                        V.tensor_tensor(chunk(dst, c), raw[c][:], chunk(dst_high, c).bitcast(F32), ALU.subtract).then_inc(left, 1)

                def rows_rest(b):
                    for g in range(2):
                        dve.wait_ge(xh_done, b * 2 + g + 1)
                        V.tensor_tensor(xl[:, 4 * g:4 * g + 4, :], turn(px[g]), xh[:, 4 * g:4 * g + 4, :].bitcast(F32), ALU.subtract).then_inc(xl_done, 1)

                V.memset(y[:], 0.0).then_inc(zeroed, 1)
                rows_rest(0)
                rest(0, gl[0], gh[0])
                rest(1, ul[0], uh[0])
                n = count(dve)
                with dve.Fori(0, n) as i:
                    for j in range(2):
                        b = i * 2 + j
                        rest(b * 3 + 2, ol, oh)
                        rest(b * 3 + 3, gl[1 - j], gh[1 - j], range(1))
                        dve.wait_ge(u_done, b + 1)
                        dve.wait_ge(silu, b + 1)
                        V.tensor_tensor(hid[:], hid[:], ph[1][:], ALU.mult).then_inc(hid_done, 1)
                        rest(b * 3 + 3, gl[1 - j], gh[1 - j], range(1, 2))
                        rows_rest(b + 1)
                        dve.wait_ge(hh_done, b + 1)
                        V.tensor_tensor(hl[:], turn(pt), hh[:].bitcast(F32), ALU.subtract).then_inc(hl_done, 1)
                        rest(b * 3 + 3, gl[1 - j], gh[1 - j], range(2, 4))
                        rest(b * 3 + 4, ul[1 - j], uh[1 - j])
                        dve.wait_ge(cleared, 16)
                        dve.wait_ge(summed, b * 2 + 2)
                        dve.wait_ge(stored, b * 16)
                        V.tensor_copy(y[:, BANK:D], py[1][:]).then_inc(taken, 1)


def combine(nc, A, R, dest, wt, mod, x, C):
    with Stage(nc, "cb") as s:
        r = [[s.sb(f"r{j}{k}", [P, D]) for k in range(2)] for j in range(2)]
        y = [s.sb(f"y{j}", [P, D]) for j in range(2)]
        pt = [[s.ps(f"pt{j}{h}") for h in range(2)] for j in range(2)]
        got, mixed, turned, added, own = s.sems("got", 2), s.sem("mixed"), s.sem("turned"), s.sem("added"), s.sem("own")
        with nc.Block() as block:
            @block.gpsimd
            def _(pool):
                for c in range(NCX):
                    if c >= 2:
                        pool.wait_ge(mixed, c - 1)
                    for k in range(2):
                        nc.gpsimd.indirect_dma_start(out=r[c % 2][k][:], out_offset=None, in_=R["yrows"],
                                                     in_offset=bass.IndirectOffsetOnAxis(ap=dest[:, c, k:k + 1], axis=0)).then_inc(got[c % 2], 16)

            @block.vector
            def _(dve):
                st = Steps(dve, own)
                for c in range(NCX):
                    dve.wait_ge(got[c % 2], 32 * (c // 2 + 1))
                    if c >= 2:
                        dve.wait_ge(turned, c - 1)
                    st.then(nc.vector.tensor_scalar(y[c % 2][:], r[c % 2][0][:], wt[:, c, 0:1], None, ALU.mult))
                    nc.vector.scalar_tensor_tensor(y[c % 2][:], r[c % 2][1][:], wt[:, c, 1:2], y[c % 2][:], ALU.mult, ALU.add).then_inc(mixed, 1)
                    dve.wait_ge(turned, c + 1)
                    for k in range(KD):
                        xs = x[:, k, c * P:(c + 1) * P]
                        nc.vector.scalar_tensor_tensor(xs, pt[c % 2][k // 4][:, k % 4 * P:(k % 4 + 1) * P], mod[:, 5 * KD + k, 0:1], xs, ALU.mult, ALU.add).then_inc(added, 1)

            @block.tensor
            def _(pe):
                for c in range(NCX):
                    pe.wait_ge(mixed, c + 1)
                    if c >= 2:
                        pe.wait_ge(added, KD * (c - 1))
                    for k in range(KD):
                        mm = nc.tensor.transpose(pt[c % 2][k // 4][:, k % 4 * P:(k % 4 + 1) * P], y[c % 2][:, k * P:(k + 1) * P], C["ident"][:])
                    mm.then_inc(turned, 1)


def first_block(nc, A, R, C):
    with Stage(nc, "b1") as s:
        mod = s.sb("mod", [P, 6 * KD, 2])
        modulation(nc, A, mod)
        first_projection(nc, A, R, mod, C["ones"])
        grid_conv(nc, A, R)
        with Stage(nc, "mix") as m:
            mixT = m.sb("mixT", [P, KD, SEQ])
            with Stage(nc, "scans") as q:
                out = q.sb("out", [P, 2, NCX, 2 * 512])
                v = q.sb("v", [P, NCH, 512])
                with Stage(nc, "gla") as g:
                    qk, fac = g.sb("qk", [P, 2, NCH, 2, 3, CH]), g.sb("fac", [P, NCH, 2, 2, 3])
                    gla_gates(nc, A, R, qk, fac, mixT[:], v[:])
                    load(nc, "lv", [(v[:], R["z_v"][0].rearrange("(c p) n -> p c n", p=P))])
                    gla_scan(nc, A, R, qk, fac, v, out[:, :, :, 0:512], C)
                load(nc, "lv2", [(v[:], R["z_v"][1].rearrange("(c p) n -> p c n", p=P))])
                with Stage(nc, "ml") as g:
                    negm, cols = g.sb("negm", [64, TOT]), g.sb("cols", [P, 2, NCH, 64])
                    mlstm_gates(nc, A, R, negm, cols, C)
                    mlstm_scan(nc, A, R, negm, cols, v, out[:, :, :, 512:1024], C)
                mixer_norm(nc, A, R, out, mixT, C)
            mixh, mixl = m.sb("mixh", [P, KD, SEQ], F32R), m.sb("mixl", [P, KD, SEQ], F32R)
            split(nc, "mixs", mixT, mixh, mixl, KD)
            gemm(nc, "wo", A["w_out"], KD, KD, lambda k, a, m: (mixh[:, k, a:a + m], mixl[:, k, a:a + m]), SEQ,
                 add_scaled(nc, lambda n: mod[:, bass.ds(n + 2 * KD, 1), 0]), evac_on="vector",
                 out_dram=R["x1"], side_dram=A["xT"].rearrange("p k t -> k p t"))
        with Stage(nc, "moe") as m:
            dest, wt, owner, pairs = m.sb("dest", [P, NCX, 2], I32), m.sb("wt", [P, NCX, 2]), m.sb("owner", [P, NBLK + 2], I32), m.sb("pairs", [P, 1], I32)
            with Stage(nc, "route") as q:
                x, h, gain = q.sb("x", [P, KD, SEQ]), q.sb("h", [P, KD, SEQ]), q.sb("gain", [P, 2, KD])
                L = q.sb("L", [P, NCX, NG + NE])
                own = q.sem("own")
                load(nc, "l2", [(x[:], R["x1"].rearrange("k p t -> p k t")), (gain[:, 0, :], A["norm2_g"])])
                with nc.Block() as block:
                    @block.vector
                    def _(dve):
                        st = Steps(dve, own)
                        st.then(nc.vector.tensor_scalar(gain[:, 1, :], mod[:, 4 * KD:5 * KD, 0], 1.0, None, ALU.add))
                        st.then(nc.vector.tensor_tensor(gain[:, 0, :], gain[:, 0, :], gain[:, 1, :], ALU.mult))
                norm_channels(nc, "n2", x, SEQ, h, lambda k: gain[:, 0, k:k + 1], lambda k: mod[:, 3 * KD + k, 0:1], C["ones"])
                router_logits(nc, A, R, h, L, C)
                route(nc, A, R, L, dest, wt, owner, pairs, C)
            experts(nc, A, R, owner, pairs, C)
            with Stage(nc, "fin") as q:
                x, g = q.sb("x", [P, KD, SEQ]), q.sb("g", [P, KD])
                load(nc, "lf", [(x[:], R["x1"].rearrange("k p t -> p k t")), (g[:], A["final_g"])])
                combine(nc, A, R, dest, wt, mod, x, C)
                norm_channels(nc, "nf", x, SEQ, x, lambda k: g[:, k:k + 1], None, C["ones"])
                load(nc, "sx", [(R["xa"].rearrange("k p t -> p k t"), x[:])])


MH, NOPE, ROPE, VH = 8, 64, 32, 64
QL, KVL = 384, 256
TWO_PI_HI = 6.28125
TWO_PI_LO = 2 * math.pi - TWO_PI_HI
ROUND = 1.5 * 2.0 ** 23
U_CQ, U_CKV, U_POOL, U_XBC, U_LG, U_LX, U_KR = 0, 3, 5, 9, 15, 19, 23
N_U = 24


def rope_tables(nc, A, cosf, sinf):
    with Stage(nc, "rope") as s:
        pos, inv = s.sb("pos", [P, SEQ], I32), s.sb("inv", [P, 1])
        got, angled, own = s.sem("got"), s.sem("angled"), s.sem("own")
        with nc.Block() as block:
            @block.sync
            def _(sp):
                sp.dma_start(pos[:], A["positions"].broadcast_to([P, SEQ])).then_inc(got, 16)
                sp.dma_start(inv[:], A["rope_inv"]).then_inc(got, 16)

            @block.vector
            def _(dve):
                V, st = nc.vector, Steps(dve, own)
                dve.wait_ge(got, 32)
                st.then(V.tensor_copy(sinf[:], pos[:]))
                st.then(V.tensor_scalar(sinf[:], sinf[:], inv[:], None, ALU.mult))
                st.then(V.tensor_scalar(cosf[:], sinf[:], 1.0 / (2 * math.pi), None, ALU.mult))
                st.then(V.tensor_scalar(cosf[:], cosf[:], ROUND, None, ALU.add))
                st.then(V.tensor_scalar(cosf[:], cosf[:], ROUND, None, ALU.subtract))
                st.then(V.scalar_tensor_tensor(sinf[:], cosf[:], -TWO_PI_HI, sinf[:], ALU.mult, ALU.add))
                st.then(V.scalar_tensor_tensor(sinf[:], cosf[:], -TWO_PI_LO, sinf[:], ALU.mult, ALU.add))
                st.then(V.tensor_scalar(cosf[:], sinf[:], math.pi / 2, -2 * math.pi, ALU.is_gt, ALU.mult))
                st.then(V.scalar_tensor_tensor(cosf[:], sinf[:], math.pi / 2, cosf[:], ALU.add, ALU.add))
                for t in (cosf, sinf):
                    st.then(V.tensor_scalar(t[:], t[:], 3.1415925, -3.1415925, ALU.min, ALU.max))
                V.tensor_copy(inv[:], inv[:]).then_inc(angled, 1)

            @block.scalar
            def _(act):
                act.wait_ge(angled, 1)
                nc.scalar.activation(cosf[:], cosf[:], ACT.Sin).then_inc(own, 1)
                nc.scalar.activation(sinf[:], sinf[:], ACT.Sin).then_inc(own, 1)


def rotate(nc, name, q, n, cosf, sinf, swap):
    with Stage(nc, name) as s:
        t = s.sb("t", [P, SEQ])
        ps = s.ps("ps", [P, 2, BANK])
        swapped, taken, own = s.sem("swapped"), s.sem("taken"), s.sem("own")
        with nc.Block() as block:
            @block.tensor
            def _(pe):
                with pe.Fori(0, n) as h:
                    pe.wait_ge(taken, h)
                    for c in range(2):
                        mm = nc.tensor.matmul(ps[:, c, :], swap[:], q[:, bass.ds(h, 1), c * BANK:(c + 1) * BANK], start=True, stop=True)
                    mm.then_inc(swapped, 1)

            @block.vector
            def _(dve):
                with dve.Fori(0, n) as h:
                    st = Steps(dve, own, h * 2)
                    qh = q[:, bass.ds(h, 1), :].rearrange("p a t -> p (a t)")
                    dve.wait_ge(swapped, h + 1)
                    nc.vector.tensor_tensor(t[:], ps[:].rearrange("p a t -> p (a t)"), sinf[:], ALU.mult).then_inc(taken, 1)
                    st.then(nc.vector.tensor_tensor(qh, qh, cosf[:], ALU.mult))
                    dve.wait_ge(taken, h + 1)
                    st.then(nc.vector.tensor_tensor(qh, qh, t[:], ALU.add))


def attention(nc, q, k, v, o, C):
    QB = SEQ // P
    SCALE = (NOPE + ROPE) ** -0.5
    with Stage(nc, "at") as s:
        qc = [s.sb(f"qc{j}", [P, SEQ]) for j in range(2)]
        pr, pT = [s.sb(f"pr{j}", [P, SEQ]) for j in range(2)], [s.sb(f"pT{j}", [P, SEQ]) for j in range(2)]
        mx, sm = [s.sb(f"mx{j}", [P, 2]) for j in range(2)], [s.sb(f"sm{j}", [P, 2]) for j in range(2)]
        S = [s.ps(f"S{j}", [P, 2 * BANK]) for j in range(2)]
        T = [s.ps(f"T{j}") for j in range(2)]
        O = [s.ps(f"O{j}") for j in range(2)]
        cut, scored, maxed, exped, turned, moved, summed, taken, own = (
            s.sem(x) for x in ("cut", "scored", "maxed", "exped", "turned", "moved", "summed", "taken", "own"))
        NT = sum(-(-(b + 1) // 4) for b in range(QB))
        before = [sum(-(-(x + 1) // 4) for x in range(b)) for b in range(QB)]
        with nc.Block() as block:
            @block.scalar
            def _(act):
                with act.Fori(0, MH // 2) as i:
                    for j in range(2):
                        hd = i * 2 + j
                        act.wait_ge(summed, hd * QB)
                        nc.scalar.activation(qc[j][:], q[:, bass.ds(hd, 1), :].rearrange("p a t -> p (a t)"), ACT.Copy).then_inc(cut, 1)
                        for b in range(QB):
                            n, w = hd * QB + b, (b + 1) * P
                            act.wait_ge(maxed, n + 1)
                            nc.scalar.activation(pr[b % 2][:, 0:w], S[b % 2][:, 0:w], ACT.Exp, bias=mx[b % 2][:, 1:2], scale=SCALE,
                                                 accum_out=sm[b % 2][:, 0:1]).then_inc(exped, 1)
                            act.wait_ge(exped, n + 1)
                            for g in range(-(-(b + 1) // 4)):
                                m = min(4, b + 1 - 4 * g)
                                act.wait_ge(turned, hd * NT + before[b] + g + 1)
                                nc.scalar.activation(pT[b % 2][:, g * BANK:g * BANK + m * P], T[(before[b] + g) % 2][:, 0:m * P], ACT.Copy).then_inc(moved, 1)

            @block.vector
            def _(dve):
                V = nc.vector
                with dve.Fori(0, MH // 2) as i:
                    for j in range(2):
                        hd = i * 2 + j
                        st = Steps(dve, own, hd * (3 * QB))
                        for b in range(QB):
                            n, w = hd * QB + b, (b + 1) * P
                            dve.wait_ge(scored, n + 1)
                            st.then(V.tensor_tensor(S[b % 2][:, w - P:w], S[b % 2][:, w - P:w], C["cutq"][:], ALU.add))
                            st.then(V.reduce_max(mx[b % 2][:, 0:1], S[b % 2][:, 0:w], AX.X))
                            V.tensor_scalar(mx[b % 2][:, 1:2], mx[b % 2][:, 0:1], -SCALE, None, ALU.mult).then_inc(maxed, 1)
                            dve.wait_ge(exped, n + 1)
                            st.then(V.reciprocal(sm[b % 2][:, 1:2], sm[b % 2][:, 0:1]))
                            dve.wait_ge(summed, n + 1)
                            V.tensor_scalar(o[:, b, bass.ds(hd * VH, VH)], O[b % 2][:, 0:VH], sm[b % 2][:, 1:2], None, ALU.mult).then_inc(taken, 1)

            @block.tensor
            def _(pe):
                with pe.Fori(0, MH // 2) as i:
                    for j in range(2):
                        hd = i * 2 + j
                        pe.wait_ge(cut, hd + 1)

                        def score(b):
                            w = (b + 1) * P
                            for a, m in chunks_of(w):
                                mm = nc.tensor.matmul(S[b % 2][:, a:a + m], qc[j][:, b * P:(b + 1) * P], k[:, bass.ds(hd, 1), a:a + m], start=True, stop=True)
                            mm.then_inc(scored, 1)

                        pe.wait_ge(taken, hd * QB)
                        score(0)
                        for b in range(QB):
                            n = hd * QB + b
                            if b + 1 < QB:
                                score(b + 1)
                            pe.wait_ge(exped, n + 1)
                            for g in range(-(-(b + 1) // 4)):
                                if before[b] + g >= 2:
                                    pe.wait_ge(moved, hd * NT + before[b] + g - 1)
                                for x in range(4 * g, min(4 * g + 4, b + 1)):
                                    mm = nc.tensor.transpose(T[(before[b] + g) % 2][:, (x - 4 * g) * P:(x - 4 * g + 1) * P], pr[b % 2][:, x * P:(x + 1) * P], C["ident"][:])
                                mm.then_inc(turned, 1)
                            pe.wait_ge(moved, hd * NT + before[b] + -(-(b + 1) // 4))
                            if b >= 2:
                                pe.wait_ge(taken, n - 1)
                            for x in range(b + 1):
                                mm = nc.tensor.matmul(O[b % 2][:, 0:VH], pT[b % 2][:, x * P:(x + 1) * P], v[:, x, bass.ds(hd * VH, VH)], start=(x == 0), stop=(x == b))
                            mm.then_inc(summed, 1)


def to_channels(nc, name, o, nt, nk, dst, gain, C):
    with Stage(nc, name) as s:
        cur, out = s.sb("cur", [P, nk * P]), s.sb("out", [P, nk, nt * P])
        g = s.sb("g", [P, nk])
        ps = s.ps("ps")
        cut, turned, moved, got = s.sem("cut"), s.sem("turned"), s.sem("moved"), s.sem("got")
        with nc.Block() as block:
            @block.vector
            def _(dve):
                with dve.Fori(0, nt) as i:
                    dve.wait_ge(turned, i)
                    nc.vector.tensor_copy(cur[:], o[:, bass.ds(i, 1), :].rearrange("p a n -> p (a n)")).then_inc(cut, 1)

            @block.tensor
            def _(pe):
                with pe.Fori(0, nt) as i:
                    pe.wait_ge(cut, i + 1)
                    pe.wait_ge(moved, i * nk)
                    for k in range(nk):
                        mm = nc.tensor.transpose(ps[:, k * P:(k + 1) * P], cur[:, k * P:(k + 1) * P], C["ident"][:])
                    mm.then_inc(turned, 1)

            @block.scalar
            def _(act):
                if gain is not None:
                    act.dma_start(g[:], gain).then_inc(got, 16)
                    act.wait_ge(got, 16)
                with act.Fori(0, nt) as i:
                    act.wait_ge(turned, i + 1)
                    for k in range(nk):
                        nc.scalar.activation(out[:, k, bass.ds(i * P, P)], ps[:, k * P:(k + 1) * P], ACT.Copy,
                                             scale=1.0 if gain is None else g[:, k:k + 1]).then_inc(moved, 1)
                act.wait_ge(moved, nt * nk)
                act.dma_start(dst.rearrange("k p t -> p k t"), out[:]).then_inc(got, 16)
                act.wait_ge(got, 16 if gain is None else 32)


def mla(nc, A, R, C):
    with Stage(nc, "mla") as s:
        q, k, v = s.sb("q", [P, MH, SEQ]), s.sb("k", [P, MH, SEQ]), s.sb("v", [P, SEQ // P, MH * VH])
        with Stage(nc, "mlp") as m:
            cq, ckv, kr = m.sb("cq", [P, 3, SEQ]), m.sb("ckv", [P, 2, SEQ]), m.sb("kr", [P, 1, SEQ])
            cosf, sinf, swap = m.sb("cosf", [P, SEQ]), m.sb("sinf", [P, SEQ]), m.sb("swap", [P, P])
            gq, gkv, wv = m.sb("gq", [P, 3]), m.sb("gkv", [P, 2]), m.sb("wv", [P, 2, MH * VH])
            load(nc, "ldm", [(cq[:], R["u"][U_CQ:U_CQ + 3].rearrange("n p t -> p n t")), (ckv[:], R["u"][U_CKV:U_CKV + 2].rearrange("n p t -> p n t")),
                             (kr[:], R["u"][U_KR:U_KR + 1].rearrange("n p t -> p n t")), (swap[:], A["swap"]),
                             (gq[:], A["q_norm"]), (gkv[:], A["kv_norm"]), (wv[:], A["w_uv"])])
            rope_tables(nc, A, cosf, sinf)
            norm_channels(nc, "nq", cq, SEQ, cq, lambda n: gq[:, n:n + 1], None, C["ones"], width=QL)
            norm_channels(nc, "nkv", ckv, SEQ, ckv, lambda n: gkv[:, n:n + 1], None, C["ones"], width=KVL)
            gemm_small(nc, "uq", A["w_uq"], 3, MH, lambda n, a, w: cq[:, n, a:a + w], SEQ,
                 lambda ns, out, ps, n, a, w, side: nc.scalar.activation(q[:, bass.ds(n, 1), a:a + w], ps.unsqueeze(1), ACT.Copy))
            rotate(nc, "rotq", q, MH, cosf, sinf, swap)
            rotate(nc, "rotk", kr, 1, cosf, sinf, swap)
            gemm_small(nc, "uk", A["w_uk"], 2, MH, lambda n, a, w: ckv[:, n, a:a + w], SEQ,
                 lambda ns, out, ps, n, a, w, side: nc.vector.tensor_tensor(k[:, bass.ds(n, 1), a:a + w], ps.unsqueeze(1), kr[:, :, a:a + w], ALU.add), evac_on="vector")
            with Stage(nc, "uv") as u:
                ps = [u.ps(f"p{c}") for c in range(SEQ // P)]
                summed, moved = u.sem("summed"), u.sem("moved")
                with nc.Block() as block:
                    @block.tensor
                    def _(pe):
                        for c in range(SEQ // P):
                            for n in range(2):
                                mm = nc.tensor.matmul(ps[c][:], ckv[:, n, c * P:(c + 1) * P], wv[:, n, :], start=(n == 0), stop=(n == 1))
                            mm.then_inc(summed, 1)

                    @block.scalar
                    def _(act):
                        for c in range(SEQ // P):
                            act.wait_ge(summed, c + 1)
                            nc.scalar.activation(v[:, c, :], ps[c][:], ACT.Copy).then_inc(moved, 1)
        o = s.sb("o", [P, SEQ // P, MH * VH])
        attention(nc, q, k, v, o, C)
        to_channels(nc, "ato", o, SEQ // P, 4, R["y"][0:4], None, C)


def pool_mixer(nc, A, R, C):
    PAD = 16
    with Stage(nc, "po") as s:
        u = s.sb("u", [P, 4, SEQ])
        buf = [s.sb(f"b{j}", [P, PAD + SEQ]) for j in range(3)]
        inv, w, sc = s.sb("inv", [P, 4, SEQ]), s.sb("w", [P, 4, P]), s.sb("sc", [P, 4])
        d, y = s.sb("d", [P, 4, SEQ]), s.sb("y", [P, 4, SEQ])
        ps = [s.ps(f"p{c}") for c in range(8)]
        got, pooled, summed, own, moved = s.sem("got"), s.sem("pooled"), s.sem("summed"), s.sem("own"), s.sem("moved")
        with nc.Block() as block:
            @block.sync
            def _(sp):
                for a, b in ((u[:], R["u"][U_POOL:U_POOL + 4].rearrange("n p t -> p n t")), (inv[:], A["pool_inv"].rearrange("(o g) t -> o g t", o=1).broadcast_to([P, 4, SEQ])),
                             (w[:], A["w_pool"]), (sc[:], A["pool_scale"])):
                    sp.dma_start(a, b).then_inc(got, 16)
                sp.wait_ge(moved, 8)
                sp.dma_start(R["y"][4:8].rearrange("n p t -> p n t"), y[:]).then_inc(got, 16)
                sp.wait_ge(got, 80)

            @block.vector
            def _(dve):
                V, st = nc.vector, Steps(dve, own)
                for j in range(3):
                    st.then(V.memset(buf[j][:, 0:PAD], 0.0))
                dve.wait_ge(got, 64)
                for g in range(4):
                    st.then(V.tensor_copy(buf[0][:, PAD:], u[:, g, :]))
                    src = 0
                    for j in range(g + 1):
                        dst = 1 + j % 2
                        st.then(V.tensor_tensor(buf[dst][:, PAD:], buf[src][:, PAD:], buf[src][:, PAD - 2 ** j:PAD - 2 ** j + SEQ], ALU.add))
                        src = dst
                    st.then(V.tensor_tensor(d[:, g, :], buf[src][:, PAD:], inv[:, g, :], ALU.mult))
                    V.tensor_tensor(d[:, g, :], d[:, g, :], u[:, g, :], ALU.subtract).then_inc(pooled, 1)

            @block.tensor
            def _(pe):
                for g in range(4):
                    pe.wait_ge(pooled, g + 1)
                    for c in range(2):
                        nc.tensor.matmul(ps[2 * g + c][:], w[:, g, :], d[:, g, c * BANK:(c + 1) * BANK], start=True, stop=True).then_inc(summed, 1)

            @block.scalar
            def _(act):
                act.wait_ge(got, 64)
                for n in range(8):
                    act.wait_ge(summed, n + 1)
                    nc.scalar.activation(y[:, n // 2, n % 2 * BANK:(n % 2 + 1) * BANK], ps[n][:], ACT.Copy, scale=sc[:, n // 2:n // 2 + 1]).then_inc(moved, 1)


def conv_causal(V, st, out, x, w):
    st.then(V.tensor_scalar(out, x[:, 0:SEQ], w(0), None, ALU.mult))
    for i in range(1, 4):
        st.then(V.scalar_tensor_tensor(out, x[:, i:i + SEQ], w(i), out, ALU.mult, ALU.add))


def rglru(nc, A, R, C):
    with Stage(nc, "lr") as s:
        x = [s.sb(f"x{j}", [P, 3 + SEQ]) for j in range(2)]
        g = [s.sb(f"g{j}", [P, SEQ]) for j in range(2)]
        xc, r, it, a, t = (s.sb(n, [P, SEQ]) for n in ("xc", "r", "it", "a", "t"))
        wa, wi = s.sb("wa", [P, 4, P]), s.sb("wi", [P, 4, P])
        cw, cb, ba, bi, lam, sp8 = s.sb("cw", [P, 4, 4]), s.sb("cb", [P, 4]), s.sb("ba", [P, 4]), s.sb("bi", [P, 4]), s.sb("lam", [P, 4]), s.sb("sp8", [P, 4])
        ps = [s.ps(f"p{c}") for c in range(4)]
        got, x_in, convd, summed, gated, ready, own, stored, done, act_own, gelued = (
            s.sem("got"), s.sems("x_in", 2), *(s.sem(n) for n in ("convd", "summed", "gated", "ready", "own", "stored", "done", "act_own", "gelued")))
        with nc.Block() as block:
            @block.sync
            def _(sp):
                for p_, q_ in ((wa, "lru_w_a"), (wi, "lru_w_i"), (cw, "lru_conv_w"), (cb, "lru_conv_b"), (ba, "lru_b_a"), (bi, "lru_b_i"), (lam, "lru_lambda")):
                    sp.dma_start(p_[:], A[q_]).then_inc(got, 16)
                for n in range(4):
                    if n >= 2:
                        sp.wait_ge(stored, 16 * (n - 1))
                    sp.dma_start(x[n % 2][:, 3:], R["u"][U_LX + n]).then_inc(x_in[n % 2], 16)
                    sp.dma_start(g[n % 2][:], R["u"][U_LG + n]).then_inc(x_in[n % 2], 16)

            @block.vector
            def _(dve):
                V, st = nc.vector, Steps(dve, own)
                for j in range(2):
                    st.then(V.memset(x[j][:, 0:3], 0.0))
                dve.wait_ge(got, 112)
                st.then(V.scalar_tensor_tensor(sp8[:], lam[:], -1.0, lam[:], ALU.mult, ALU.min))
                dve.wait_ge(act_own, 2)
                st.then(V.tensor_scalar(lam[:], lam[:], -1.0, 0.0, ALU.mult, ALU.max))
                st.then(V.tensor_tensor(lam[:], lam[:], sp8[:], ALU.add))
                st.then(V.tensor_scalar(lam[:], lam[:], -8.0, None, ALU.mult))
                for n in range(4):
                    dve.wait_ge(x_in[n % 2], 32 * (n // 2 + 1))
                    conv_causal(V, st, xc[:], x[n % 2], lambda i: cw[:, n, i:i + 1])
                    V.tensor_scalar(xc[:], xc[:], cb[:, n:n + 1], None, ALU.add).then_inc(convd, 1)
                    dve.wait_ge(gated, 4 * n + 4)
                    V.tensor_scalar(r[:], r[:], lam[:, n:n + 1], None, ALU.mult).then_inc(ready, 1)
                    st.then(V.tensor_tensor(xc[:], xc[:], it[:], ALU.mult))
                    dve.wait_ge(act_own, 2 + 3 * n + 2)
                    st.then(V.tensor_tensor(it[:], a[:], a[:], ALU.mult))
                    st.then(V.scalar_tensor_tensor(t[:], it[:], 1.0, t[:], ALU.add, ALU.mult))
                    V.tensor_copy(it[:], t[:]).then_inc(ready, 1)
                    dve.wait_ge(act_own, 2 + 3 * n + 3)
                    st.then(V.tensor_tensor(xc[:], xc[:], it[:], ALU.mult))
                    st.then(V.tensor_tensor_scan(out=t[:], data0=a[:], data1=xc[:], initial=0.0, op0=ALU.mult, op1=ALU.add))
                    dve.wait_ge(gelued, n + 1)
                    V.tensor_tensor(g[n % 2][:], g[n % 2][:], t[:], ALU.mult).then_inc(done, 1)

            @block.tensor
            def _(pe):
                for n in range(4):
                    pe.wait_ge(convd, n + 1)
                    for c in range(4):
                        w = wa if c < 2 else wi
                        nc.tensor.matmul(ps[c][:], w[:, n, :], xc[:, c % 2 * BANK:(c % 2 + 1) * BANK], start=True, stop=True).then_inc(summed, 1)

            @block.scalar
            def _(act):
                S = nc.scalar
                act.wait_ge(got, 112)
                act.wait_ge(own, 3)
                S.activation(sp8[:], sp8[:], ACT.Exp).then_inc(act_own, 1)
                act.wait_ge(act_own, 1)
                S.activation(sp8[:], sp8[:], ACT.Ln, bias=1.0).then_inc(act_own, 1)
                for n in range(4):
                    for c in range(4):
                        act.wait_ge(summed, 4 * n + c + 1)
                        dst, b = (r, ba) if c < 2 else (it, bi)
                        S.activation(dst[:, c % 2 * BANK:(c % 2 + 1) * BANK], ps[c][:], ACT.Sigmoid, bias=b[:, n:n + 1]).then_inc(gated, 1)
                    act.wait_ge(ready, 2 * n + 1)
                    S.activation(a[:], r[:], ACT.Exp).then_inc(act_own, 1)
                    S.activation(t[:], r[:], ACT.Tanh, scale=-1.0).then_inc(act_own, 1)
                    act.wait_ge(x_in[n % 2], 32 * (n // 2 + 1))
                    S.activation(g[n % 2][:], g[n % 2][:], ACT.Gelu_apprx_tanh).then_inc(gelued, 1)
                    act.wait_ge(ready, 2 * n + 2)
                    S.activation(it[:], it[:], ACT.Sqrt).then_inc(act_own, 1)
                    act.wait_ge(done, n + 1)
                    act.dma_start(R["y"][12 + n], g[n % 2][:]).then_inc(stored, 16)
                    act.wait_ge(stored, 16 * n + 16)


SH, SHD, SDN = 8, 64, 64
NCK = SEQ // P


def ssd_conv(nc, A, R, xt, bt, bch, cz, C):
    with Stage(nc, "sc") as s:
        x = [s.sb(f"x{j}", [P, 3 + SEQ]) for j in range(2)]
        xo, cur = s.sb("xo", [P, 6, SEQ]), s.sb("cur", [P, 5, P])
        cw, cb = s.sb("cw", [P, 6, 4]), s.sb("cb", [P, 6])
        ps = s.ps("ps", [P, 2 * BANK])
        got, x_in, own, convd, silu, cut, turned, moved, padded = (s.sem("got"), s.sems("x_in", 2), *(s.sem(n) for n in (
            "own", "convd", "silu", "cut", "turned", "moved", "padded")))
        with nc.Block() as block:
            @block.sync
            def _(sp):
                sp.dma_start(cw[:], A["ssd_conv_w"]).then_inc(got, 16)
                sp.dma_start(cb[:], A["ssd_conv_b"]).then_inc(got, 16)
                for n in range(6):
                    if n >= 2:
                        sp.wait_ge(convd, n - 1)
                    sp.dma_start(x[n % 2][:, 3:], R["u"][U_XBC + n]).then_inc(x_in[n % 2], 16)

            @block.vector
            def _(dve):
                V, st = nc.vector, Steps(dve, own)
                for j in range(2):
                    st.then(V.memset(x[j][:, 0:3], 0.0))
                st.then(V.memset(cz[:], 0.0))
                dve.wait_ge(got, 32)
                for n in range(6):
                    dve.wait_ge(x_in[n % 2], 16 * (n // 2 + 1))
                    conv_causal(V, st, xo[:, n, :], x[n % 2], lambda i: cw[:, n, i:i + 1])
                    V.tensor_copy(cb[:, n:n + 1], cb[:, n:n + 1]).then_inc(convd, 1)
                with dve.Fori(0, NCK) as i:
                    dve.wait_ge(silu, 6)
                    dve.wait_ge(turned, i)
                    V.tensor_copy(cur[:], xo[:, 0:5, bass.ds(i * P, P)]).then_inc(cut, 1)
                V.tensor_copy(bch[:], xo[:, 4, :]).then_inc(padded, 1)
                for g in range(2):
                    V.tensor_copy(cz[g * 64:g * 64 + 64, g, :], xo[g * 64:g * 64 + 64, 5, :]).then_inc(padded, 1)
                dve.wait_ge(padded, 3)

            @block.scalar
            def _(act):
                act.wait_ge(got, 32)
                for n in range(6):
                    act.wait_ge(convd, n + 1)
                    nc.scalar.activation(xo[:, n, :], xo[:, n, :], ACT.Silu, bias=cb[:, n:n + 1]).then_inc(silu, 1)
                with act.Fori(0, NCK) as i:
                    act.wait_ge(turned, i + 1)
                    nc.scalar.activation(xt[:, bass.ds(i, 1), :], ps[:, 0:BANK].unsqueeze(1), ACT.Copy).then_inc(moved, 1)
                    nc.scalar.activation(bt[:, bass.ds(i, 1), :], ps[:, BANK:BANK + P].unsqueeze(1), ACT.Copy).then_inc(moved, 1)

            @block.tensor
            def _(pe):
                with pe.Fori(0, NCK) as i:
                    pe.wait_ge(cut, i + 1)
                    pe.wait_ge(moved, i * 2)
                    for n in range(5):
                        mm = nc.tensor.transpose(ps[:, n * P:(n + 1) * P], cur[:, n, :], C["ident"][:])
                    mm.then_inc(turned, 1)


def ssd_decays(nc, A, R, dt, a, acs, tot, eacs, back, incl, C):
    with Stage(nc, "sa") as s:
        al, bi, u = s.sb("al", [P, SH]), s.sb("bi", [P, SH]), s.sb("u", [P, NCK, SH])
        ps, pt = s.ps("ps"), s.ps("pt")
        got, own, ready, exped, summed = (s.sem(n) for n in ("got", "own", "ready", "exped", "summed"))
        with nc.Block() as block:
            @block.sync
            def _(sp):
                sp.dma_start(dt[:], R["dt2"][0].rearrange("(c p) h -> p c h", p=P)).then_inc(got, 16)
                sp.dma_start(al[:], A["ssd_a_log"].broadcast_to([P, SH])).then_inc(got, 16)
                sp.dma_start(bi[:], A["ssd_dt_bias"].broadcast_to([P, SH])).then_inc(got, 16)

            @block.vector
            def _(dve):
                V, st = nc.vector, Steps(dve, own)
                over = lambda x: x[:].unsqueeze(1).broadcast_to([P, NCK, SH])
                dve.wait_ge(got, 48)
                st.then(V.tensor_tensor(incl[:], C["earlier"][:], C["ident"][:], ALU.add))
                st.then(V.tensor_tensor(dt[:], dt[:], over(bi), ALU.add))
                V.scalar_tensor_tensor(u[:], dt[:], -1.0, dt[:], ALU.mult, ALU.min).then_inc(ready, 1)
                dve.wait_ge(exped, 3)
                st.then(V.scalar_tensor_tensor(dt[:], dt[:], 0.0, u[:], ALU.max, ALU.add))
                st.then(V.scalar_tensor_tensor(a[:], dt[:], -1.0, over(al), ALU.mult, ALU.mult))
                V.tensor_copy(al[:], al[:]).then_inc(ready, 1)
                dve.wait_ge(summed, 2)
                flat = lambda x: x[:].rearrange("p c h -> p (c h)")
                st.then(V.tensor_copy(flat(acs), ps[:, 0:NCK * SH]))
                st.then(V.tensor_copy(flat(tot), pt[:, 0:NCK * SH]))
                V.tensor_tensor(back[:], tot[:], acs[:], ALU.subtract).then_inc(ready, 1)

            @block.tensor
            def _(pe):
                pe.wait_ge(ready, 2)
                nc.tensor.matmul(ps[:, 0:NCK * SH], incl[:], a[:].rearrange("p c h -> p (c h)"), start=True, stop=True).then_inc(summed, 1)
                nc.tensor.matmul(pt[:, 0:NCK * SH], C["ones"][:], a[:].rearrange("p c h -> p (c h)"), start=True, stop=True).then_inc(summed, 1)

            @block.scalar
            def _(act):
                S = nc.scalar
                act.wait_ge(got, 48)
                S.activation(al[:], al[:], ACT.Exp).then_inc(exped, 1)
                act.wait_ge(ready, 1)
                S.activation(u[:], u[:], ACT.Exp).then_inc(exped, 1)
                act.wait_ge(exped, 2)
                S.activation(u[:], u[:], ACT.Ln, bias=1.0).then_inc(exped, 1)
                act.wait_ge(ready, 3)
                S.activation(eacs[:], acs[:], ACT.Exp).then_inc(exped, 1)
                S.activation(back[:], back[:], ACT.Exp).then_inc(exped, 1)
                S.activation(tot[:], tot[:], ACT.Exp).then_inc(exped, 1)


def ssd(nc, A, R, C):
    with Stage(nc, "sd") as s:
        xt, y = s.sb("xt", [P, NCK, SH * SHD]), s.sb("y", [P, NCK, SH * SHD])
        bt, bch, cz = s.sb("bt", [P, NCK, P]), s.sb("bch", [P, SEQ]), s.sb("cz", [P, 2, SEQ])
        dt, a, acs, tot, eacs, back = (s.sb(n, [P, NCK, SH]) for n in ("dt", "a", "acs", "tot", "eacs", "back"))
        incl = s.sb("incl", [P, P])
        ssd_conv(nc, A, R, xt, bt, bch, cz, C)
        ssd_decays(nc, A, R, dt, a, acs, tot, eacs, back, incl, C)
        with Stage(nc, "ss") as q:
            abc, L, M = q.sb("abc", [P, SH, P]), q.sb("L", [P, SH, P]), q.sb("M", [P, SH, P])
            bc, btc, cc = q.sb("bc", [P, P]), q.sb("btc", [P, P]), q.sb("cc", [P, 2, P])
            xdt, xb, S, t, dsk = (q.sb(n, [P, SH * SHD]) for n in ("xdt", "xb", "S", "t", "dsk"))
            d8 = q.sb("d8", [P, SH])
            rows, cb, yd, yo, new = q.ps("rows", [P, 2 * BANK]), q.ps("cb"), q.ps("yd"), q.ps("yo"), q.ps("new")
            got, own, cut, rowed, ready, exped, masked, summed, updated = (q.sem(n) for n in (
                "got", "own", "cut", "rowed", "ready", "exped", "masked", "summed", "updated"))
            heads = lambda x: x.rearrange("p (h d) -> p h d", h=SH)
            wide = lambda x: x.rearrange("p c h -> p (c h)").unsqueeze(2).broadcast_to([P, SH, SHD])
            with nc.Block() as block:
                @block.sync
                def _(sp):
                    sp.dma_start(d8[:], A["ssd_d"].broadcast_to([P, SH])).then_inc(got, 16)

                @block.vector
                def _(dve):
                    V = nc.vector
                    dve.wait_ge(got, 16)
                    V.tensor_copy(heads(dsk[:]), d8[:].unsqueeze(2).broadcast_to([P, SH, SHD])).then_inc(own, 1)
                    V.memset(S[:], 0.0).then_inc(own, 1)
                    dve.wait_ge(own, 2)
                    with dve.Fori(0, NCK) as i:
                        st = Steps(dve, own, i * 8 + 2)
                        at = lambda x: x[:, bass.ds(i, 1), :]
                        x_i = heads(at(xt).rearrange("p a n -> p (a n)"))
                        y_i = at(y).rearrange("p a n -> p (a n)")
                        V.tensor_copy(abc[:], at(a).rearrange("p c h -> p (c h)").unsqueeze(2).broadcast_to([P, SH, P])).then_inc(cut, 1)
                        V.tensor_copy(bc[:], bch[:, bass.ds(i * P, P)]).then_inc(cut, 1)
                        V.tensor_copy(cc[:], cz[:, :, bass.ds(i * P, P)]).then_inc(cut, 1)
                        V.tensor_copy(btc[:], at(bt).rearrange("p a n -> p (a n)")).then_inc(cut, 1)
                        st.then(V.tensor_tensor(heads(xdt[:]), x_i, wide(at(dt)), ALU.mult))
                        V.tensor_tensor(heads(xb[:]), heads(xdt[:]), wide(at(back)), ALU.mult).then_inc(cut, 1)
                        dve.wait_ge(rowed, i * 2 + 1)
                        st.then(V.tensor_tensor(L[:], heads(rows[:]), at(acs).rearrange("p c h -> p (c h)").unsqueeze(2).broadcast_to([P, SH, P]), ALU.subtract))
                        V.tensor_tensor(L[:], L[:], C["cut"][:, 0:1, :].broadcast_to([P, SH, P]), ALU.min).then_inc(ready, 1)
                        st.then(V.tensor_tensor(t[:], at(xt).rearrange("p a n -> p (a n)"), dsk[:], ALU.mult))
                        dve.wait_ge(exped, i + 1)
                        dve.wait_ge(rowed, i * 2 + 2)
                        for g in range(2):
                            V.tensor_tensor(M[:, 4 * g:4 * g + 4, :], L[:, 4 * g:4 * g + 4, :],
                                            cb[:, g * P:(g + 1) * P].unsqueeze(1).broadcast_to([P, 4, P]), ALU.mult).then_inc(masked, 1)
                        dve.wait_ge(summed, i * 3 + 1)
                        st.then(V.tensor_tensor(heads(y_i), heads(yo[:]), wide(at(eacs)), ALU.mult))
                        st.then(V.tensor_tensor(y_i, y_i, t[:], ALU.add))
                        st.then(V.tensor_tensor(heads(S[:]), heads(S[:]), wide(at(tot)), ALU.mult))
                        dve.wait_ge(summed, i * 3 + 2)
                        st.then(V.tensor_tensor(S[:], S[:], new[:], ALU.add))
                        dve.wait_ge(summed, i * 3 + 3)
                        st.then(V.tensor_tensor(y_i, y_i, yd[:], ALU.add))

                @block.tensor
                def _(pe):
                    mmul = nc.tensor.matmul
                    with pe.Fori(0, NCK) as i:
                        pe.wait_ge(cut, i * 5 + 5)
                        pe.wait_ge(own, i * 8 + 2)
                        for h in range(SH):
                            mm = mmul(rows[:, h * P:(h + 1) * P], abc[:, h, :], incl[:], start=True, stop=True)
                        mm.then_inc(rowed, 1)
                        for g in range(2):
                            mm = mmul(cb[:, g * P:(g + 1) * P], bc[:], cc[:, g, :], start=True, stop=True)
                        mm.then_inc(rowed, 1)
                        for g in range(2):
                            mm = mmul(yo[:, g * 256:(g + 1) * 256], cc[:, g, :], S[:, g * 256:(g + 1) * 256], start=True, stop=True)
                        mm.then_inc(summed, 1)
                        mmul(new[:], btc[:], xb[:], start=True, stop=True).then_inc(summed, 1)
                        pe.wait_ge(masked, i * 2 + 2)
                        for h in range(SH):
                            mm = mmul(yd[:, h * SHD:(h + 1) * SHD], M[:, h, :], xdt[:, h * SHD:(h + 1) * SHD], start=True, stop=True)
                        mm.then_inc(summed, 1)

                @block.scalar
                def _(act):
                    with act.Fori(0, NCK) as i:
                        act.wait_ge(ready, i + 1)
                        nc.scalar.activation(L[:], L[:], ACT.Exp).then_inc(exped, 1)
        with Stage(nc, "sg") as q:
            z, ms = q.sb("z", [P, NCK, SH * SHD]), q.sb("ms", [P, NCK])
            got, own, silu, rooted = (q.sem(n) for n in ("got", "own", "silu", "rooted"))
            with nc.Block() as block:
                @block.sync
                def _(sp):
                    sp.dma_start(z[:], R["z2"][0].rearrange("(c p) n -> p c n", p=P)).then_inc(got, 16)

                @block.scalar
                def _(act):
                    act.wait_ge(got, 16)
                    nc.scalar.activation(z[:], z[:], ACT.Silu).then_inc(silu, 1)
                    act.wait_ge(own, 4)
                    nc.scalar.activation(ms[:], ms[:], ACT.Sqrt).then_inc(rooted, 1)

                @block.vector
                def _(dve):
                    V, st = nc.vector, Steps(dve, own)
                    dve.wait_ge(silu, 1)
                    st.then(V.tensor_tensor(y[:], y[:], z[:], ALU.mult))
                    st.then(V.tensor_tensor(z[:], y[:], y[:], ALU.mult))
                    st.then(V.reduce_sum(ms[:], z[:], AX.X))
                    st.then(V.tensor_scalar(ms[:], ms[:], 1.0 / (SH * SHD), EPS, ALU.mult, ALU.add))
                    dve.wait_ge(rooted, 1)
                    st.then(V.reciprocal(ms[:], ms[:]))
                    st.then(V.tensor_tensor(y[:], y[:], ms[:].unsqueeze(2).broadcast_to([P, NCK, SH * SHD]), ALU.mult))
        to_channels(nc, "sdo", y, NCK, 4, R["y"][8:12], A["ssd_norm"], C)


def gated_products(nc, name, w, kb, h, y, acc):
    with Stage(nc, name) as s:
        W = Weights(nc, s, w, (KD + kb) * P, KD)
        sg, t = [s.sb(f"sg{j}", [P, SEQ]) for j in range(2)], s.sb("t", [P, SEQ])
        ps = [s.ps(f"g{j}", [P, 2 * BANK]) for j in range(2)]
        py = [s.ps(f"y{j}", [P, 2 * BANK]) for j in range(2)]
        summed, gated, taken, own = s.sem("summed"), s.sem("gated"), s.sem("taken"), s.sem("own")
        with nc.Block() as block:
            @block.sync
            def _(sp):
                W.load(sp)

            @block.gpsimd
            def _(pool):
                W.halve(pool)

            @block.tensor
            def _(pe):
                with pe.Fori(0, KD // 2) as i:
                    for j in range(2):
                        pe.wait_ge(W.split[j], i + 1)
                        pe.wait_ge(taken, i * 2)
                        for c in range(2):
                            cut = slice(c * BANK, (c + 1) * BANK)
                            for k in range(KD):
                                mm = product3(nc, ps[j][:, cut], W.tile(j, k), (h[0][:, k, cut], h[1][:, k, cut]), k == 0, k == KD - 1)
                        mm.then_inc(summed, 1)
                        for c in range(2):
                            cut = slice(c * BANK, (c + 1) * BANK)
                            for k in range(kb):
                                mm = product3(nc, py[j][:, cut], W.tile(j, KD + k), (y[0][:, k, cut], y[1][:, k, cut]), k == 0, k == kb - 1)
                        mm.then_inc(W.used[j], 1)

            @block.scalar
            def _(act):
                with act.Fori(0, KD // 2) as i:
                    for j in range(2):
                        act.wait_ge(summed, i * 2 + j + 1)
                        act.wait_ge(taken, i * 2)
                        nc.scalar.activation(sg[j][:], ps[j][:], ACT.Sigmoid).then_inc(gated, 1)

            @block.vector
            def _(dve):
                with dve.Fori(0, KD // 2) as i:
                    for j in range(2):
                        n = i * 2 + j
                        dve.wait_ge(W.used[j], i + 1)
                        dve.wait_ge(gated, n + 1)
                        dve.wait_ge(own, n)
                        nc.vector.tensor_tensor(t[:], sg[j][:], py[j][:], ALU.mult).then_inc(taken, 1)
                        dve.wait_ge(taken, n + 1)
                        a = acc[:, bass.ds(n, 1), :].rearrange("p a t -> p (a t)")
                        nc.vector.tensor_tensor(a, a, t[:], ALU.add).then_inc(own, 1)


def second_block(nc, A, R, C, out):
    tiles_of = lambda r: r.rearrange("k p t -> p k t")
    with Stage(nc, "b2") as s:
        gains = s.sb("gains", [P, 4, KD])
        high, rest = s.sb("high", [P, KD, SEQ], F32R), s.sb("rest", [P, KD, SEQ], F32R)
        pair = lambda k, a, m: (high[:, k, a:a + m], rest[:, k, a:a + m])
        with Stage(nc, "in5") as f:
            x = f.sb("x", [P, KD, SEQ])
            load(nc, "l5", [(gains[:, n, :], A[g]) for n, g in enumerate(("g_mix", "g_mlp", "g_ple", "g_final"))] + [(x[:], tiles_of(R["xa"]))])
            norm_split(nc, "n5", x, SEQ, high, rest, lambda k: gains[:, 0, k:k + 1], None, C["ones"])
        gemm(nc, "u1", A["w_in2"], KD, N_U, pair, SEQ, lambda ns, out, ps, n, a, m, side: ns.activation(out, ps, ACT.Copy), out_dram=R["u"])
        gemm_tokens(nc, "u2", A["w_in_z"], 1, 512, high, rest, 0, NCK, R["z2"])
        gemm_tokens(nc, "u3", A["w_in_dt"], 1, SH, high, rest, 0, NCK, R["dt2"])
        mla(nc, A, R, C)
        pool_mixer(nc, A, R, C)
        ssd(nc, A, R, C)
        rglru(nc, A, R, C)
        with Stage(nc, "out5") as f:
            x = f.sb("x", [P, KD, SEQ])
            branches(nc, A, R, x, high, rest)
            split(nc, "sm", x, high, rest, KD)
            gemm(nc, "wo2", A["w_out2"], KD, KD, pair, SEQ,
                 lambda ns, out, ps, n, a, w, side: ns.tensor_tensor(x[:, bass.ds(n, 1), a:a + w], ps.unsqueeze(1), side.unsqueeze(1), ALU.add),
                 evac_on="vector", side_dram=R["xa"])
            norm_split(nc, "n6", x, SEQ, high, rest, lambda k: gains[:, 1, k:k + 1], None, C["ones"])
            with Stage(nc, "ff") as g:
                hidh, hidl = g.sb("hidh", [P, KD, SEQ], F32R), g.sb("hidl", [P, KD, SEQ], F32R)
                for q in range(4):
                    feed_up(nc, f"fu{q}", A["w_ff1"][q * KD:(q + 1) * KD], pair, hidh, hidl)
                    gemm(nc, f"fd{q}", A["w_ff2"][q * KD:(q + 1) * KD], KD, KD, lambda k, a, m: (hidh[:, k, a:a + m], hidl[:, k, a:a + m]),
                         SEQ, onto(nc, x), evac_on="vector")
            norm_split(nc, "n7", x, SEQ, high, rest, lambda k: gains[:, 2, k:k + 1], None, C["ones"])
            with Stage(nc, "pl") as g:
                p_, ph, pl = g.sb("p", [P, 2, SEQ]), g.sb("ph", [P, 2, SEQ], F32R), g.sb("pl", [P, 2, SEQ], F32R)
                load(nc, "lp", [(p_[:], A["pT"])])
                split(nc, "sp", p_, ph, pl, 2)
                gated_products(nc, "ple", A["w_ple"], 2, (high, rest), (ph, pl), x)
            norm_channels(nc, "n8", x, SEQ, x, lambda k: gains[:, 3, k:k + 1], None, C["ones"])
            load(nc, "store", [(out, x[:])])


def onto(nc, x):
    def evac(ns, out, ps, n, a, m, side):
        t = x[:, bass.ds(n, 1), a:a + m]
        return ns.tensor_tensor(t, t, ps.unsqueeze(1), ALU.add)
    return evac


def branches(nc, A, R, merged, high, rest):
    with Stage(nc, "branch") as g:
        y, yh, yl = g.sb("y", [P, 4, SEQ]), g.sb("yh", [P, 4, SEQ], F32R), g.sb("yl", [P, 4, SEQ], F32R)
        zeroed = g.sem("zeroed")
        with nc.Block() as block:
            @block.vector
            def _(dve):
                nc.vector.memset(merged[:], 0.0).then_inc(zeroed, 1)
                dve.wait_ge(zeroed, 1)
        for b in range(4):
            load(nc, f"ly{b}", [(y[:], R["y"][4 * b:4 * b + 4].rearrange("k p t -> p k t"))])
            split(nc, f"sy{b}", y, yh, yl, 4)
            gated_products(nc, f"br{b}", A["w_merge"][KD * b:KD * (b + 1)], 4, (high, rest), (yh, yl), merged)


def feed_up(nc, name, w, rhs, hidh, hidl):
    with Stage(nc, name) as s:
        W = Weights(nc, s, w, D, KD)
        t = [s.sb(f"t{j}", [P, 1, SEQ]) for j in range(2)]
        ps = [s.ps(f"p{j}", [P, 2 * BANK]) for j in range(2)]
        taken, squared, rounded, left = s.sem("taken"), s.sem("squared"), s.sem("hid_rounded"), s.sem("left")
        with nc.Block() as block:
            @block.sync
            def _(sp):
                W.load(sp)

            @block.gpsimd
            def _(pool):
                W.halve(pool)

            @block.tensor
            def _(pe):
                with pe.Fori(0, KD // 2) as i:
                    for j in range(2):
                        pe.wait_ge(W.split[j], i + 1)
                        pe.wait_ge(taken, i * 2)
                        for c in range(2):
                            for k in range(KD):
                                mm = product3(nc, ps[j][:, c * BANK:(c + 1) * BANK], W.tile(j, k), rhs(k, c * BANK, BANK), k == 0, k == KD - 1)
                        mm.then_inc(W.used[j], 1)

            @block.scalar
            def _(act):
                with act.Fori(0, KD // 2) as i:
                    for j in range(2):
                        n = i * 2 + j
                        act.wait_ge(W.used[j], i + 1)
                        act.wait_ge(left, i * 2)
                        nc.scalar.activation(t[j][:], ps[j][:].unsqueeze(1), ACT.Relu).then_inc(taken, 1)
                        act.wait_ge(squared, n + 1)
                        nc.scalar.activation(hidh[:, bass.ds(n, 1), :], t[j][:], ACT.Copy).then_inc(rounded, 1)

            @block.vector
            def _(dve):
                with dve.Fori(0, KD // 2) as i:
                    for j in range(2):
                        n = i * 2 + j
                        dve.wait_ge(taken, n + 1)
                        nc.vector.tensor_tensor(t[j][:], t[j][:], t[j][:], ALU.mult).then_inc(squared, 1)
                        dve.wait_ge(rounded, n + 1)
                        nc.vector.tensor_tensor(hidl[:, bass.ds(n, 1), :], t[j][:], hidh[:, bass.ds(n, 1), :].bitcast(F32), ALU.subtract).then_inc(left, 1)
                dve.wait_ge(left, KD)


SCRATCH = dict(z_cm=(CM1, P, TOT), z_v=(2, TOT, 512), z_g=(2, SEQ, 512), mqk=(8, P, TOT),
               x1=(KD, P, SEQ), h2rows=(SEQ, D), yrows=(NBLK * SLOT, D),
               u=(N_U, P, SEQ), y=(16, P, SEQ), z2=(1, SEQ, MH * VH), dt2=(1, SEQ, SH), xa=(KD, P, SEQ), xb=(KD, P, SEQ))


def program(nc, A, out):
    R = {k: nc.dram_tensor(k, shape, F32, kind="Internal").ap() for k, shape in SCRATCH.items()}
    R["slots"] = nc.dram_tensor("slots", ((NBLK + 1) * SLOT, 16), I32, kind="Internal").ap()
    with Stage(nc, "all") as s:
        C = {k: s.sb(k, shape, dt) for k, shape, dt in (
            ("keep", [P, 2, P], I32), ("cut", [P, 2, P], F32), ("cutq", [P, P], F32), ("ident", [P, P], F32),
            ("earlier", [P, P], F32))}
        load(nc, "consts", [(t[:], A[k]) for k, t in C.items()])
        C["ones"] = s.sb("ones", [P, P])
        filled = s.sem("filled")
        with nc.Block() as block:
            @block.vector
            def _(dve):
                nc.vector.memset(C["ones"][:], 1.0).then_inc(filled, 1)
                dve.wait_ge(filled, 1)
        first_block(nc, A, R, C)
        second_block(nc, A, R, C, out)


def tiles(w):
    k, n = w.shape
    return np.ascontiguousarray(w.reshape(k // P, P, n // P, P).transpose(2, 1, 0, 3)).reshape(n // P, P, k)


def slabs(w, width):
    k, n = w.shape
    return np.ascontiguousarray(w.reshape(k // P, P, n // width, width).transpose(2, 1, 0, 3)).reshape(n // width, P, -1)


def columns(v):
    return np.ascontiguousarray(v.reshape(-1, P).T)


def lay_out(I):
    A = {}
    A["xT"] = I["x"][0].T.reshape(KD, P, SEQ).transpose(1, 0, 2)
    A["ctxT"] = I["ctx"][0].T.reshape(KD, P, CTX).transpose(1, 0, 2)
    A["c2"] = np.stack([I["c"][0], I["c_ctx"]], -1).reshape(KD, P, 2).transpose(1, 0, 2)
    A["ada_w"] = tiles(I["ada_w"][0]).reshape(12, 4, P, D).transpose(0, 2, 1, 3).reshape(12, P, 4 * D)
    A["ada_b"] = columns(I["ada_b"][0])
    A["norm1_g"] = columns(I["norm1_g"][0])
    w = I["w_in"][0]
    q, k, v, g, lr, mqk, mv, mo, mi, mf = np.split(w, np.cumsum([256, 256, 512, 512, 32, 1024, 512, 512, 8]), axis=1)
    small = np.zeros((D, 2 * P), w.dtype)
    small[:, 0:16], small[:, 32:48], small[:, 64:72], small[:, 96:104] = lr[:, :16], lr[:, 16:], mi, mf
    A["w_in_cm"] = tiles(np.concatenate([q, k, mqk, small], 1))
    A["w_in_v"] = slabs(np.concatenate([v, mv], 1), 512)
    A["w_in_g"] = slabs(np.concatenate([g, mo], 1), 512)
    A["conv_w"] = I["ml_conv_w"][0].reshape(9, 8, P).transpose(2, 1, 0)
    A["conv_b"] = columns(I["ml_conv_b"][0])
    A["conv_post"] = np.repeat(np.array([1.0] * 4 + [ML_D ** -0.5] * 4, np.float32)[None], P, 0)
    up = np.zeros((P, 2, P), np.float32)
    for d in range(2):
        up[32 * d:32 * d + 16] = I["gla_up_w"][0][d].reshape(16, 2, P)
    A["gla_up_w"] = up
    A["gla_up_b"] = I["gla_up_b"][0].reshape(4, P).T
    sm = np.ones((2, TOT), np.float32)
    sm[0, ::CH] = 0
    sm[1, CH - 1::CH] = 0
    A["scan_mask"] = sm
    gate = np.zeros((2, 64, 1), np.float32)
    for d in range(2):
        gate[0, 32 * d:32 * d + 4, 0], gate[1, 32 * d:32 * d + 4, 0] = I["ml_i_b"][0][d], I["ml_f_b"][0][d]
    A["ml_i_b"], A["ml_f_b"] = gate
    t = np.arange(P)
    keep = np.stack([t[:, None] <= t[None], t[:, None] >= t[None]], 1)
    A["keep"] = keep.astype(np.int32)
    A["cut"] = np.where(keep, 0.0, NEG).astype(np.float32)
    A["cutq"] = A["cut"][:, 1]
    A["ident"] = np.eye(P, dtype=np.float32)
    pick = np.zeros((64, 8, P), np.float32)
    for d in range(2):
        for n in range(4):
            pick[32 * d + n, 4 * d + n] = 1
    A["pick"] = pick
    A["earlier"] = (t[:, None] < t[None]).astype(np.float32)
    A["mix_g"] = columns(np.concatenate([I["gla_norm_g"][0], I["ml_norm_g"][0]]))
    A["w_out"] = tiles(I["w_out"][0])
    A["norm2_g"], A["final_g"] = columns(I["norm2_g"][0]), columns(I["final_norm_g"])
    A["router_w"] = np.concatenate([I["router_group_w"][0], I["router_expert_w"][0]], 1).reshape(KD, P, NG + NE).transpose(1, 0, 2)
    A["router_b"] = np.concatenate([I["router_group_b"][0], I["router_expert_b"][0]])[None]
    A["expert_ids"] = np.arange(NE, dtype=np.float32)[None]
    A["block_ids"] = np.arange(NBLK + 2, dtype=np.float32)[None]
    up = I["expert_w_in"][0].reshape(NE, 4, 2, P, 2, DE).transpose(0, 4, 1, 3, 2, 5).reshape(NE, 8, P, D)
    A["expert_w"] = np.concatenate([up, I["expert_w_out"][0].reshape(NE, 4, P, D)], 1).reshape(NE * 12, P, D)
    lay_out_second(I, A)
    return A


def lay_out_second(I, A):
    J = {k[:-2]: v for k, v in I.items() if k.endswith("_2")}
    w = J["w_in"][0]
    cq, ckv, kr, po, z, xbc, dt, lg, lx, gates = np.split(w, np.cumsum([384, 256, 32, 512, 512, 768, 8, 512, 512]), axis=1)
    last = np.zeros((D, P), w.dtype)
    last[:, NOPE:NOPE + ROPE] = kr
    A["w_in2"] = tiles(np.concatenate([cq, ckv, po, xbc, lg, lx, last], 1))
    A["w_in_z"], A["w_in_dt"] = slabs(z, 512), slabs(dt, SH)
    for k in ("g_mix", "g_mlp", "g_ple", "q_norm", "kv_norm", "pool_scale", "ssd_conv_b", "ssd_norm",
              "lru_conv_b", "lru_b_a", "lru_b_i", "lru_lambda"):
        A[k] = columns(J[k][0])
    A["g_final"] = columns(J["g_final"])
    A["positions"] = J["positions"]
    half = ROPE // 2
    inv = (np.float32(1.0) / np.power(np.float32(10000.0), np.arange(0, ROPE, 2, dtype=np.float32) / np.float32(ROPE))).astype(np.float32)
    A["rope_inv"] = np.zeros((P, 1), np.float32)
    A["rope_inv"][NOPE:NOPE + half, 0] = A["rope_inv"][NOPE + half:NOPE + ROPE, 0] = inv
    swap = np.zeros((P, P), np.float32)
    for n in range(half):
        swap[NOPE + half + n, NOPE + n], swap[NOPE + n, NOPE + half + n] = -1, 1
    A["swap"] = swap
    uq = np.zeros((QL, MH, P), w.dtype)
    uq[:, :, 0:NOPE + ROPE] = J["w_uq"][0].reshape(QL, MH, NOPE + ROPE)
    A["w_uq"] = tiles(uq.reshape(QL, MH * P))
    ukv = J["w_ukv"][0].reshape(KVL, MH, NOPE + VH)
    uk = np.zeros((KVL, MH, P), w.dtype)
    uk[:, :, 0:NOPE] = ukv[:, :, 0:NOPE]
    A["w_uk"] = tiles(uk.reshape(KVL, MH * P))
    A["w_uv"] = ukv[:, :, NOPE:].reshape(2, P, MH * VH).transpose(1, 0, 2)
    t = np.arange(SEQ)
    A["pool_inv"] = np.stack([np.float32(1.0) / np.minimum(t + 1, n).astype(np.float32) for n in (2, 4, 8, 16)])
    A["w_pool"] = J["w_pool"][0].transpose(1, 0, 2)
    A["ssd_conv_w"] = J["ssd_conv_w"][0].reshape(4, 6, P).transpose(2, 1, 0)
    for k in ("ssd_a_log", "ssd_dt_bias", "ssd_d"):
        A[k] = J[k]
    for k in ("lru_w_a", "lru_w_i"):
        blocks = np.zeros((P, 4, P), w.dtype)
        for n in range(8):
            r = slice(n % 2 * 64, n % 2 * 64 + 64)
            blocks[r, n // 2, r] = J[k][0][n]
        A[k] = blocks
    A["lru_conv_w"] = J["lru_conv_w"][0].reshape(4, 4, P).transpose(2, 1, 0)
    gate = tiles(gates).reshape(4, KD, P, D)
    branch = np.stack([tiles(J["w_branch"][0][n]) for n in range(4)])
    A["w_merge"] = np.concatenate([gate, branch], -1).reshape(4 * KD, P, -1)
    A["w_out2"], A["w_ff1"], A["w_ff2"] = tiles(J["w_out"][0]), tiles(J["w_ff1"][0]), np.concatenate([tiles(part) for part in np.split(J["w_ff2"][0], 4)])
    A["w_ple"] = np.concatenate([tiles(J["w_ple_gate"][0]), tiles(J["w_ple"][0])], -1)
    A["pT"] = J["p"][0, 0].T.reshape(2, P, SEQ).transpose(1, 0, 2)




def kernel(**inputs):
    import concourse.bacc as bacc
    from concourse.bass_utils import run_bass_kernel_spmd

    nc = bacc.Bacc("TRN2", target_bir_lowering=False, num_devices=1)
    arrays = {"in_" + k: np.ascontiguousarray(v) for k, v in lay_out({k: np.asarray(v) for k, v in inputs.items()}).items()}
    A = {k[3:]: nc.dram_tensor(k, v.shape, mybir.dt.from_np(v.dtype), kind="ExternalInput").ap() for k, v in arrays.items()}
    out = nc.dram_tensor("out", (P, KD, SEQ), F32, kind="ExternalOutput").ap()
    program(nc, A, out)
    r = run_bass_kernel_spmd(nc, [arrays], core_ids=[0])
    return r.results[0]["out"].transpose(1, 0, 2).reshape(1, D, SEQ).transpose(0, 2, 1)
```

```python
import math
from contextlib import ExitStack

import numpy as np

import concourse.bass as bass
from concourse import mybir

F32 = mybir.dt.float32
I32 = mybir.dt.int32
F32R = mybir.dt.float32r
U32 = mybir.dt.uint32
ALU = mybir.AluOpType
ACT = mybir.ActivationFunctionType
AX = mybir.AxisListType

P = 128
D = 1024
KD = D // P
SEQ, CTX = 1024, 256
TOT = CTX + SEQ
EPS = 1e-6
CH = 128
NCC, NCX = CTX // CH, SEQ // CH
NCH = NCC + NCX
GRID_W = 64
NEG = -1e30
BANK = 512
NE, NG, EG, DE = 32, 4, 8, 512
SLOT = 128
NBLK = SEQ * 2 // SLOT + NE


class Stage:

    def __init__(self, nc, name):
        self.nc, self.name, self.stack, self.used = nc, name, ExitStack(), []

    def __enter__(self):
        return self

    def __exit__(self, *a):
        if self.used and a[0] is None:
            self.nc.clear_and_free_semaphores(self.used)
            self.nc.all_engine_barrier()
        return self.stack.__exit__(*a)

    def sb(self, name, shape, dt=F32):
        return self.stack.enter_context(self.nc.sbuf_tensor(f"{self.name}_{name}", shape, dt))

    def ps(self, name, shape=(P, BANK)):
        return self.stack.enter_context(self.nc.psum_tensor(f"{self.name}_{name}", list(shape), F32))

    def sem(self, name):
        self.used.append(self.nc.alloc_semaphore(f"{self.name}_{name}"))
        return self.used[-1]

    def sems(self, name, n):
        return [self.sem(f"{name}{i}") for i in range(n)]


class Steps:

    def __init__(self, eng, sem, n=0):
        self.eng, self.sem, self.n = eng, sem, n

    def then(self, ins):
        ins.then_inc(self.sem, 1)
        self.n = self.n + 1
        self.eng.wait_ge(self.sem, self.n)


def chunks_of(total, step=BANK):
    return [(a, min(step, total - a)) for a in range(0, total, step)]


def load(nc, name, pairs):
    with Stage(nc, name) as s:
        loaded = s.sem("loaded")
        with nc.Block() as block:
            @block.sync
            def _(sp):
                for dst, src in pairs:
                    sp.dma_start(dst, src).then_inc(loaded, 16)
                sp.wait_ge(loaded, 16 * len(pairs))


def product3(nc, out, w, x, first, last):
    nc.tensor.matmul(out, w[0], x[0], start=first, stop=False)
    nc.tensor.matmul(out, w[0], x[1], start=False, stop=False)
    return nc.tensor.matmul(out, w[1], x[0], start=False, stop=last)


def split(nc, name, t, high, rest, n):
    with Stage(nc, name) as s:
        rounded, left = s.sem("rounded"), s.sem("left")
        with nc.Block() as block:
            @block.scalar
            def _(act):
                for k in range(n):
                    nc.scalar.activation(high[:, k], t[:, k], ACT.Copy).then_inc(rounded, 1)

            @block.vector
            def _(dve):
                for k in range(n):
                    dve.wait_ge(rounded, k + 1)
                    nc.vector.tensor_tensor(rest[:, k], t[:, k], high[:, k].bitcast(F32), ALU.subtract).then_inc(left, 1)
                dve.wait_ge(left, n)


class Weights:

    def __init__(self, nc, s, w, size, turns):
        self.nc, self.w, self.turns = nc, w, turns
        self.raw = [s.sb(f"raw{j}", [P, size]) for j in range(2)]
        self.high = [s.sb(f"high{j}", [P, size], F32R) for j in range(2)]
        self.one, self.filled = s.sb("one", [P, 1]), s.sem("filled")
        self.low = [s.sb(f"low{j}", [P, size], F32R) for j in range(2)]
        self.w_in, self.rounded, self.split, self.used = s.sems("w_in", 2), s.sem("rounded"), s.sems("split", 2), s.sems("used", 2)

    def load(self, sp):
        with sp.Fori(0, self.turns // 2) as i:
            for j in range(2):
                sp.wait_ge(self.split[j], i)
                sp.dma_start(self.raw[j][:], self.w[i * 2 + j]).then_inc(self.w_in[j], 16)

    def halve(self, pool):
        g = self.nc.gpsimd
        g.memset(self.one[:], 1.0).then_inc(self.filled, 1)
        pool.wait_ge(self.filled, 1)
        with pool.Fori(0, self.turns // 2) as i:
            for j in range(2):
                pool.wait_ge(self.w_in[j], i * 16 + 16)
                pool.wait_ge(self.used[j], i)
                g.tensor_tensor(self.high[j][:], self.raw[j][:], self.one[:].broadcast_to(self.raw[j].shape), ALU.mult).then_inc(self.rounded, 1)
                pool.wait_ge(self.rounded, i * 2 + j + 1)
                g.tensor_tensor(self.low[j][:], self.raw[j][:], self.high[j][:].bitcast(F32), ALU.subtract).then_inc(self.split[j], 1)

    def tile(self, j, k):
        return self.high[j][:, k * P:(k + 1) * P], self.low[j][:, k * P:(k + 1) * P]


def gemm(nc, name, w, kt, nt, rhs, total, evac, evac_on="scalar", out_dram=None, side_dram=None):
    cs = chunks_of(total)
    nb = len(cs)
    with Stage(nc, name) as s:
        W = Weights(nc, s, w, kt * P, nt)
        ob = [s.sb(f"o{j}", [P, total]) for j in range(2)] if out_dram is not None else None
        xb = [s.sb(f"x{j}", [P, total]) for j in range(2)] if side_dram is not None else None
        ps = [[s.ps(f"p{j}_{c}") for c in range(nb)] for j in range(2)]
        summed, out_taken, stored, x_in = s.sems("summed", 2), s.sems("taken", 2), s.sems("stored", 2), s.sems("x_in", 2)
        with nc.Block() as block:
            @block.sync
            def _(sp):
                W.load(sp)

            @block.gpsimd
            def _(pool):
                W.halve(pool)

            @block.tensor
            def _(pe):
                with pe.Fori(0, nt // 2) as i:
                    for j in range(2):
                        pe.wait_ge(W.split[j], i + 1)
                        pe.wait_ge(out_taken[j], i * nb)
                        for c, (a, m) in enumerate(cs):
                            for k in range(kt):
                                mm = product3(nc, ps[j][c][:, 0:m], W.tile(j, k), rhs(k, a, m), k == 0, k == kt - 1)
                            mm.then_inc(summed[j] if c < nb - 1 else W.used[j], 1)

            def take(eng, ns, i):
                for j in range(2):
                    if ob:
                        eng.wait_ge(stored[j], i * 16)
                    if xb:
                        eng.wait_ge(x_in[j], i * 16 + 16)
                    for c, (a, m) in enumerate(cs):
                        if c < nb - 1:
                            eng.wait_ge(summed[j], i * (nb - 1) + c + 1)
                        else:
                            eng.wait_ge(W.used[j], i + 1)
                        evac(ns, ob[j][:, a:a + m] if ob else None, ps[j][c][:, 0:m], i * 2 + j, a, m,
                             xb[j][:, a:a + m] if xb else None).then_inc(out_taken[j], 1)

            if evac_on == "vector":
                @block.vector
                def _(dve):
                    with dve.Fori(0, nt // 2) as i:
                        take(dve, nc.vector, i)

            @block.scalar
            def _(act):
                if evac_on == "scalar" or ob or xb:
                    with act.Fori(0, nt // 2) as i:
                        if xb:
                            for j in range(2):
                                act.wait_ge(out_taken[j], i * nb)
                                act.dma_start(xb[j][:], side_dram[i * 2 + j]).then_inc(x_in[j], 16)
                        if evac_on == "scalar":
                            take(act, nc.scalar, i)
                        if ob:
                            for j in range(2):
                                act.wait_ge(out_taken[j], i * nb + nb)
                                act.dma_start(out_dram[i * 2 + j], ob[j][:]).then_inc(stored[j], 16)
                if ob:
                    for j in range(2):
                        act.wait_ge(stored[j], nt // 2 * 16)


def gemm_tokens(nc, name, w, groups, width, h, hl, t0, nt, out_dram, beside=None):
    total, half = groups * nt, KD * width // 2
    conv, tiles_ = beside or (None, [])
    turn = {(x + 1) * total // len(tiles_) - 1: n for x, n in enumerate(tiles_)}
    with Stage(nc, name) as s:
        raw = s.sb("raw", [P, KD * width])
        wh = [s.sb(f"h{g}", [P, KD * width], F32R) for g in range(groups)]
        wl = [s.sb(f"l{g}", [P, KD * width], F32R) for g in range(groups)]
        ob = [s.sb(f"o{b}", [P, width]) for b in range(4)]
        ps = [s.ps(f"p{b}") for b in range(4)]
        w_in, summed, taken, stored = s.sems("w_in", 2), s.sem("summed"), s.sem("taken"), s.sems("stored", 4)
        rounded, parted = s.sem("rounded"), s.sem("parted")
        cut = [slice(x * half, (x + 1) * half) for x in range(2)]
        with nc.Block() as block:
            @block.sync
            def _(sp):
                for g in range(groups):
                    for x in range(2):
                        if g:
                            sp.wait_ge(parted, g * 2 + x - 1)
                        sp.dma_start(raw[:, cut[x]], w[g][:, cut[x]]).then_inc(w_in[x], 16)
                for n in tiles_:
                    conv.load(sp, n)

            @block.gpsimd
            def _(pool):
                for g in range(groups):
                    for x in range(2):
                        pool.wait_ge(rounded, g * 2 + x + 1)
                        nc.gpsimd.tensor_tensor(wl[g][:, cut[x]], raw[:, cut[x]], wh[g][:, cut[x]].bitcast(F32), ALU.subtract).then_inc(parted, 1)

            @block.tensor
            def _(pe):
                for n in range(total):
                    g, t = divmod(n, nt)
                    if n >= 4:
                        pe.wait_ge(taken, n - 3)
                    for k in range(KD):
                        if t == 0 and k % (KD // 2) == 0:
                            pe.wait_ge(parted, g * 2 + k // (KD // 2) + 1)
                        part, rows = slice(k * width, (k + 1) * width), slice(t0 + t * P, t0 + (t + 1) * P)
                        mm = product3(nc, ps[n % 4][:, 0:width], (h[:, k, rows], hl[:, k, rows]),
                                      (wh[g][:, part], wl[g][:, part]), k == 0, k == KD - 1)
                    mm.then_inc(summed, 1)

            if conv:
                @block.vector
                def _(dve):
                    if tiles_[0] == 0:
                        conv.zero(dve)
                    for n in tiles_:
                        conv.convolve(dve, n)

            @block.scalar
            def _(act):
                def high(g):
                    for x in range(2):
                        act.wait_ge(w_in[x], g * 16 + 16)
                        nc.scalar.activation(wh[g][:, cut[x]], raw[:, cut[x]], ACT.Copy).then_inc(rounded, 1)

                high(0)
                for n in range(total):
                    g, t = divmod(n, nt)
                    act.wait_ge(summed, n + 1)
                    if n >= 4:
                        act.wait_ge(stored[n % 4], n // 4 * 16)
                    nc.scalar.activation(ob[n % 4][:], ps[n % 4][:, 0:width], ACT.Copy).then_inc(taken, 1)
                    act.wait_ge(taken, n + 1)
                    act.dma_start(out_dram[g][t * P:(t + 1) * P, :], ob[n % 4][:]).then_inc(stored[n % 4], 16)
                    if t == 2 and g + 1 < groups:
                        high(g + 1)
                    if n in turn:
                        conv.gate(act, turn[n])
                for b in range(4):
                    act.wait_ge(stored[b], -(-(total - b) // 4) * 16)


def gemm_small(nc, name, w, kt, nt, rhs, total, evac, evac_on="scalar", out_dram=None, side=None, side_dram=None, unroll=2):
    cs = chunks_of(total)
    nb = len(cs)
    with Stage(nc, name) as s:
        wb = [s.sb(f"w{j}", [P, kt * P]) for j in range(unroll)]
        ob = [s.sb(f"o{j}", [P, total]) for j in range(unroll)] if out_dram is not None else None
        xb = [s.sb(f"x{j}", [P, total]) for j in range(unroll)] if side_dram is not None else None
        ps = [[s.ps(f"p{j}_{c}") for c in range(nb)] for j in range(unroll)]
        w_in, summed, out_taken = s.sems("w_in", unroll), s.sems("summed", unroll), s.sems("taken", unroll)
        stored, x_in = s.sems("stored", unroll), s.sems("x_in", unroll)
        with nc.Block() as block:
            @block.sync
            def _(sp):
                with sp.Fori(0, nt // unroll) as i:
                    for j in range(unroll):
                        sp.wait_ge(summed[j], i * nb)
                        sp.dma_start(wb[j][:], w[i * unroll + j]).then_inc(w_in[j], 16)
                        if xb:
                            sp.wait_ge(out_taken[j], i * nb)
                            sp.dma_start(xb[j][:], side_dram[i * unroll + j]).then_inc(x_in[j], 16)

            @block.tensor
            def _(pe):
                with pe.Fori(0, nt // unroll) as i:
                    for j in range(unroll):
                        pe.wait_ge(w_in[j], i * 16 + 16)
                        pe.wait_ge(out_taken[j], i * nb)
                        for c, (a, m) in enumerate(cs):
                            for k in range(kt):
                                mm = nc.tensor.matmul(ps[j][c][:, 0:m], wb[j][:, k * P:(k + 1) * P], rhs(k, a, m),
                                                      start=(k == 0), stop=(k == kt - 1))
                            mm.then_inc(summed[j], 1)

            def take(eng, ns, i):
                for j in range(unroll):
                    if ob:
                        eng.wait_ge(stored[j], i * 16)
                    if xb:
                        eng.wait_ge(x_in[j], i * 16 + 16)
                    for c, (a, m) in enumerate(cs):
                        eng.wait_ge(summed[j], i * nb + c + 1)
                        evac(ns, ob[j][:, a:a + m] if ob else None, ps[j][c][:, 0:m], i * unroll + j, a, m,
                             xb[j][:, a:a + m] if xb else None).then_inc(out_taken[j], 1)

            if evac_on == "vector":
                @block.vector
                def _(dve):
                    with dve.Fori(0, nt // unroll) as i:
                        take(dve, nc.vector, i)

            @block.scalar
            def _(act):
                if evac_on == "scalar" or ob:
                    with act.Fori(0, nt // unroll) as i:
                        if evac_on == "scalar":
                            take(act, nc.scalar, i)
                        if ob:
                            for j in range(unroll):
                                act.wait_ge(out_taken[j], i * nb + nb)
                                act.dma_start(out_dram[i * unroll + j], ob[j][:]).then_inc(stored[j], 16)
                if ob:
                    for j in range(unroll):
                        act.wait_ge(stored[j], nt // unroll * 16)


def norm_channels(nc, name, src, total, dst, gain, shift, ones, width=D):
    kt = width // P
    cs = chunks_of(total)
    with Stage(nc, name) as s:
        sq = [s.sb(f"sq{j}", [P, BANK]) for j in range(2)]
        rs = s.sb("rs", [P, total])
        ps = [s.ps(f"p{c}") for c in range(len(cs))]
        squared, used, summed = s.sem("squared"), s.sem("used"), s.sem("summed")
        meant, rooted, scaled, own = s.sem("meant"), s.sem("rooted"), s.sem("scaled"), s.sem("own")
        with nc.Block() as block:
            @block.scalar
            def _(act):
                n = 0
                for a, m in cs:
                    for k in range(kt):
                        if n >= 2:
                            act.wait_ge(used, n - 1)
                        nc.scalar.activation(sq[n % 2][:, 0:m], src[:, k, a:a + m], ACT.Square).then_inc(squared, 1)
                        n += 1
                for c, (a, m) in enumerate(cs):
                    act.wait_ge(meant, c + 1)
                    nc.scalar.activation(rs[:, a:a + m], rs[:, a:a + m], ACT.Sqrt).then_inc(rooted, 1)
                for k in range(kt):
                    act.wait_ge(scaled, k + 1)
                    nc.scalar.activation(dst[:, k, 0:total], dst[:, k, 0:total], ACT.Identity,
                                         bias=shift(k) if shift else 0.0, scale=gain(k)).then_inc(own, 1)

            @block.tensor
            def _(pe):
                n = 0
                for c, (a, m) in enumerate(cs):
                    for k in range(kt):
                        pe.wait_ge(squared, n + 1)
                        mm = nc.tensor.matmul(ps[c][:, 0:m], ones[:, 0:P], sq[n % 2][:, 0:m], start=(k == 0), stop=(k == kt - 1))
                        mm.then_inc(used, 1)
                        n += 1

            @block.vector
            def _(dve):
                for c, (a, m) in enumerate(cs):
                    dve.wait_ge(used, kt * (c + 1))
                    nc.vector.tensor_scalar(rs[:, a:a + m], ps[c][:, 0:m], 1.0 / width, EPS, ALU.mult, ALU.add).then_inc(meant, 1)
                for c, (a, m) in enumerate(cs):
                    dve.wait_ge(rooted, c + 1)
                    nc.vector.reciprocal(rs[:, a:a + m], rs[:, a:a + m]).then_inc(summed, 1)
                dve.wait_ge(summed, len(cs))
                for k in range(kt):
                    nc.vector.tensor_tensor(dst[:, k, 0:total], src[:, k, 0:total], rs[:], ALU.mult).then_inc(scaled, 1)


def norm_split(nc, name, src, total, high, rest, gain, shift, ones):
    cs = chunks_of(total)
    with Stage(nc, name) as s:
        sq = [s.sb(f"sq{j}", [P, BANK]) for j in range(2)]
        rs = s.sb("rs", [P, total])
        t, y = [s.sb(f"t{j}", [P, total]) for j in range(2)], [s.sb(f"y{j}", [P, total]) for j in range(2)]
        ps = [s.ps(f"p{c}") for c in range(len(cs))]
        squared, used, inverted = s.sem("squared"), s.sem("used"), s.sem("inverted")
        meant, rooted, scaled, gained, left = s.sem("meant"), s.sem("rooted"), s.sem("scaled"), s.sem("gained"), s.sem("left")
        with nc.Block() as block:
            @block.scalar
            def _(act):
                n = 0
                for a, m in cs:
                    for k in range(KD):
                        if n >= 2:
                            act.wait_ge(used, n - 1)
                        nc.scalar.activation(sq[n % 2][:, 0:m], src[:, k, a:a + m], ACT.Square).then_inc(squared, 1)
                        n += 1
                for c, (a, m) in enumerate(cs):
                    act.wait_ge(meant, c + 1)
                    nc.scalar.activation(rs[:, a:a + m], rs[:, a:a + m], ACT.Sqrt).then_inc(rooted, 1)
                for k in range(KD):
                    act.wait_ge(scaled, k + 1)
                    if k >= 2:
                        act.wait_ge(left, k - 1)
                    for out in (y[k % 2][:], high[:, k, 0:total]):
                        nc.scalar.activation(out, t[k % 2][:], ACT.Identity, bias=shift(k) if shift else 0.0, scale=gain(k)).then_inc(gained, 1)

            @block.tensor
            def _(pe):
                n = 0
                for c, (a, m) in enumerate(cs):
                    for k in range(KD):
                        pe.wait_ge(squared, n + 1)
                        nc.tensor.matmul(ps[c][:, 0:m], ones[:, 0:P], sq[n % 2][:, 0:m], start=(k == 0), stop=(k == KD - 1)).then_inc(used, 1)
                        n += 1

            @block.vector
            def _(dve):
                for c, (a, m) in enumerate(cs):
                    dve.wait_ge(used, KD * (c + 1))
                    nc.vector.tensor_scalar(rs[:, a:a + m], ps[c][:, 0:m], 1.0 / D, EPS, ALU.mult, ALU.add).then_inc(meant, 1)
                for c, (a, m) in enumerate(cs):
                    dve.wait_ge(rooted, c + 1)
                    nc.vector.reciprocal(rs[:, a:a + m], rs[:, a:a + m]).then_inc(inverted, 1)
                dve.wait_ge(inverted, len(cs))
                for k in range(KD + 1):
                    if k < KD:
                        if k >= 2:
                            dve.wait_ge(gained, 2 * (k - 1))
                        nc.vector.tensor_tensor(t[k % 2][:], src[:, k, 0:total], rs[:], ALU.mult).then_inc(scaled, 1)
                    if k:
                        dve.wait_ge(gained, 2 * k)
                        nc.vector.tensor_tensor(rest[:, k - 1, 0:total], y[(k - 1) % 2][:], high[:, k - 1, 0:total].bitcast(F32), ALU.subtract).then_inc(left, 1)
                dve.wait_ge(left, KD)


def modulation(nc, A, C, mod):
    nt = 6 * KD
    slabs_ = nt * P // BANK
    with Stage(nc, "ada") as s:
        c2, cs = s.sb("c2", [P, KD, 2]), s.sb("cs", [P, KD, 2])
        bias, rows = s.sb("bias", [P, nt]), s.sb("rows", [2, nt * P])
        wb = [s.sb(f"w{j}", [P, KD * BANK]) for j in range(3)]
        ps, pt = [s.ps(f"p{j}") for j in range(3)], s.ps("pt")
        c_in, silu, w_in, used, taken = s.sem("c_in"), s.sem("silu"), s.sems("w_in", 3), s.sems("used", 3), s.sems("taken", 3)
        turned, own = s.sem("turned"), s.sem("own")
        with nc.Block() as block:
            @block.sync
            def _(sp):
                sp.dma_start(c2[:], A["c2"]).then_inc(c_in, 16)
                sp.dma_start(bias[:], A["ada_b"]).then_inc(c_in, 16)
                with sp.Fori(0, slabs_ // 3) as i:
                    for j in range(3):
                        sp.wait_ge(used[j], i)
                        sp.dma_start(wb[j][:], A["ada_w"][i * 3 + j]).then_inc(w_in[j], 16)

            @block.scalar
            def _(act):
                act.wait_ge(c_in, 32)
                nc.scalar.activation(cs[:], c2[:], ACT.Silu).then_inc(silu, 1)

            @block.tensor
            def _(pe):
                pe.wait_ge(silu, 1)
                with pe.Fori(0, slabs_ // 3) as i:
                    for j in range(3):
                        pe.wait_ge(w_in[j], i * 16 + 16)
                        pe.wait_ge(taken[j], i)
                        for k in range(KD):
                            mm = nc.tensor.matmul(ps[j][0:2, :], cs[:, k, :], wb[j][:, k * BANK:(k + 1) * BANK], start=(k == 0), stop=(k == KD - 1))
                        mm.then_inc(used[j], 1)
                for j in range(3):
                    pe.wait_ge(taken[j], slabs_ // 3)
                for n in range(nt):
                    mm = nc.tensor.transpose(pt[:, 2 * n:2 * n + 2], rows[:, n * P:(n + 1) * P], C["ident"][0:2, 0:2])
                mm.then_inc(turned, 1)

            @block.vector
            def _(dve):
                with dve.Fori(0, slabs_ // 3) as i:
                    for j in range(3):
                        dve.wait_ge(used[j], i + 1)
                        nc.vector.tensor_copy(rows[:, bass.ds((i * 3 + j) * BANK, BANK)], ps[j][0:2, :]).then_inc(taken[j], 1)
                dve.wait_ge(c_in, 32)
                dve.wait_ge(turned, 1)
                st = Steps(dve, own)
                st.then(nc.vector.tensor_tensor(mod[:], pt[:, 0:2 * nt].rearrange("p (n s) -> p n s", s=2),
                                                bias[:].unsqueeze(2).broadcast_to([P, nt, 2]), ALU.add))


GLA_H, GLA_DK, GLA_DV, LR = 4, 64, 128, 16
ML_H, ML_D = 4, 128
CM1 = 14


def first_projection(nc, A, R, mod, ones):
    with Stage(nc, "zin") as s:
        hh, hl = s.sb("hh", [P, KD, TOT], F32R), s.sb("hl", [P, KD, TOT], F32R)
        with Stage(nc, "znorm") as z:
            h, gain, shift = z.sb("h", [P, KD, TOT]), z.sb("gain", [P, 2, KD]), z.sb("shift", [P, 2, KD])
            own = z.sem("own")
            load(nc, "zld", [(h[:, :, 0:CTX], A["ctxT"]), (h[:, :, CTX:TOT], A["xT"]), (gain[:, 0, :], A["norm1_g"])])
            with nc.Block() as block:
                @block.vector
                def _(dve):
                    st = Steps(dve, own)
                    st.then(nc.vector.tensor_copy(gain[:, 1, :], gain[:, 0, :]))
                    st.then(nc.vector.tensor_scalar(shift[:], mod[:, KD:2 * KD, :].rearrange("p k s -> p s k"), 1.0, None, ALU.add))
                    st.then(nc.vector.tensor_tensor(gain[:], gain[:], shift[:], ALU.mult))
                    st.then(nc.vector.tensor_copy(shift[:], mod[:, 0:KD, :].rearrange("p k s -> p s k")))
            for name, n, at in (("nc", 1, slice(0, CTX)), ("nx", 0, slice(CTX, TOT))):
                norm_split(nc, name, h[:, :, at], at.stop - at.start, hh[:, :, at], hl[:, :, at],
                           lambda k: gain[:, n, k:k + 1], lambda k: shift[:, n, k:k + 1], ones)
        rhs = lambda k, a, m: (hh[:, k, a:a + m], hl[:, k, a:a + m])
        copy = lambda ns, out, ps, n, a, m, side: ns.activation(out, ps, ACT.Copy)
        gemm(nc, "z1", A["w_in_cm"], KD, CM1, rhs, TOT, copy, out_dram=R["z_cm"])
        conv = GridConv(nc, s, A, R)
        half = conv.TILES // 2
        gemm_tokens(nc, "z3", A["w_in_v"], 2, 512, hh, hl, 0, NCH, R["z_v"], beside=(conv, range(0, half)))
        gemm_tokens(nc, "z4", A["w_in_g"], 2, 512, hh, hl, CTX, NCX, R["z_g"], beside=(conv, range(half, 2 * half)))


class GridConv:
    TILES, ROWS = 8, SEQ // GRID_W

    def __init__(self, nc, s, A, R):
        self.nc, self.A, self.R = nc, A, R
        self.w, self.b, self.post = s.sb("w", [P, self.TILES, 9]), s.sb("b", [P, self.TILES]), s.sb("post", [P, self.TILES])
        self.pad = [s.sb(f"pad{j}", [P, self.ROWS + 2, GRID_W + 2]) for j in range(2)]
        self.padc = [s.sb(f"padc{j}", [P, CTX + 2]) for j in range(2)]
        self.raw = [s.sb(f"raw{j}", [P, TOT]) for j in range(2)]
        self.out = [s.sb(f"out{j}", [P, TOT]) for j in range(2)]
        self.consts, self.x_in, self.zeroed, self.taken = s.sem("consts"), s.sems("x_in", 2), s.sem("zeroed"), s.sems("taken", 2)
        self.summed, self.gated, self.done, self.stored, self.own = (
            s.sems("summed", 2), s.sems("gated", 2), s.sems("done", 2), s.sems("stored", 2), s.sem("own"))
        self.steps = 0

    def load(self, sp, n):
        j = n % 2
        if n == 0:
            for dst, src in ((self.w, "conv_w"), (self.b, "conv_b"), (self.post, "conv_post")):
                sp.dma_start(dst[:], self.A[src]).then_inc(self.consts, 16)
        if n >= 2:
            sp.wait_ge(self.taken[j], n // 2)
        sp.dma_start(self.raw[j][:], self.R["z_cm"][n + 4]).then_inc(self.x_in[j], 16)

    def zero(self, dve):
        for t in (*self.pad, *self.padc):
            self.nc.vector.memset(t[:], 0.0).then_inc(self.zeroed, 1)
        dve.wait_ge(self.zeroed, 4)
        dve.wait_ge(self.consts, 48)

    def convolve(self, dve, n):
        V, j, rows = self.nc.vector, n % 2, self.ROWS
        st = Steps(dve, self.own, self.steps)
        pad, padc, raw, out = self.pad[j], self.padc[j], self.raw[j], self.out[j]
        dve.wait_ge(self.x_in[j], n // 2 * 16 + 16)
        if n >= 2:
            dve.wait_ge(self.stored[j], n // 2 * 16)
        st.then(V.tensor_copy(padc[:, 1:CTX + 1], raw[:, 0:CTX]))
        st.then(V.tensor_copy(pad[:, 1:rows + 1, 1:GRID_W + 1], raw[:, CTX:TOT].rearrange("p (r c) -> p r c", c=GRID_W)))
        oc, ox = out[:, 0:CTX], out[:, CTX:TOT].rearrange("p (r c) -> p r c", c=GRID_W)
        tap = lambda q: self.w[:, n, q:q + 1]
        V.tensor_scalar(oc, padc[:, 0:CTX], tap(3), None, ALU.mult).then_inc(self.taken[j], 1)
        dve.wait_ge(self.taken[j], n // 2 + 1)
        st.then(V.tensor_scalar(ox, pad[:, 0:rows, 0:GRID_W], tap(0), None, ALU.mult))
        for q in (1, 2):
            st.then(V.scalar_tensor_tensor(oc, padc[:, q:q + CTX], tap(3 + q), oc, ALU.mult, ALU.add))
        for q in range(1, 8):
            st.then(V.scalar_tensor_tensor(ox, pad[:, q // 3:q // 3 + rows, q % 3:q % 3 + GRID_W], tap(q), ox, ALU.mult, ALU.add))
        V.scalar_tensor_tensor(ox, pad[:, 2:2 + rows, 2:2 + GRID_W], tap(8), ox, ALU.mult, ALU.add).then_inc(self.summed[j], 1)
        dve.wait_ge(self.gated[j], n // 2 + 1)
        V.tensor_scalar(out[:], out[:], self.post[:, n:n + 1], None, ALU.mult).then_inc(self.done[j], 1)
        self.steps = st.n

    def gate(self, act, n):
        j = n % 2
        act.wait_ge(self.summed[j], n // 2 + 1)
        self.nc.scalar.activation(self.out[j][:], self.out[j][:], ACT.Silu, bias=self.b[:, n:n + 1]).then_inc(self.gated[j], 1)
        act.wait_ge(self.done[j], n // 2 + 1)
        act.dma_start(self.R["mqk"][n], self.out[j][:]).then_inc(self.stored[j], 16)
        if n >= self.TILES - 2:
            act.wait_ge(self.stored[j], self.TILES // 2 * 16)


ORDER = [list(range(NCH)), list(range(NCC - 1, -1, -1)) + list(range(NCH - 1, NCC - 1, -1))]


def gla_gates(nc, A, R, qk, fac, room, room2):
    cs = chunks_of(TOT)
    with Stage(nc, "gg") as s:
        lr, up = s.sb("lr", [P, TOT]), s.sb("up", [P, 2, P])
        upb = s.sb("upb", [P, 4])
        room = room.rearrange("p a b -> p (a b)")
        raw = room[:, 0:4 * TOT].rearrange("p (n t) -> p n t", t=TOT)
        mask = room[:, 4 * TOT:6 * TOT].rearrange("p (n t) -> p n t", t=TOT)
        room2 = room2.rearrange("p a b -> p (a b)")
        g, u, t, e = (room2[:, n * TOT:(n + 1) * TOT] for n in range(4))
        f = s.sb("f", [P, 3, NCH])
        ps = [s.ps(f"p{c}") for c in range(len(cs))]
        got, summed, exped, own, zeroed = s.sem("got"), s.sem("summed"), s.sem("exped"), s.sem("own"), s.sem("zeroed")
        per = len(cs) + 13
        with nc.Block() as block:
            @block.sync
            def _(sp):
                for dst, src in ((lr[:], R["z_cm"][12]), (up[:], A["gla_up_w"]), (upb[:], A["gla_up_b"]),
                                 (raw, R["z_cm"][0:4].rearrange("n p t -> p n t")),
                                 (mask[:, 0, :], A["scan_mask"][0:1, :].broadcast_to([P, TOT])),
                                 (mask[:, 1, :], A["scan_mask"][1:2, :].broadcast_to([P, TOT]))):
                    sp.dma_start(dst, src).then_inc(got, 16)

            @block.tensor
            def _(pe):
                pe.wait_ge(got, 96)
                for n in range(4):
                    d, ti = n // 2, n % 2
                    if n:
                        pe.wait_ge(own, per * (n - 1) + len(cs))
                    for c, (a, m) in enumerate(cs):
                        nc.tensor.matmul(ps[c][:, 0:m], up[32 * d:32 * d + LR, ti, :], lr[32 * d:32 * d + LR, a:a + m],
                                         start=True, stop=True).then_inc(summed, 1)

            @block.gpsimd
            def _(pool):
                for x in range(2):
                    for d in range(2):
                        nc.gpsimd.memset(qk[64 - 64 * x:128 - 64 * x, d, :, :, x, :], 0.0).then_inc(zeroed, 1)
                pool.wait_ge(zeroed, 4)

            @block.vector
            def _(dve):
                dve.wait_ge(got, 96)
                st = Steps(dve, own)
                for n in range(4):
                    d, ti = n // 2, n % 2
                    dve.wait_ge(summed, len(cs) * (n + 1))
                    for c, (a, m) in enumerate(cs):
                        st.then(nc.vector.tensor_scalar(g[:, a:a + m], ps[c][:, 0:m], upb[:, n:n + 1], None, ALU.add))
                    st.then(nc.vector.scalar_tensor_tensor(u[:], g[:], -1.0, g[:], ALU.mult, ALU.min))
                    dve.wait_ge(exped, 5 * n + 2)
                    st.then(nc.vector.scalar_tensor_tensor(g[:], g[:], 0.0, u[:], ALU.min, ALU.subtract))
                    st.then(nc.vector.tensor_scalar(g[:], g[:], 1.0 / 16.0, None, ALU.mult))
                    r = slice(None) if d == 0 else slice(None, None, -1)
                    st.then(nc.vector.tensor_tensor_scan(out=t[:, r], data0=mask[:, d, r], data1=g[:, r], initial=0.0,
                                                         op0=ALU.mult, op1=ALU.add))
                    tc = t[:].rearrange("p (c t) -> p c t", t=CH)
                    mid = tc[:, :, CH // 2 - 1 if d == 0 else CH // 2]
                    end = tc[:, :, CH - 1 if d == 0 else 0]
                    st.then(nc.vector.tensor_copy(f[:, 0, :], mid))
                    st.then(nc.vector.tensor_copy(f[:, 1, :], end))
                    st.then(nc.vector.tensor_tensor(f[:, 2, :], f[:, 1, :], f[:, 0, :], ALU.subtract))
                    st.then(nc.vector.tensor_tensor(u[:].rearrange("p (c t) -> p c t", t=CH), tc,
                                                    f[:, 0, :].unsqueeze(2).broadcast_to([P, NCH, CH]), ALU.subtract))
                    dve.wait_ge(exped, 5 * n + 5)
                    first, rest = (slice(0, NCC), slice(NCC, NCH)) if d == 0 else (slice(NCC - 1, None, -1), slice(NCH - 1, NCC - 1, -1))
                    st.then(nc.vector.tensor_copy(fac[:, 0:NCC, d, ti, :].rearrange("p n f -> p f n"), f[:, :, first]))
                    st.then(nc.vector.tensor_copy(fac[:, NCC:NCH, d, ti, :].rearrange("p n f -> p f n"), f[:, :, rest]))
                    ch = lambda x: x.rearrange("p (c t) -> p c t", t=CH)
                    for x in range(2):
                        rows = slice(64 * x, 64 * x + 64)
                        st.then(nc.vector.scalar_tensor_tensor(qk[rows, d, :, ti, x, :], ch(e[:])[rows], GLA_DK ** -0.5,
                                                               ch(raw[:, ti, :])[rows], ALU.mult, ALU.mult))
                    st.then(nc.vector.tensor_tensor(qk[:, d, :, ti, 2, :], ch(u[:]), ch(raw[:, 2 + ti, :]), ALU.mult))

            @block.scalar
            def _(act):
                for n in range(4):
                    start = per * n
                    act.wait_ge(own, start + len(cs) + 1)
                    nc.scalar.activation(u[:], u[:], ACT.Exp).then_inc(exped, 1)
                    act.wait_ge(exped, 5 * n + 1)
                    nc.scalar.activation(u[:], u[:], ACT.Ln, bias=1.0).then_inc(exped, 1)
                    act.wait_ge(own, start + len(cs) + 8)
                    nc.scalar.activation(e[:], u[:], ACT.Exp).then_inc(exped, 1)
                    act.wait_ge(exped, 5 * n + 3)
                    nc.scalar.activation(u[:], u[:], ACT.Exp, scale=-1.0).then_inc(exped, 1)
                    nc.scalar.activation(f[:], f[:], ACT.Exp).then_inc(exped, 1)


def gla_scan(nc, A, R, qk, fac, v, out, C):
    with Stage(nc, "gs") as s:
        cur = s.sb("cur", [P, 2, 2, 3, CH])
        att, kt = s.sb("att", [P, 2, GLA_H, CH]), s.sb("kt", [P, 4, CH])
        seen = s.sb("seen", [P, 1])
        state, mid, add = s.sb("state", [P, 4, GLA_DV]), s.sb("mid", [P, 4, GLA_DV]), s.sb("add", [P, 4, GLA_DV])
        pa = s.ps("pa", [P, 2, BANK])
        pk, po = s.ps("pk"), [s.ps(f"po{d}") for d in range(2)]
        pst = s.ps("pst", [P, 4, 2 * GLA_DV])
        cut, att_done, kt_done, masked, kt_taken, mid_done, o_done, stepped, o_taken, own = (
            s.sem(x) for x in ("cut", "att_done", "kt_done", "masked", "kt_taken", "mid_done", "o_done", "stepped", "o_taken", "own"))
        factor = lambda n, f, rows=slice(0, P): fac[rows, bass.ds(n, 1), :, :, f].rearrange("p n d t -> p (n d t)").unsqueeze(2)

        def steps(emit, eng):
            for n in range(NCC):
                emit(n, [ORDER[0][n], ORDER[1][n]], None)
            with eng.Fori(0, NCX) as i:
                emit(i + NCC, [i + NCC, i * -1 + NCH - 1], i)

        with nc.Block() as block:
            @block.vector
            def _(dve):
                st = Steps(dve, own)
                st.then(nc.vector.memset(att[:], 0.0))
                st.then(nc.vector.memset(state[:], 0.0))
                n_own = 4

                def emit(n, c, i):
                    st = Steps(dve, own, n * n_own + 2)
                    dve.wait_ge(stepped, n)
                    for d in range(2):
                        ins = nc.vector.tensor_copy(cur[:, d], qk[:, d, bass.ds(c[d], 1)].rearrange("p a t q c -> p (a t) q c"))
                        ins.then_inc(cut, 1)
                    if i is not None:
                        nc.vector.tensor_tensor(mid[:], state[:], factor(n, 0).broadcast_to([P, 4, GLA_DV]), ALU.mult).then_inc(mid_done, 1)
                        dve.wait_ge(att_done, i + 1)
                        nc.vector.memset(seen[:], 0.0)
                        for d in range(2):
                            nc.vector.copy_predicated(att[:, d], C["keep"][:, d].unsqueeze(1).broadcast_to([P, GLA_H, CH]),
                                                      pa[:, d].rearrange("p (h t) -> p h t", t=CH)).then_inc(masked, 1)
                    dve.wait_ge(stepped, n + 1)
                    for half in range(2):
                        rows = slice(64 * half, 64 * half + 64)
                        st.then(nc.vector.tensor_tensor(add[rows], pst[rows, :, half * GLA_DV:(half + 1) * GLA_DV],
                                                        factor(n, 2, rows).broadcast_to([64, 4, GLA_DV]), ALU.mult))
                    if i is not None:
                        dve.wait_ge(mid_done, i + 1)
                    st.then(nc.vector.tensor_tensor(state[:], state[:], factor(n, 1).broadcast_to([P, 4, GLA_DV]), ALU.mult))
                    st.then(nc.vector.tensor_tensor(state[:], state[:], add[:], ALU.add))

                steps(emit, dve)

            @block.tensor
            def _(pe):
                def emit(n, c, i):
                    pe.wait_ge(cut, n * 2 + 2)
                    if i is not None:
                        for d in range(2):
                            for h in range(GLA_H):
                                mm = nc.tensor.matmul(pa[:, d, h * CH:(h + 1) * CH], cur[:, d, h // 2, 2, :], cur[:, d, h // 2, h % 2, :],
                                                      start=True, stop=True)
                        mm.then_inc(att_done, 1)
                    for q in range(4):
                        mm = nc.tensor.transpose(pk[:, q * CH:(q + 1) * CH], cur[:, q // 2, q % 2, 2, :], C["ident"][:])
                    mm.then_inc(kt_done, 1)
                    if i is not None:
                        pe.wait_ge(masked, i * 2 + 2)
                        pe.wait_ge(mid_done, i + 1)
                        pe.wait_ge(o_taken, i * 2)
                        for d in range(2):
                            for h in range(GLA_H):
                                o = po[d][:, h * GLA_DV:(h + 1) * GLA_DV]
                                nc.tensor.matmul(o, att[:, d, h, :], v[:, bass.ds(c[d], 1), h * GLA_DV:(h + 1) * GLA_DV], start=True, stop=False)
                                mm = nc.tensor.matmul(o, cur[:, d, h // 2, h % 2, :], mid[:, 2 * d + h // 2, :], start=False, stop=True)
                        mm.then_inc(o_done, 1)
                    pe.wait_ge(kt_taken, n + 1)
                    for q in range(4):
                        t = q % 2
                        mm = nc.tensor.matmul(pst[:, q, :], kt[:, q, :], v[:, bass.ds(c[q // 2], 1), t * 256:t * 256 + 256], start=True, stop=True)
                    mm.then_inc(stepped, 1)

                steps(emit, pe)

            @block.scalar
            def _(act):
                def emit(n, c, i):
                    act.wait_ge(kt_done, n + 1)
                    act.wait_ge(stepped, n)
                    nc.scalar.activation(kt[:], pk[:], ACT.Copy).then_inc(kt_taken, 1)
                    if i is not None:
                        act.wait_ge(o_done, i + 1)
                        for d in range(2):
                            nc.scalar.activation(out[:, d, bass.ds(c[d] - NCC, 1), :], po[d][:], ACT.Copy).then_inc(o_taken, 1)

                steps(emit, act)


def mlstm_gates(nc, A, R, negm, cols, C):
    R64 = 64
    with Stage(nc, "mg") as s:
        ig, fg, t, zero = s.sb("ig", [R64, TOT]), s.sb("fg", [R64, TOT]), s.sb("t", [R64, TOT]), s.sb("zero", [R64, TOT])
        ib, fb = s.sb("ib", [R64, 1]), s.sb("fb", [R64, 1])
        ps = [s.ps(f"p{b}") for b in range(3)]
        zeroed, got, exped, rows, turned, own = (s.sem(x) for x in ("zeroed", "got", "exped", "rows", "turned", "own"))
        with nc.Block() as block:
            @block.sync
            def _(sp):
                sp.wait_ge(zeroed, 2)
                for d in range(2):
                    r = slice(32 * d, 32 * d + 4)
                    sp.dma_start(ig[r, :], R["z_cm"][12, 64 + 4 * d:68 + 4 * d, :]).then_inc(got, 16)
                    sp.dma_start(fg[r, :], R["z_cm"][12, 96 + 4 * d:100 + 4 * d, :]).then_inc(got, 16)
                sp.dma_start(ib[:], A["ml_i_b"]).then_inc(got, 16)
                sp.dma_start(fb[:], A["ml_f_b"]).then_inc(got, 16)

            @block.vector
            def _(dve):
                nc.vector.memset(ig[:], 0.0).then_inc(zeroed, 1)
                nc.vector.memset(fg[:], 0.0).then_inc(zeroed, 1)
                st = Steps(dve, own)
                V = nc.vector
                st.then(V.memset(zero[:], 1.0))
                dve.wait_ge(got, 96)
                st.then(V.tensor_scalar(fg[:], fg[:], fb[:], None, ALU.add))
                st.then(V.scalar_tensor_tensor(t[:], fg[:], -1.0, fg[:], ALU.mult, ALU.min))
                dve.wait_ge(exped, 2)
                st.then(V.scalar_tensor_tensor(fg[:], fg[:], 0.0, t[:], ALU.min, ALU.subtract))
                seg = [[(slice(0, 4), slice(0, TOT), None)],
                       [(slice(32, 36), slice(CTX - 1, None, -1), None), (slice(32, 36), slice(TOT - 1, CTX - 1, -1), 0)]]
                st.then(V.memset(t[:], 0.0))
                for d in range(2):
                    for r, c, first in seg[d]:
                        st.then(V.tensor_tensor_scan(out=t[r, c], data0=zero[r, c], data1=fg[r, c],
                                                     initial=0.0 if first is None else t[r, 0:1], op0=ALU.mult, op1=ALU.add))
                st.then(V.tensor_scalar(ig[:], ig[:], ib[:], None, ALU.add))
                st.then(V.tensor_tensor(ig[:], ig[:], t[:], ALU.subtract))
                st.then(V.memset(fg[:], 0.0))
                for d in range(2):
                    for r, c, first in seg[d]:
                        st.then(V.tensor_tensor_scan(out=fg[r, c], data0=ig[r, c], data1=ig[r, c],
                                                     initial=0.0 if first is None else fg[r, 0:1], op0=ALU.max, op1=ALU.max))
                st.then(V.tensor_scalar(negm[:], fg[:], -1.0, None, ALU.mult))
                V.tensor_tensor(t[:], negm[:], t[:], ALU.subtract).then_inc(rows, 1)
                for b in range(3):
                    dve.wait_ge(turned, b + 1)
                    n = min(8, 2 * NCH - 8 * b)
                    st.then(V.tensor_copy(cols[:].rearrange("p a c r -> p (a c) r")[:, 8 * b:8 * b + n, :],
                                          ps[b][:, 0:n * R64].rearrange("p (c r) -> p c r", r=R64)))

            @block.scalar
            def _(act):
                act.wait_ge(own, 3)
                nc.scalar.activation(t[:], t[:], ACT.Exp).then_inc(exped, 1)
                act.wait_ge(exped, 1)
                nc.scalar.activation(t[:], t[:], ACT.Ln, bias=1.0).then_inc(exped, 1)
                act.wait_ge(own, 18)
                nc.scalar.activation(cols[:, 1], cols[:, 1], ACT.Exp).then_inc(exped, 1)

            @block.tensor
            def _(pe):
                pe.wait_ge(rows, 1)
                for b in range(3):
                    n = min(8, 2 * NCH - 8 * b)
                    for j in range(n):
                        a, c = (8 * b + j) // NCH, (8 * b + j) % NCH
                        mm = nc.tensor.transpose(ps[b][:, j * R64:(j + 1) * R64], (ig, t)[a][:, c * CH:(c + 1) * CH], C["ident"][0:R64, 0:R64])
                    mm.then_inc(turned, 1)


MS_CTX, MS_LAT = 6, 13


def mlstm_scan(nc, A, R, negm, cols, v, out, C):
    H = ML_H
    heads = lambda x: x.rearrange("p (h t) -> p h t", h=H)
    wide = lambda x: x.unsqueeze(2).broadcast_to([P, H, CH])

    def steps(eng, phases):
        for n in range(NCC):
            for phase in phases:
                for w in both:
                    phase(w, n, ORDER[w.d][n], None)
        with eng.Fori(0, NCX) as i:
            for phase in phases:
                for w in both:
                    phase(w, i + NCC, (i + NCC) if w.d == 0 else (i * -1 + NCH - 1), i)

    class Way:

        def __init__(self, s, d):
            self.d = d
            self.kcur, self.arg, self.inter, self.qw, self.pt, self.kw = (
                s.sb(f"{x}{d}", [P, H, CH]) for x in ("kcur", "arg", "inter", "qw", "pt", "kw"))
            self.state, self.norm, self.mbefore = s.sb(f"state{d}", [P, H, ML_D]), s.sb(f"norm{d}", [P, H]), s.sb(f"mbefore{d}", [P, H])
            self.kd, self.den = s.sb(f"kd{d}", [P, 2, H]), s.sb(f"den{d}", [P, H])
            self.pm, self.pk, self.pq, self.pd = (s.ps(f"{x}{d}") for x in ("pm", "pk", "pq", "pd"))
            (self.k_cut, self.rows_up, self.args, self.exps, self.qk_done, self.kt_done, self.q_in, self.weighed, self.kw_done,
             self.o_done, self.den_read, self.stepped, self.own) = (s.sem(f"{x}{d}") for x in (
                 "k_cut", "rows_up", "args", "exps", "qk_done", "kt_done", "q_in", "weighed", "kw_done", "o_done", "den_read", "stepped", "own"))

    with Stage(nc, "ms") as s:
        q, k = s.sb("q", [P, H, TOT]), s.sb("k", [P, H, TOT])
        ones1, pick = s.sb("ones1", [P, 1]), s.sb("pick", [64, 2 * ML_H, P])
        both = [Way(s, d) for d in range(2)]
        got, start = s.sem("got"), s.sem("start")
        with nc.Block() as block:
            @block.sync
            def _(sp):
                sp.dma_start(q[:], R["mqk"][0:4].rearrange("n p t -> p n t")).then_inc(got, 16)
                sp.dma_start(k[:], R["mqk"][4:8].rearrange("n p t -> p n t")).then_inc(got, 16)
                sp.dma_start(pick[:], A["pick"]).then_inc(got, 16)

            @block.scalar
            def _(act):
                act.wait_ge(got, 48)

                def cut(w, n, c, i):
                    act.wait_ge(w.stepped, n)
                    nc.scalar.activation(w.kcur[:], k[:, :, bass.ds(c * CH, CH)], ACT.Copy).then_inc(w.k_cut, 1)

                def exps(w, n, c, i):
                    act.wait_ge(w.args, n + 1)
                    if i is not None:
                        nc.scalar.activation(w.inter[:], w.inter[:], ACT.Exp).then_inc(w.exps, 1)
                        nc.scalar.activation(w.arg[:], w.arg[:], ACT.Exp).then_inc(w.exps, 1)
                    nc.scalar.activation(w.kd[:], w.kd[:], ACT.Exp).then_inc(w.exps, 1)

                steps(act, [cut, exps])

            @block.vector
            def _(dve):
                V = nc.vector
                st = Steps(dve, start)
                for w in both:
                    for x in (w.state, w.norm, w.mbefore):
                        st.then(V.memset(x[:], 0.0))
                st.then(V.memset(ones1[:], 1.0))
                dve.wait_ge(got, 48)

                def own(w, n, i, done):
                    return Steps(dve, w.own, (n * MS_CTX if i is None else i * MS_LAT + NCC * MS_CTX) + done)

                def args(w, n, c, i):
                    st = own(w, n, i, 0)
                    last = CH - 1 if w.d == 0 else 0
                    bcol = cols[:, 0, bass.ds(c, 1), 32 * w.d:32 * w.d + H].rearrange("p a h -> p (a h)")
                    dve.wait_ge(w.rows_up, n + 1)
                    mend = heads(w.pm[:])[:, :, last]
                    st.then(V.tensor_tensor(w.kd[:, 0], bcol, mend, ALU.add))
                    st.then(V.tensor_tensor(w.kd[:, 1], w.mbefore[:], mend, ALU.add))
                    if i is not None:
                        st.then(V.tensor_tensor(w.inter[:], heads(w.pm[:]), wide(w.mbefore[:]), ALU.add))
                        st.then(V.tensor_tensor(w.arg[:], heads(w.pm[:]), wide(bcol), ALU.add))
                        st.then(V.tensor_tensor(w.arg[:], w.arg[:], C["cut"][:, w.d].unsqueeze(1).broadcast_to([P, H, CH]), ALU.min))
                    V.tensor_scalar(w.mbefore[:], mend, -1.0, None, ALU.mult).then_inc(w.args, 1)

                def weigh(w, n, c, i):
                    e = n if i is None else i * 3 + NCC
                    if i is not None:
                        dve.wait_ge(w.exps, e + 1)
                        V.tensor_tensor(w.qw[:], w.inter[:], q[:, :, bass.ds(c * CH, CH)], ALU.mult).then_inc(w.q_in, 1)
                        dve.wait_ge(w.exps, e + 2)
                        dve.wait_ge(w.qk_done, i + 1)
                        V.tensor_tensor(w.pt[:], w.arg[:], heads(w.pq[:]), ALU.mult).then_inc(w.weighed, 1)
                    dve.wait_ge(w.exps, e + (1 if i is None else 3))
                    dve.wait_ge(w.kt_done, n + 1)
                    V.tensor_tensor(w.kw[:], heads(w.pk[:]), wide(w.kd[:, 0]), ALU.mult).then_inc(w.kw_done, 1)

                def give(w, n, c, i):
                    if i is None:
                        return
                    st = own(w, n, i, 5)
                    dve.wait_ge(w.o_done, i + 1)
                    V.tensor_copy(w.den[:], w.pd[:, 0:H]).then_inc(w.den_read, 1)
                    dve.wait_ge(w.den_read, i + 1)
                    st.then(V.scalar_tensor_tensor(w.den[:], w.den[:], -1.0, w.den[:], ALU.mult, ALU.max))
                    st.then(V.tensor_tensor(w.den[:], w.den[:], cols[:, 1, bass.ds(c, 1), 32 * w.d:32 * w.d + H].rearrange("p a h -> p (a h)"), ALU.max))
                    st.then(V.reciprocal(w.den[:], w.den[:]))
                    st.then(V.tensor_tensor(out[:, w.d, bass.ds(c - NCC, 1), :].rearrange("p a (h e) -> p (a h) e", h=H),
                                            heads(w.pq[:]), wide(w.den[:]), ALU.mult))

                def step(w, n, c, i):
                    st = own(w, n, i, 2 if i is None else 9)
                    dve.wait_ge(w.stepped, n + 1)
                    st.then(V.tensor_tensor(w.state[:], w.state[:], wide(w.kd[:, 1]), ALU.mult))
                    st.then(V.tensor_tensor(w.state[:], w.state[:], heads(w.pk[:]), ALU.add))
                    st.then(V.tensor_tensor(w.norm[:], w.norm[:], w.kd[:, 1], ALU.mult))
                    st.then(V.tensor_tensor(w.norm[:], w.norm[:], w.pd[:, H:2 * H], ALU.add))

                steps(dve, [args, weigh, give, step])

            @block.tensor
            def _(pe):
                pe.wait_ge(got, 48)
                pe.wait_ge(start, 7)

                def own_before(n, i):
                    return n * MS_CTX if i is None else i * MS_LAT + NCC * MS_CTX

                def first(w, n, c, i):
                    pe.wait_ge(w.own, own_before(n, i))
                    for h in range(H):
                        mm = nc.tensor.matmul(w.pm[:, h * CH:(h + 1) * CH], pick[:, w.d * H + h, :], negm[:, bass.ds(c * CH, CH)], start=True, stop=True)
                    mm.then_inc(w.rows_up, 1)
                    pe.wait_ge(w.k_cut, n + 1)
                    for h in range(H):
                        mm = nc.tensor.transpose(w.pk[:, h * CH:(h + 1) * CH], w.kcur[:, h, :], C["ident"][:])
                    mm.then_inc(w.kt_done, 1)
                    if i is not None:
                        for h in range(H):
                            mm = nc.tensor.matmul(w.pq[:, h * CH:(h + 1) * CH], w.kcur[:, h, :], q[:, h, bass.ds(c * CH, CH)], start=True, stop=True)
                        mm.then_inc(w.qk_done, 1)

                def second(w, n, c, i):
                    if i is None:
                        return
                    pe.wait_ge(w.q_in, i + 1)
                    pe.wait_ge(w.weighed, i + 1)
                    for h in range(H):
                        nc.tensor.matmul(w.pq[:, h * CH:(h + 1) * CH], w.pt[:, h, :], v[:, bass.ds(c, 1), h * ML_D:(h + 1) * ML_D], start=True, stop=False)
                        nc.tensor.matmul(w.pq[:, h * CH:(h + 1) * CH], w.qw[:, h, :], w.state[:, h, :], start=False, stop=True)
                        nc.tensor.matmul(w.pd[:, h:h + 1], w.pt[:, h, :], ones1[:], start=True, stop=False)
                        mm = nc.tensor.matmul(w.pd[:, h:h + 1], w.qw[:, h, :], w.norm[:, h:h + 1], start=False, stop=True)
                    mm.then_inc(w.o_done, 1)

                def third(w, n, c, i):
                    pe.wait_ge(w.kw_done, n + 1)
                    if i is not None:
                        pe.wait_ge(w.den_read, i + 1)
                    for h in range(H):
                        nc.tensor.matmul(w.pk[:, h * CH:(h + 1) * CH], w.kw[:, h, :], v[:, bass.ds(c, 1), h * ML_D:(h + 1) * ML_D], start=True, stop=True)
                        mm = nc.tensor.matmul(w.pd[:, H + h:H + h + 1], w.kw[:, h, :], ones1[:], start=True, stop=True)
                    mm.then_inc(w.stepped, 1)

                steps(pe, [first, second, third])


def mixer_norm(nc, A, R, out, mixT, C):
    H = 8
    with Stage(nc, "mn") as s:
        gate = s.sb("gate", [P, NCX, 2 * 512])
        sq, y = [s.sb(f"sq{j}", [P, D]) for j in range(4)], [s.sb(f"y{j}", [P, D]) for j in range(2)]
        ss, gn = s.sb("ss", [P, NCX, H]), s.sb("gn", [P, KD])
        pt = [[s.ps(f"pt{j}{x}") for x in range(2)] for j in range(2)]
        got, added, squared, reduced, meant, rooted, inverted, gated = (
            s.sem(x) for x in ("got", "added", "squared", "reduced", "meant", "rooted", "inverted", "gated"))
        normed, y_done, turned, moved = s.sems("normed", 2), s.sems("y_done", 2), s.sems("turned", 2), s.sems("moved", 2)
        flat = lambda x: x.rearrange("p a n -> p (a n)")
        heads = lambda x: x.rearrange("p (h e) -> p h e", h=H)
        with nc.Block() as block:
            @block.sync
            def _(sp):
                for x in range(2):
                    sp.dma_start(gate[:, :, x * 512:(x + 1) * 512], R["z_g"][x].rearrange("(c p) n -> p c n", p=P)).then_inc(got, 16)
                sp.dma_start(gn[:], A["mix_g"]).then_inc(got, 16)

            @block.vector
            def _(dve):
                V = nc.vector
                with dve.Fori(0, NCX) as c:
                    h = flat(out[:, 0, bass.ds(c, 1), :])
                    V.tensor_tensor(h, h, flat(out[:, 1, bass.ds(c, 1), :]), ALU.add).then_inc(added, 1)
                with dve.Fori(0, NCX // 4) as i:
                    for j in range(4):
                        c = i * 4 + j
                        dve.wait_ge(squared, c + 1)
                        V.tensor_reduce(flat(ss[:, bass.ds(c, 1), :]), heads(sq[j][:]), AX.X, ALU.add).then_inc(reduced, 1)
                dve.wait_ge(reduced, NCX)
                V.tensor_scalar(ss[:], ss[:], 1.0 / CH, EPS, ALU.mult, ALU.add).then_inc(meant, 1)
                dve.wait_ge(rooted, 1)
                V.reciprocal(ss[:], ss[:]).then_inc(inverted, 1)
                dve.wait_ge(inverted, 1)
                dve.wait_ge(gated, 2)
                with dve.Fori(0, NCX // 2) as i:
                    for j in range(2):
                        c = i * 2 + j
                        rs = flat(ss[:, bass.ds(c, 1), :]).unsqueeze(2).broadcast_to([P, H, CH])
                        dve.wait_ge(y_done[j], i)
                        V.tensor_tensor(heads(sq[j][:]), heads(flat(out[:, 0, bass.ds(c, 1), :])), rs, ALU.mult).then_inc(normed[j], 1)
                        dve.wait_ge(normed[j], i + 1)
                        dve.wait_ge(turned[j], i)
                        V.tensor_tensor(y[j][:], sq[j][:], flat(gate[:, bass.ds(c, 1), :]), ALU.mult).then_inc(y_done[j], 1)

            @block.scalar
            def _(act):
                S = nc.scalar
                with act.Fori(0, NCX // 4) as i:
                    for j in range(4):
                        c = i * 4 + j
                        act.wait_ge(added, c + 1)
                        act.wait_ge(reduced, i * 4)
                        S.activation(sq[j][:], flat(out[:, 0, bass.ds(c, 1), :]), ACT.Square).then_inc(squared, 1)
                act.wait_ge(meant, 1)
                S.activation(ss[:], ss[:], ACT.Sqrt).then_inc(rooted, 1)
                act.wait_ge(got, 48)
                S.activation(gate[:, :, 0:512], gate[:, :, 0:512], ACT.Silu).then_inc(gated, 1)
                S.activation(gate[:, :, 512:1024], gate[:, :, 512:1024], ACT.Sigmoid).then_inc(gated, 1)
                with act.Fori(0, NCX // 2) as i:
                    for j in range(2):
                        act.wait_ge(turned[j], i + 1)
                        for n in range(KD):
                            S.activation(mixT[:, n, bass.ds((i * 2 + j) * CH, CH)], pt[j][n // 4][:, n % 4 * CH:(n % 4 + 1) * CH], ACT.Copy,
                                         scale=gn[:, n:n + 1]).then_inc(moved[j], 1)

            @block.tensor
            def _(pe):
                with pe.Fori(0, NCX // 2) as i:
                    for j in range(2):
                        pe.wait_ge(y_done[j], i + 1)
                        pe.wait_ge(moved[j], i * KD)
                        for n in range(KD):
                            mm = nc.tensor.transpose(pt[j][n // 4][:, n % 4 * CH:(n % 4 + 1) * CH], y[j][:, n * CH:(n + 1) * CH], C["ident"][:])
                        mm.then_inc(turned[j], 1)


def add_scaled(nc, gain):
    return lambda ns, out, ps, n, a, m, side: nc.vector.scalar_tensor_tensor(out, ps, gain(n), side, ALU.mult, ALU.add)


def router_logits(nc, A, R, h, L, C):
    with Stage(nc, "rl") as s:
        w, b = s.sb("w", [P, KD, NG + NE]), s.sb("b", [P, NG + NE])
        row = [s.sb(f"row{j}", [P, D]) for j in range(2)]
        pl, pt = [s.ps(f"pl{j}") for j in range(2)], [[s.ps(f"pt{j}{x}") for x in range(2)] for j in range(2)]
        got, logits, biased, turned, moved, stored = s.sem("got"), s.sem("logits"), s.sem("biased"), s.sem("turned"), s.sem("moved"), s.sems("stored", 2)
        with nc.Block() as block:
            @block.sync
            def _(sp):
                sp.dma_start(w[:], A["router_w"]).then_inc(got, 16)
                sp.dma_start(b[:], A["router_b"].broadcast_to([P, NG + NE])).then_inc(got, 16)
                for c in range(NCX):
                    sp.wait_ge(moved, 2 * c + 2)
                    sp.dma_start(R["h2rows"][c * P:(c + 1) * P, :], row[c % 2][:]).then_inc(stored[c % 2], 16)
                for j in range(2):
                    sp.wait_ge(stored[j], 16 * NCX // 2)

            @block.tensor
            def _(pe):
                pe.wait_ge(got, 32)
                for c in range(NCX):
                    if c >= 2:
                        pe.wait_ge(biased, c - 1)
                    for k in range(KD):
                        mm = nc.tensor.matmul(pl[c % 2][:, 0:NG + NE], h[:, k, c * P:(c + 1) * P], w[:, k, :], start=(k == 0), stop=(k == KD - 1))
                    mm.then_inc(logits, 1)
                    if c >= 2:
                        pe.wait_ge(moved, 2 * (c - 1))
                    for k in range(KD):
                        mm = nc.tensor.transpose(pt[c % 2][k // 4][:, k % 4 * P:(k % 4 + 1) * P], h[:, k, c * P:(c + 1) * P], C["ident"][:])
                    mm.then_inc(turned, 1)

            @block.vector
            def _(dve):
                dve.wait_ge(got, 32)
                for c in range(NCX):
                    dve.wait_ge(logits, c + 1)
                    nc.vector.tensor_tensor(L[:, c, :], pl[c % 2][:, 0:NG + NE], b[:], ALU.add).then_inc(biased, 1)

            @block.scalar
            def _(act):
                for c in range(NCX):
                    act.wait_ge(turned, c + 1)
                    if c >= 2:
                        act.wait_ge(stored[c % 2], 16 * (c // 2))
                    for x in range(2):
                        nc.scalar.activation(row[c % 2][:, x * BANK:(x + 1) * BANK], pt[c % 2][x][:], ACT.Copy).then_inc(moved, 1)


def route(nc, A, R, L, dest, wt, owner, pairs, C):
    with Stage(nc, "rt") as s:
        oh, ohn = s.sb("oh", [P, NCX, NG]), s.sb("ohn", [P, NCX, NG])
        t8, gm, gs = s.sb("t8", [P, NCX]), s.sb("gm", [P, NCX]), s.sb("gs", [P, NCX])
        em, top, topi, topf = s.sb("em", [P, NCX, NE]), s.sb("top", [P, NCX, 8]), s.sb("topi", [P, NCX, 8], U32), s.sb("topf", [P, NCX, 2])
        hot, both, base = s.sb("hot", [P, NCX, 2, NE]), s.sb("both", [P, NCX, NE]), s.sb("base", [P, NCX, NE])
        cnt, nb, cum, one = s.sb("cnt", [P, NE]), s.sb("nb", [P, NE]), s.sb("cum", [P, NE]), s.sb("one", [P, NE])
        before = s.sb("before", [P, NE])
        destf, ids = s.sb("destf", [P, NCX, 2]), s.sb("ids", [P, NE])
        tok, zero = s.sb("tok", [P, NCX, 16], I32), s.sb("zero", [P, (NBLK + 1) * 16], I32)
        bids, evens, le = s.sb("bids", [P, NBLK + 2]), s.sb("evens", [P, NBLK + 2]), s.sb("le", [P, NBLK + 2, NE])
        pos, pc = s.ps("pos"), s.ps("pc")
        got, hots, counted, exps, placed, filled, noted, scattered, own = (
            s.sem(x) for x in ("got", "hots", "counted", "exps", "placed", "filled", "noted", "scattered", "own"))
        with nc.Block() as block:
            @block.sync
            def _(sp):
                sp.dma_start(ids[:], A["expert_ids"].broadcast_to([P, NE])).then_inc(got, 16)
                sp.dma_start(bids[:], A["block_ids"].broadcast_to([P, NBLK + 2])).then_inc(got, 16)
                sp.wait_ge(noted, 1)
                sp.dma_start(R["slots"].rearrange("(p a) n -> p (a n)", p=P), zero[:]).then_inc(filled, 16)

            @block.gpsimd
            def _(pool):
                nc.gpsimd.memset(zero[:], 0).then_inc(noted, 1)
                nc.gpsimd.iota(tok[:], pattern=[[P, NCX], [0, 16]], base=0, channel_multiplier=1).then_inc(noted, 1)
                pool.wait_ge(noted, 2)
                pool.wait_ge(placed, 1)
                pool.wait_ge(filled, 16)
                for c in range(NCX):
                    for k in range(2):
                        nc.gpsimd.indirect_dma_start(out=R["slots"], out_offset=bass.IndirectOffsetOnAxis(ap=dest[:, c, k:k + 1], axis=0),
                                                     in_=tok[:, c, :], in_offset=None).then_inc(scattered, 16)
                pool.wait_ge(scattered, 16 * 2 * NCX)

            @block.vector
            def _(dve):
                V = nc.vector
                st = Steps(dve, own)
                gl, el = L[:, :, 0:NG], L[:, :, NG:NG + NE]
                st.then(V.tensor_reduce(gm[:], gl, AX.X, ALU.max))
                gmw = gm[:].unsqueeze(2).broadcast_to([P, NCX, NG])
                st.then(V.tensor_tensor(oh[:], gl, gmw, ALU.is_equal))
                st.then(V.tensor_tensor(ohn[:], gl, gmw, ALU.subtract))
                dve.wait_ge(exps, 1)
                st.then(V.tensor_reduce(gs[:], ohn[:], AX.X, ALU.add))
                st.then(V.reciprocal(gs[:], gs[:]))
                st.then(V.tensor_copy(gm[:], oh[:, :, 0]))
                for g in range(1, NG):
                    st.then(V.tensor_scalar(t8[:], gm[:], -1.0, 1.0, ALU.mult, ALU.add))
                    st.then(V.tensor_tensor(oh[:, :, g], oh[:, :, g], t8[:], ALU.mult))
                    st.then(V.tensor_tensor(gm[:], gm[:], oh[:, :, g], ALU.add))
                st.then(V.tensor_scalar(ohn[:], oh[:], -NEG, NEG, ALU.mult, ALU.add))
                for g in range(NG):
                    part = em[:, :, g * EG:(g + 1) * EG]
                    w8 = lambda x: x[:, :, g:g + 1].broadcast_to([P, NCX, EG])
                    st.then(V.tensor_tensor(part, el[:, :, g * EG:(g + 1) * EG], w8(oh), ALU.mult))
                    st.then(V.tensor_tensor(part, part, w8(ohn), ALU.add))
                for c in range(NCX):
                    st.then(V.max(out=top[:, c, :], in_=em[:, c, :]))
                    st.then(V.max_index(out=topi[:, c, :], in_max=top[:, c, :], in_values=em[:, c, :]))
                st.then(V.tensor_copy(topf[:], topi[:, :, 0:2]))
                dve.wait_ge(got, 32)
                for k in range(2):
                    st.then(V.tensor_tensor(hot[:, :, k, :], ids[:].unsqueeze(1).broadcast_to([P, NCX, NE]),
                                            topf[:, :, k:k + 1].broadcast_to([P, NCX, NE]), ALU.is_equal))
                V.tensor_tensor(both[:], hot[:, :, 0, :], hot[:, :, 1, :], ALU.add).then_inc(hots, 1)
                st.then(V.tensor_tensor(t8[:], top[:, :, 1], top[:, :, 0], ALU.subtract))
                V.tensor_copy(gm[:], t8[:]).then_inc(hots, 1)
                dve.wait_ge(exps, 2)
                st.then(V.tensor_scalar(t8[:], gm[:], 1.0, None, ALU.add))
                st.then(V.reciprocal(t8[:], t8[:]))
                st.then(V.tensor_tensor(wt[:, :, 0], gs[:], t8[:], ALU.mult))
                st.then(V.tensor_tensor(wt[:, :, 1], wt[:, :, 0], gm[:], ALU.mult))
                dve.wait_ge(counted, 1)
                st.then(V.tensor_copy(cnt[:], pc[:, 0:NE]))
                st.then(V.memset(nb[:], 1.0))
                st.then(V.memset(one[:], 1.0))
                for j in range(1, SEQ // SLOT):
                    st.then(V.scalar_tensor_tensor(nb[:], cnt[:], float(SLOT * j), nb[:], ALU.is_gt, ALU.add))
                st.then(V.tensor_tensor_scan(out=cum[:], data0=one[:], data1=nb[:], initial=0.0, op0=ALU.mult, op1=ALU.add))
                st.then(V.tensor_tensor(before[:], cum[:], nb[:], ALU.subtract))
                st.then(V.scalar_tensor_tensor(evens[:], bids[:], 2.0, cum[:, NE - 1:NE].broadcast_to([P, NBLK + 2]), ALU.mult, ALU.is_lt))
                st.then(V.tensor_reduce(one[:, 0:1], evens[:], AX.X, ALU.add))
                st.then(V.tensor_copy(pairs[:], one[:, 0:1]))
                st.then(V.tensor_tensor(le[:], bids[:].unsqueeze(2).broadcast_to([P, NBLK + 2, NE]),
                                        cum[:].unsqueeze(1).broadcast_to([P, NBLK + 2, NE]), ALU.is_ge))
                st.then(V.tensor_reduce(bids[:], le[:], AX.X, ALU.add))
                st.then(V.tensor_scalar(bids[:], bids[:], float(NE - 1), None, ALU.min))
                st.then(V.tensor_copy(owner[:], bids[:]))
                st.then(V.tensor_scalar(before[:], before[:], float(SLOT), None, ALU.mult))
                st.then(V.tensor_tensor(base[:], pos[:, 0:NCX * NE].rearrange("p (c e) -> p c e", e=NE),
                                        before[:].unsqueeze(1).broadcast_to([P, NCX, NE]), ALU.add))
                for k in range(2):
                    st.then(V.tensor_tensor(hot[:, :, k, :], hot[:, :, k, :], base[:], ALU.mult))
                st.then(V.tensor_reduce(destf[:], hot[:], AX.X, ALU.add))
                V.tensor_copy(dest[:], destf[:]).then_inc(placed, 1)

            @block.scalar
            def _(act):
                act.wait_ge(own, 3)
                nc.scalar.activation(ohn[:], ohn[:], ACT.Exp).then_inc(exps, 1)
                act.wait_ge(hots, 2)
                nc.scalar.activation(gm[:], gm[:], ACT.Exp).then_inc(exps, 1)

            @block.tensor
            def _(pe):
                pe.wait_ge(hots, 1)
                for c in range(NCX):
                    for j in range(c):
                        nc.tensor.matmul(pos[:, c * NE:(c + 1) * NE], C["ones"][:], both[:, j, :], start=(j == 0), stop=False)
                    nc.tensor.matmul(pos[:, c * NE:(c + 1) * NE], C["earlier"][:], both[:, c, :], start=(c == 0), stop=True)
                for c in range(NCX):
                    mm = nc.tensor.matmul(pc[:, 0:NE], C["ones"][:], both[:, c, :], start=(c == 0), stop=(c == NCX - 1))
                mm.then_inc(counted, 1)


def experts(nc, A, R, owner, pairs, C):
    with Stage(nc, "ex") as s:
        raw = [s.sb(f"raw{c}", [P, D]) for c in range(4)]
        gh, gl, uh, ul = ([s.sb(f"{n}{j}", [P, KD, DE], F32R) for j in range(2)] for n in ("gh", "gl", "uh", "ul"))
        oh, ol = s.sb("oh", [P, DE // P, D], F32R), s.sb("ol", [P, DE // P, D], F32R)
        idx, x, y = s.sb("idx", [P, 16], I32), s.sb("x", [P, D]), s.sb("y", [P, D])
        xh, xl = s.sb("xh", [P, KD, P], F32R), s.sb("xl", [P, KD, P], F32R)
        hid, hh, hl = s.sb("hid", [P, DE]), s.sb("hh", [P, DE // P, P], F32R), s.sb("hl", [P, DE // P, P], F32R)
        px, ph, py = ([s.ps(f"{n}{j}") for j in range(2)] for n in ("px", "ph", "py"))
        pt, carry = s.ps("pt"), s.sb("carry", [P, 1])
        raw_in = s.sems("raw_in", 4)
        (zeroed, cleared, carried, rounded, left, idx_in, x_in, turned, xh_done, xl_done, g_done, u_done, silu, hid_done,
         h_turned, hh_done, hl_done, summed, taken, stored) = (s.sem(n) for n in (
             "zeroed", "cleared", "carried", "rounded", "left", "idx_in", "x_in", "turned", "xh_done", "xl_done", "g_done",
             "u_done", "silu", "hid_done", "h_turned", "hh_done", "hl_done", "summed", "taken", "stored"))
        chunk = lambda t, c: t[:].rearrange("p k n -> p (k n)")[:, c * D:(c + 1) * D]
        turn = lambda t: t[:].rearrange("p (k t) -> p k t", t=P)
        with nc.Block() as block:
            def count(eng):
                return eng.value_load(pairs[0:1, 0:1], min_val=NE // 2, max_val=NBLK // 2)

            @block.sync
            def _(sp):
                def unit(m, e, part):
                    for c in range(4):
                        if not isinstance(m, int) or m:
                            sp.wait_ge(left, m * 4 + c - 3)
                        sp.dma_start(raw[c][:], A["expert_w"][e * 12 + (part * 4 + c)]).then_inc(raw_in[c], 16)

                unit(0, 0, 0)
                unit(1, 0, 1)
                unit(2, 0, 2)
                sp.wait_ge(zeroed, 1)
                sp.dma_start(R["yrows"][NE * SLOT:NBLK * SLOT, :].rearrange("(b p) n -> p b n", p=P),
                             y[:].unsqueeze(1).broadcast_to([P, NBLK - NE, D])).then_inc(cleared, 16)
                n = count(sp)
                with sp.Fori(0, n) as i:
                    for j in range(2):
                        b = i * 2 + j
                        after = sp.value_load(owner[0:1, bass.ds(b + 1, 1)], min_val=0, max_val=NE - 1)
                        unit(b * 3 + 3, after, 0)
                        unit(b * 3 + 4, after, 1)
                        unit(b * 3 + 5, after, 2)
                        sp.wait_ge(taken, b * 2 + 2)
                        sp.dma_start(R["yrows"][bass.ds(b * SLOT, SLOT), :], y[:]).then_inc(stored, 16)

            @block.gpsimd
            def _(pool):
                n = count(pool)
                with pool.Fori(0, n * 2 + 1) as b:
                    pool.wait_ge(carried, b)
                    pool.wait_ge(x_in, b * 16)
                    pool.dma_start(idx[:], R["slots"][bass.ds(b * SLOT, SLOT), :]).then_inc(idx_in, 16)
                    pool.wait_ge(idx_in, b * 16 + 16)
                    pool.wait_ge(turned, b * 2)
                    nc.gpsimd.tensor_tensor(carry[:], C["ones"][:, 0:1], C["ones"][:, 0:1], ALU.add).then_inc(carried, 1)
                    nc.gpsimd.indirect_dma_start(out=x[:], out_offset=None, in_=R["h2rows"],
                                                 in_offset=bass.IndirectOffsetOnAxis(ap=idx[:, 0:1], axis=0)).then_inc(x_in, 16)

            @block.tensor
            def _(pe):
                def rows_turned(b):
                    pe.wait_ge(x_in, b * 16 + 16)
                    for k in range(KD):
                        mm = nc.tensor.transpose(px[k // 4][:, k % 4 * P:(k % 4 + 1) * P], x[:, k * P:(k + 1) * P], C["ident"][:])
                        if k % 4 == 3:
                            mm.then_inc(turned, 1)

                def up(b, wh, wl, out, unit, done):
                    pe.wait_ge(left, b * 12 + 4 * unit + 4)
                    for k in range(KD):
                        mm = product3(nc, out[:], (xh[:, k, :], xl[:, k, :]), (wh[:, k, :], wl[:, k, :]), k == 0, k == KD - 1)
                    mm.then_inc(done, 1)

                rows_turned(0)
                n = count(pe)
                with pe.Fori(0, n) as i:
                    for j in range(2):
                        b = i * 2 + j
                        pe.wait_ge(xl_done, b * 2 + 2)
                        pe.wait_ge(hid_done, b)
                        up(b, gh[j], gl[j], ph[0], 0, g_done)
                        up(b, uh[j], ul[j], ph[1], 1, u_done)
                        rows_turned(b + 1)
                        pe.wait_ge(hid_done, b + 1)
                        for k in range(DE // P):
                            mm = nc.tensor.transpose(pt[:, k * P:(k + 1) * P], hid[:, k * P:(k + 1) * P], C["ident"][:])
                        mm.then_inc(h_turned, 1)
                        pe.wait_ge(left, b * 12 + 12)
                        pe.wait_ge(hl_done, b + 1)
                        pe.wait_ge(taken, b * 2)
                        for g in range(2):
                            cut = slice(g * BANK, (g + 1) * BANK)
                            for k in range(DE // P):
                                mm = product3(nc, py[g][:], (hh[:, k, :], hl[:, k, :]), (oh[:, k, cut], ol[:, k, cut]), k == 0, k == DE // P - 1)
                            mm.then_inc(summed, 1)

            @block.scalar
            def _(act):
                S = nc.scalar

                def high(m, dst, cs=range(4)):
                    for c in cs:
                        act.wait_ge(raw_in[c], m * 16 + 16)
                        S.activation(chunk(dst, c), raw[c][:], ACT.Copy).then_inc(rounded, 1)

                def rows_high(b):
                    for g in range(2):
                        act.wait_ge(turned, b * 2 + g + 1)
                        S.activation(xh[:, 4 * g:4 * g + 4, :], turn(px[g]), ACT.Copy).then_inc(xh_done, 1)

                rows_high(0)
                high(0, gh[0])
                high(1, uh[0])
                n = count(act)
                with act.Fori(0, n) as i:
                    for j in range(2):
                        b = i * 2 + j
                        high(b * 3 + 2, oh)
                        act.wait_ge(g_done, b + 1)
                        S.activation(hid[:], ph[0][:], ACT.Silu).then_inc(silu, 1)
                        high(b * 3 + 3, gh[1 - j], range(2))
                        rows_high(b + 1)
                        act.wait_ge(h_turned, b + 1)
                        S.activation(hh[:], turn(pt), ACT.Copy).then_inc(hh_done, 1)
                        high(b * 3 + 3, gh[1 - j], range(2, 4))
                        high(b * 3 + 4, uh[1 - j])
                        act.wait_ge(cleared, 16)
                        act.wait_ge(summed, b * 2 + 2)
                        act.wait_ge(stored, b * 16)
                        S.activation(y[:, 0:BANK], py[0][:], ACT.Copy).then_inc(taken, 1)
                act.wait_ge(stored, n * 32)
                S.activation(hid[:, 0:1], hid[:, 0:1], ACT.Copy)

            @block.vector
            def _(dve):
                V = nc.vector

                def rest(m, dst, dst_high, cs=range(4)):
                    for c in cs:
                        dve.wait_ge(rounded, m * 4 + c + 1)
                        V.tensor_tensor(chunk(dst, c), raw[c][:], chunk(dst_high, c).bitcast(F32), ALU.subtract).then_inc(left, 1)

                def rows_rest(b):
                    for g in range(2):
                        dve.wait_ge(xh_done, b * 2 + g + 1)
                        V.tensor_tensor(xl[:, 4 * g:4 * g + 4, :], turn(px[g]), xh[:, 4 * g:4 * g + 4, :].bitcast(F32), ALU.subtract).then_inc(xl_done, 1)

                V.memset(y[:], 0.0).then_inc(zeroed, 1)
                rows_rest(0)
                rest(0, gl[0], gh[0])
                rest(1, ul[0], uh[0])
                n = count(dve)
                with dve.Fori(0, n) as i:
                    for j in range(2):
                        b = i * 2 + j
                        rest(b * 3 + 2, ol, oh)
                        rest(b * 3 + 3, gl[1 - j], gh[1 - j], range(1))
                        dve.wait_ge(u_done, b + 1)
                        dve.wait_ge(silu, b + 1)
                        V.tensor_tensor(hid[:], hid[:], ph[1][:], ALU.mult).then_inc(hid_done, 1)
                        rest(b * 3 + 3, gl[1 - j], gh[1 - j], range(1, 2))
                        rows_rest(b + 1)
                        dve.wait_ge(hh_done, b + 1)
                        V.tensor_tensor(hl[:], turn(pt), hh[:].bitcast(F32), ALU.subtract).then_inc(hl_done, 1)
                        rest(b * 3 + 3, gl[1 - j], gh[1 - j], range(2, 4))
                        rest(b * 3 + 4, ul[1 - j], uh[1 - j])
                        dve.wait_ge(cleared, 16)
                        dve.wait_ge(summed, b * 2 + 2)
                        dve.wait_ge(stored, b * 16)
                        V.tensor_copy(y[:, BANK:D], py[1][:]).then_inc(taken, 1)


def combine(nc, A, R, dest, wt, mod, x, C):
    with Stage(nc, "cb") as s:
        r = [[s.sb(f"r{j}{k}", [P, D]) for k in range(2)] for j in range(2)]
        y = [s.sb(f"y{j}", [P, D]) for j in range(2)]
        pt = [[s.ps(f"pt{j}{h}") for h in range(2)] for j in range(2)]
        got, mixed, turned, added, own = s.sems("got", 2), s.sem("mixed"), s.sem("turned"), s.sem("added"), s.sem("own")
        with nc.Block() as block:
            @block.gpsimd
            def _(pool):
                for c in range(NCX):
                    if c >= 2:
                        pool.wait_ge(mixed, c - 1)
                    for k in range(2):
                        nc.gpsimd.indirect_dma_start(out=r[c % 2][k][:], out_offset=None, in_=R["yrows"],
                                                     in_offset=bass.IndirectOffsetOnAxis(ap=dest[:, c, k:k + 1], axis=0)).then_inc(got[c % 2], 16)

            @block.vector
            def _(dve):
                st = Steps(dve, own)
                for c in range(NCX):
                    dve.wait_ge(got[c % 2], 32 * (c // 2 + 1))
                    if c >= 2:
                        dve.wait_ge(turned, c - 1)
                    st.then(nc.vector.tensor_scalar(y[c % 2][:], r[c % 2][0][:], wt[:, c, 0:1], None, ALU.mult))
                    nc.vector.scalar_tensor_tensor(y[c % 2][:], r[c % 2][1][:], wt[:, c, 1:2], y[c % 2][:], ALU.mult, ALU.add).then_inc(mixed, 1)
                    dve.wait_ge(turned, c + 1)
                    for k in range(KD):
                        xs = x[:, k, c * P:(c + 1) * P]
                        nc.vector.scalar_tensor_tensor(xs, pt[c % 2][k // 4][:, k % 4 * P:(k % 4 + 1) * P], mod[:, 5 * KD + k, 0:1], xs, ALU.mult, ALU.add).then_inc(added, 1)

            @block.tensor
            def _(pe):
                for c in range(NCX):
                    pe.wait_ge(mixed, c + 1)
                    if c >= 2:
                        pe.wait_ge(added, KD * (c - 1))
                    for k in range(KD):
                        mm = nc.tensor.transpose(pt[c % 2][k // 4][:, k % 4 * P:(k % 4 + 1) * P], y[c % 2][:, k * P:(k + 1) * P], C["ident"][:])
                    mm.then_inc(turned, 1)


def first_block(nc, A, R, C):
    with Stage(nc, "b1") as s:
        mod = s.sb("mod", [P, 6 * KD, 2])
        modulation(nc, A, C, mod)
        first_projection(nc, A, R, mod, C["ones"])
        with Stage(nc, "mix") as m:
            mixT = m.sb("mixT", [P, KD, SEQ])
            with Stage(nc, "scans") as q:
                out = q.sb("out", [P, 2, NCX, 2 * 512])
                v = q.sb("v", [P, NCH, 512])
                with Stage(nc, "gla") as g:
                    qk, fac = g.sb("qk", [P, 2, NCH, 2, 3, CH]), g.sb("fac", [P, NCH, 2, 2, 3])
                    gla_gates(nc, A, R, qk, fac, mixT[:], v[:])
                    load(nc, "lv", [(v[:], R["z_v"][0].rearrange("(c p) n -> p c n", p=P))])
                    gla_scan(nc, A, R, qk, fac, v, out[:, :, :, 0:512], C)
                load(nc, "lv2", [(v[:], R["z_v"][1].rearrange("(c p) n -> p c n", p=P))])
                with Stage(nc, "ml") as g:
                    negm, cols = g.sb("negm", [64, TOT]), g.sb("cols", [P, 2, NCH, 64])
                    mlstm_gates(nc, A, R, negm, cols, C)
                    mlstm_scan(nc, A, R, negm, cols, v, out[:, :, :, 512:1024], C)
                mixer_norm(nc, A, R, out, mixT, C)
            mixh, mixl = m.sb("mixh", [P, KD, SEQ], F32R), m.sb("mixl", [P, KD, SEQ], F32R)
            split(nc, "mixs", mixT, mixh, mixl, KD)
            gemm(nc, "wo", A["w_out"], KD, KD, lambda k, a, m: (mixh[:, k, a:a + m], mixl[:, k, a:a + m]), SEQ,
                 add_scaled(nc, lambda n: mod[:, bass.ds(n + 2 * KD, 1), 0]), evac_on="vector",
                 out_dram=R["x1"], side_dram=A["xT"].rearrange("p k t -> k p t"))
        with Stage(nc, "moe") as m:
            dest, wt, owner, pairs = m.sb("dest", [P, NCX, 2], I32), m.sb("wt", [P, NCX, 2]), m.sb("owner", [P, NBLK + 2], I32), m.sb("pairs", [P, 1], I32)
            with Stage(nc, "route") as q:
                x, h, gain = q.sb("x", [P, KD, SEQ]), q.sb("h", [P, KD, SEQ]), q.sb("gain", [P, 2, KD])
                L = q.sb("L", [P, NCX, NG + NE])
                own = q.sem("own")
                load(nc, "l2", [(x[:], R["x1"].rearrange("k p t -> p k t")), (gain[:, 0, :], A["norm2_g"])])
                with nc.Block() as block:
                    @block.vector
                    def _(dve):
                        st = Steps(dve, own)
                        st.then(nc.vector.tensor_scalar(gain[:, 1, :], mod[:, 4 * KD:5 * KD, 0], 1.0, None, ALU.add))
                        st.then(nc.vector.tensor_tensor(gain[:, 0, :], gain[:, 0, :], gain[:, 1, :], ALU.mult))
                norm_channels(nc, "n2", x, SEQ, h, lambda k: gain[:, 0, k:k + 1], lambda k: mod[:, 3 * KD + k, 0:1], C["ones"])
                router_logits(nc, A, R, h, L, C)
                route(nc, A, R, L, dest, wt, owner, pairs, C)
            experts(nc, A, R, owner, pairs, C)
            with Stage(nc, "fin") as q:
                x, g = q.sb("x", [P, KD, SEQ]), q.sb("g", [P, KD])
                load(nc, "lf", [(x[:], R["x1"].rearrange("k p t -> p k t")), (g[:], A["final_g"])])
                combine(nc, A, R, dest, wt, mod, x, C)
                norm_channels(nc, "nf", x, SEQ, x, lambda k: g[:, k:k + 1], None, C["ones"])
                load(nc, "sx", [(R["xa"].rearrange("k p t -> p k t"), x[:])])


MH, NOPE, ROPE, VH = 8, 64, 32, 64
QL, KVL = 384, 256
TWO_PI_HI = 6.28125
TWO_PI_LO = 2 * math.pi - TWO_PI_HI
ROUND = 1.5 * 2.0 ** 23
U_CQ, U_CKV, U_POOL, U_XBC, U_LG, U_LX, U_KR = 0, 3, 5, 9, 15, 19, 23
N_U = 24


def rope_tables(nc, A, cosf, sinf):
    with Stage(nc, "rope") as s:
        pos, inv = s.sb("pos", [P, SEQ], I32), s.sb("inv", [P, 1])
        got, angled, own = s.sem("got"), s.sem("angled"), s.sem("own")
        with nc.Block() as block:
            @block.sync
            def _(sp):
                sp.dma_start(pos[:], A["positions"].broadcast_to([P, SEQ])).then_inc(got, 16)
                sp.dma_start(inv[:], A["rope_inv"]).then_inc(got, 16)

            @block.vector
            def _(dve):
                V, st = nc.vector, Steps(dve, own)
                dve.wait_ge(got, 32)
                st.then(V.tensor_copy(sinf[:], pos[:]))
                st.then(V.tensor_scalar(sinf[:], sinf[:], inv[:], None, ALU.mult))
                st.then(V.tensor_scalar(cosf[:], sinf[:], 1.0 / (2 * math.pi), None, ALU.mult))
                st.then(V.tensor_scalar(cosf[:], cosf[:], ROUND, None, ALU.add))
                st.then(V.tensor_scalar(cosf[:], cosf[:], ROUND, None, ALU.subtract))
                st.then(V.scalar_tensor_tensor(sinf[:], cosf[:], -TWO_PI_HI, sinf[:], ALU.mult, ALU.add))
                st.then(V.scalar_tensor_tensor(sinf[:], cosf[:], -TWO_PI_LO, sinf[:], ALU.mult, ALU.add))
                st.then(V.tensor_scalar(cosf[:], sinf[:], math.pi / 2, -2 * math.pi, ALU.is_gt, ALU.mult))
                st.then(V.scalar_tensor_tensor(cosf[:], sinf[:], math.pi / 2, cosf[:], ALU.add, ALU.add))
                for t in (cosf, sinf):
                    st.then(V.tensor_scalar(t[:], t[:], 3.1415925, -3.1415925, ALU.min, ALU.max))
                V.tensor_copy(inv[:], inv[:]).then_inc(angled, 1)

            @block.scalar
            def _(act):
                act.wait_ge(angled, 1)
                nc.scalar.activation(cosf[:], cosf[:], ACT.Sin).then_inc(own, 1)
                nc.scalar.activation(sinf[:], sinf[:], ACT.Sin).then_inc(own, 1)


def rotate(nc, name, q, n, cosf, sinf, swap):
    with Stage(nc, name) as s:
        t = s.sb("t", [P, SEQ])
        two = min(n, 2)
        ps = [s.ps(f"ps{j}", [P, 2, BANK]) for j in range(two)]
        swapped, taken, own = s.sems("swapped", two), s.sems("taken", two), s.sem("own")
        with nc.Block() as block:
            @block.tensor
            def _(pe):
                with pe.Fori(0, n // two) as i:
                    for j in range(two):
                        pe.wait_ge(taken[j], i)
                        for c in range(2):
                            mm = nc.tensor.matmul(ps[j][:, c, :], swap[:], q[:, bass.ds(i * two + j, 1), c * BANK:(c + 1) * BANK], start=True, stop=True)
                        mm.then_inc(swapped[j], 1)

            @block.vector
            def _(dve):
                with dve.Fori(0, n // two) as i:
                    for j in range(two):
                        h = i * two + j
                        st = Steps(dve, own, h * 2)
                        qh = q[:, bass.ds(h, 1), :].rearrange("p a t -> p (a t)")
                        dve.wait_ge(swapped[j], i + 1)
                        nc.vector.tensor_tensor(t[:], ps[j][:].rearrange("p a t -> p (a t)"), sinf[:], ALU.mult).then_inc(taken[j], 1)
                        st.then(nc.vector.tensor_tensor(qh, qh, cosf[:], ALU.mult))
                        dve.wait_ge(taken[j], i + 1)
                        st.then(nc.vector.tensor_tensor(qh, qh, t[:], ALU.add))


def attention(nc, q, k, v, o, C):
    QB = SEQ // P
    SCALE = (NOPE + ROPE) ** -0.5
    with Stage(nc, "at") as s:
        qc = [s.sb(f"qc{j}", [P, SEQ]) for j in range(2)]
        pr, pT = [s.sb(f"pr{j}", [P, SEQ]) for j in range(2)], [s.sb(f"pT{j}", [P, SEQ]) for j in range(2)]
        mx, sm = [s.sb(f"mx{j}", [P, 2]) for j in range(2)], [s.sb(f"sm{j}", [P, 2]) for j in range(2)]
        S = [s.ps(f"S{j}", [P, 2 * BANK]) for j in range(2)]
        T = [s.ps(f"T{j}") for j in range(2)]
        O = [s.ps(f"O{j}") for j in range(2)]
        cut, scored, maxed, exped, turned, moved, summed, taken, own = (
            s.sem(x) for x in ("cut", "scored", "maxed", "exped", "turned", "moved", "summed", "taken", "own"))
        NT = sum(-(-(b + 1) // 4) for b in range(QB))
        before = [sum(-(-(x + 1) // 4) for x in range(b)) for b in range(QB)]
        with nc.Block() as block:
            @block.scalar
            def _(act):
                with act.Fori(0, MH // 2) as i:
                    for j in range(2):
                        hd = i * 2 + j
                        act.wait_ge(summed, hd * QB)
                        nc.scalar.activation(qc[j][:], q[:, bass.ds(hd, 1), :].rearrange("p a t -> p (a t)"), ACT.Copy).then_inc(cut, 1)
                        for b in range(QB):
                            n, w = hd * QB + b, (b + 1) * P
                            act.wait_ge(maxed, n + 1)
                            nc.scalar.activation(pr[b % 2][:, 0:w], S[b % 2][:, 0:w], ACT.Exp, bias=mx[b % 2][:, 1:2], scale=SCALE,
                                                 accum_out=sm[b % 2][:, 0:1]).then_inc(exped, 1)
                            act.wait_ge(exped, n + 1)
                            for g in range(-(-(b + 1) // 4)):
                                m = min(4, b + 1 - 4 * g)
                                act.wait_ge(turned, hd * NT + before[b] + g + 1)
                                nc.scalar.activation(pT[b % 2][:, g * BANK:g * BANK + m * P], T[(before[b] + g) % 2][:, 0:m * P], ACT.Copy).then_inc(moved, 1)

            @block.vector
            def _(dve):
                V = nc.vector
                with dve.Fori(0, MH // 2) as i:
                    for j in range(2):
                        hd = i * 2 + j
                        st = Steps(dve, own, hd * (3 * QB))

                        def greatest(b):
                            n, w = hd * QB + b, (b + 1) * P
                            dve.wait_ge(scored, n + 1)
                            st.then(V.tensor_tensor(S[b % 2][:, w - P:w], S[b % 2][:, w - P:w], C["cutq"][:], ALU.add))
                            st.then(V.reduce_max(mx[b % 2][:, 0:1], S[b % 2][:, 0:w], AX.X))
                            V.tensor_scalar(mx[b % 2][:, 1:2], mx[b % 2][:, 0:1], -SCALE, None, ALU.mult).then_inc(maxed, 1)

                        greatest(0)
                        for b in range(QB):
                            if b + 1 < QB:
                                greatest(b + 1)
                            dve.wait_ge(exped, hd * QB + b + 1)
                            st.then(V.reciprocal(sm[b % 2][:, 1:2], sm[b % 2][:, 0:1]))
                            dve.wait_ge(summed, hd * QB + b + 1)
                            V.tensor_scalar(o[:, b, bass.ds(hd * VH, VH)], O[b % 2][:, 0:VH], sm[b % 2][:, 1:2], None, ALU.mult).then_inc(taken, 1)

            @block.tensor
            def _(pe):
                with pe.Fori(0, MH // 2) as i:
                    for j in range(2):
                        hd = i * 2 + j
                        pe.wait_ge(cut, hd + 1)

                        def score(b):
                            w = (b + 1) * P
                            for a, m in chunks_of(w):
                                mm = nc.tensor.matmul(S[b % 2][:, a:a + m], qc[j][:, b * P:(b + 1) * P], k[:, bass.ds(hd, 1), a:a + m], start=True, stop=True)
                            mm.then_inc(scored, 1)

                        pe.wait_ge(taken, hd * QB)
                        score(0)
                        score(1)
                        for b in range(QB):
                            n = hd * QB + b
                            pe.wait_ge(exped, n + 1)
                            for g in range(-(-(b + 1) // 4)):
                                if before[b] + g >= 2:
                                    pe.wait_ge(moved, hd * NT + before[b] + g - 1)
                                for x in range(4 * g, min(4 * g + 4, b + 1)):
                                    mm = nc.tensor.transpose(T[(before[b] + g) % 2][:, (x - 4 * g) * P:(x - 4 * g + 1) * P], pr[b % 2][:, x * P:(x + 1) * P], C["ident"][:])
                                mm.then_inc(turned, 1)
                            if b + 2 < QB:
                                score(b + 2)
                            pe.wait_ge(moved, hd * NT + before[b] + -(-(b + 1) // 4))
                            if b >= 2:
                                pe.wait_ge(taken, n - 1)
                            for x in range(b + 1):
                                mm = nc.tensor.matmul(O[b % 2][:, 0:VH], pT[b % 2][:, x * P:(x + 1) * P], v[:, x, bass.ds(hd * VH, VH)], start=(x == 0), stop=(x == b))
                            mm.then_inc(summed, 1)


def to_channels(nc, name, o, nt, nk, dst, gain, C):
    with Stage(nc, name) as s:
        cur, out = s.sb("cur", [P, nk * P]), s.sb("out", [P, nk, nt * P])
        g = s.sb("g", [P, nk])
        ps = s.ps("ps")
        cut, turned, moved, got = s.sem("cut"), s.sem("turned"), s.sem("moved"), s.sem("got")
        with nc.Block() as block:
            @block.vector
            def _(dve):
                with dve.Fori(0, nt) as i:
                    dve.wait_ge(turned, i)
                    nc.vector.tensor_copy(cur[:], o[:, bass.ds(i, 1), :].rearrange("p a n -> p (a n)")).then_inc(cut, 1)

            @block.tensor
            def _(pe):
                with pe.Fori(0, nt) as i:
                    pe.wait_ge(cut, i + 1)
                    pe.wait_ge(moved, i * nk)
                    for k in range(nk):
                        mm = nc.tensor.transpose(ps[:, k * P:(k + 1) * P], cur[:, k * P:(k + 1) * P], C["ident"][:])
                    mm.then_inc(turned, 1)

            @block.scalar
            def _(act):
                if gain is not None:
                    act.dma_start(g[:], gain).then_inc(got, 16)
                    act.wait_ge(got, 16)
                with act.Fori(0, nt) as i:
                    act.wait_ge(turned, i + 1)
                    for k in range(nk):
                        nc.scalar.activation(out[:, k, bass.ds(i * P, P)], ps[:, k * P:(k + 1) * P], ACT.Copy,
                                             scale=1.0 if gain is None else g[:, k:k + 1]).then_inc(moved, 1)
                act.wait_ge(moved, nt * nk)
                act.dma_start(dst.rearrange("k p t -> p k t"), out[:]).then_inc(got, 16)
                act.wait_ge(got, 16 if gain is None else 32)


def mla(nc, A, R, C):
    with Stage(nc, "mla") as s:
        q, k, v = s.sb("q", [P, MH, SEQ]), s.sb("k", [P, MH, SEQ]), s.sb("v", [P, SEQ // P, MH * VH])
        with Stage(nc, "mlp") as m:
            cq, ckv, kr = m.sb("cq", [P, 3, SEQ]), m.sb("ckv", [P, 2, SEQ]), m.sb("kr", [P, 1, SEQ])
            cosf, sinf, swap = m.sb("cosf", [P, SEQ]), m.sb("sinf", [P, SEQ]), m.sb("swap", [P, P])
            gq, gkv, wv = m.sb("gq", [P, 3]), m.sb("gkv", [P, 2]), m.sb("wv", [P, 2, MH * VH])
            load(nc, "ldm", [(cq[:], R["u"][U_CQ:U_CQ + 3].rearrange("n p t -> p n t")), (ckv[:], R["u"][U_CKV:U_CKV + 2].rearrange("n p t -> p n t")),
                             (kr[:], R["u"][U_KR:U_KR + 1].rearrange("n p t -> p n t")), (swap[:], A["swap"]),
                             (gq[:], A["q_norm"]), (gkv[:], A["kv_norm"]), (wv[:], A["w_uv"])])
            rope_tables(nc, A, cosf, sinf)
            norm_channels(nc, "nq", cq, SEQ, cq, lambda n: gq[:, n:n + 1], None, C["ones"], width=QL)
            norm_channels(nc, "nkv", ckv, SEQ, ckv, lambda n: gkv[:, n:n + 1], None, C["ones"], width=KVL)
            gemm_small(nc, "uq", A["w_uq"], 3, MH, lambda n, a, w: cq[:, n, a:a + w], SEQ,
                 lambda ns, out, ps, n, a, w, side: nc.scalar.activation(q[:, bass.ds(n, 1), a:a + w], ps.unsqueeze(1), ACT.Copy))
            rotate(nc, "rotq", q, MH, cosf, sinf, swap)
            rotate(nc, "rotk", kr, 1, cosf, sinf, swap)
            gemm_small(nc, "uk", A["w_uk"], 2, MH, lambda n, a, w: ckv[:, n, a:a + w], SEQ,
                 lambda ns, out, ps, n, a, w, side: nc.vector.tensor_tensor(k[:, bass.ds(n, 1), a:a + w], ps.unsqueeze(1), kr[:, :, a:a + w], ALU.add), evac_on="vector")
            with Stage(nc, "uv") as u:
                ps = [u.ps(f"p{c}") for c in range(SEQ // P)]
                summed, moved = u.sem("summed"), u.sem("moved")
                with nc.Block() as block:
                    @block.tensor
                    def _(pe):
                        for c in range(SEQ // P):
                            for n in range(2):
                                mm = nc.tensor.matmul(ps[c][:], ckv[:, n, c * P:(c + 1) * P], wv[:, n, :], start=(n == 0), stop=(n == 1))
                            mm.then_inc(summed, 1)

                    @block.scalar
                    def _(act):
                        for c in range(SEQ // P):
                            act.wait_ge(summed, c + 1)
                            nc.scalar.activation(v[:, c, :], ps[c][:], ACT.Copy).then_inc(moved, 1)
        o = s.sb("o", [P, SEQ // P, MH * VH])
        attention(nc, q, k, v, o, C)
        to_channels(nc, "ato", o, SEQ // P, 4, R["y"][0:4], None, C)


def pool_mixer(nc, A, R, C):
    PAD = 16
    with Stage(nc, "po") as s:
        u = s.sb("u", [P, 4, SEQ])
        buf = [s.sb(f"b{j}", [P, PAD + SEQ]) for j in range(3)]
        inv, w, sc = s.sb("inv", [P, 4, SEQ]), s.sb("w", [P, 4, P]), s.sb("sc", [P, 4])
        d, y = s.sb("d", [P, 4, SEQ]), s.sb("y", [P, 4, SEQ])
        ps = [s.ps(f"p{c}") for c in range(8)]
        got, pooled, summed, own, moved = s.sem("got"), s.sem("pooled"), s.sem("summed"), s.sem("own"), s.sem("moved")
        with nc.Block() as block:
            @block.sync
            def _(sp):
                for a, b in ((u[:], R["u"][U_POOL:U_POOL + 4].rearrange("n p t -> p n t")), (inv[:], A["pool_inv"].rearrange("(o g) t -> o g t", o=1).broadcast_to([P, 4, SEQ])),
                             (w[:], A["w_pool"]), (sc[:], A["pool_scale"])):
                    sp.dma_start(a, b).then_inc(got, 16)
                sp.wait_ge(moved, 8)
                sp.dma_start(R["y"][4:8].rearrange("n p t -> p n t"), y[:]).then_inc(got, 16)
                sp.wait_ge(got, 80)

            @block.vector
            def _(dve):
                V, st = nc.vector, Steps(dve, own)
                for j in range(3):
                    st.then(V.memset(buf[j][:, 0:PAD], 0.0))
                dve.wait_ge(got, 64)
                for g in range(4):
                    st.then(V.tensor_copy(buf[0][:, PAD:], u[:, g, :]))
                    src = 0
                    for j in range(g + 1):
                        dst = 1 + j % 2
                        st.then(V.tensor_tensor(buf[dst][:, PAD:], buf[src][:, PAD:], buf[src][:, PAD - 2 ** j:PAD - 2 ** j + SEQ], ALU.add))
                        src = dst
                    st.then(V.tensor_tensor(d[:, g, :], buf[src][:, PAD:], inv[:, g, :], ALU.mult))
                    V.tensor_tensor(d[:, g, :], d[:, g, :], u[:, g, :], ALU.subtract).then_inc(pooled, 1)

            @block.tensor
            def _(pe):
                for g in range(4):
                    pe.wait_ge(pooled, g + 1)
                    for c in range(2):
                        nc.tensor.matmul(ps[2 * g + c][:], w[:, g, :], d[:, g, c * BANK:(c + 1) * BANK], start=True, stop=True).then_inc(summed, 1)

            @block.scalar
            def _(act):
                act.wait_ge(got, 64)
                for n in range(8):
                    act.wait_ge(summed, n + 1)
                    nc.scalar.activation(y[:, n // 2, n % 2 * BANK:(n % 2 + 1) * BANK], ps[n][:], ACT.Copy, scale=sc[:, n // 2:n // 2 + 1]).then_inc(moved, 1)


def conv_causal(V, st, out, x, w):
    st.then(V.tensor_scalar(out, x[:, 0:SEQ], w(0), None, ALU.mult))
    for i in range(1, 4):
        st.then(V.scalar_tensor_tensor(out, x[:, i:i + SEQ], w(i), out, ALU.mult, ALU.add))


def rglru(nc, A, R, C):
    with Stage(nc, "lr") as s:
        x = [s.sb(f"x{j}", [P, 3 + SEQ]) for j in range(2)]
        g = [s.sb(f"g{j}", [P, SEQ]) for j in range(2)]
        a, t = s.sb("a", [P, SEQ]), s.sb("t", [P, SEQ])
        xcs, rs, its = ([s.sb(f"{n}{j}", [P, SEQ]) for j in range(2)] for n in ("xc", "r", "it"))
        wa, wi = s.sb("wa", [P, 4, P]), s.sb("wi", [P, 4, P])
        cw, cb, ba, bi, lam, sp8 = s.sb("cw", [P, 4, 4]), s.sb("cb", [P, 4]), s.sb("ba", [P, 4]), s.sb("bi", [P, 4]), s.sb("lam", [P, 4]), s.sb("sp8", [P, 4])
        ps = [s.ps(f"p{c}") for c in range(4)]
        got, x_in, convd, summed, gated, ready, own, stored, done, act_own, gelued = (
            s.sem("got"), s.sems("x_in", 2), *(s.sem(n) for n in ("convd", "summed", "gated", "ready", "own")), s.sems("stored", 2),
            *(s.sem(n) for n in ("done", "act_own", "gelued")))
        with nc.Block() as block:
            @block.sync
            def _(sp):
                for p_, q_ in ((wa, "lru_w_a"), (wi, "lru_w_i"), (cw, "lru_conv_w"), (cb, "lru_conv_b"), (ba, "lru_b_a"), (bi, "lru_b_i"), (lam, "lru_lambda")):
                    sp.dma_start(p_[:], A[q_]).then_inc(got, 16)
                for n in range(4):
                    if n >= 2:
                        sp.wait_ge(stored[n % 2], 16 * (n // 2))
                    sp.dma_start(x[n % 2][:, 3:], R["u"][U_LX + n]).then_inc(x_in[n % 2], 16)
                    sp.dma_start(g[n % 2][:], R["u"][U_LG + n]).then_inc(x_in[n % 2], 16)

            @block.vector
            def _(dve):
                V, st = nc.vector, Steps(dve, own)
                for j in range(2):
                    st.then(V.memset(x[j][:, 0:3], 0.0))
                dve.wait_ge(got, 112)
                st.then(V.scalar_tensor_tensor(sp8[:], lam[:], -1.0, lam[:], ALU.mult, ALU.min))
                dve.wait_ge(act_own, 2)
                st.then(V.tensor_scalar(lam[:], lam[:], -1.0, 0.0, ALU.mult, ALU.max))
                st.then(V.tensor_tensor(lam[:], lam[:], sp8[:], ALU.add))
                st.then(V.tensor_scalar(lam[:], lam[:], -8.0, None, ALU.mult))

                def conv(n):
                    xc = xcs[n % 2]
                    dve.wait_ge(x_in[n % 2], 32 * (n // 2 + 1))
                    conv_causal(V, st, xc[:], x[n % 2], lambda i: cw[:, n, i:i + 1])
                    V.tensor_scalar(xc[:], xc[:], cb[:, n:n + 1], None, ALU.add).then_inc(convd, 1)

                conv(0)
                for n in range(4):
                    if n < 3:
                        conv(n + 1)
                    xc, r, it = xcs[n % 2], rs[n % 2], its[n % 2]
                    dve.wait_ge(gated, 4 * n + 4)
                    V.tensor_scalar(r[:], r[:], lam[:, n:n + 1], None, ALU.mult).then_inc(ready, 1)
                    st.then(V.tensor_tensor(xc[:], xc[:], it[:], ALU.mult))
                    dve.wait_ge(act_own, 2 + 3 * n + 2)
                    st.then(V.tensor_tensor(it[:], a[:], a[:], ALU.mult))
                    st.then(V.scalar_tensor_tensor(t[:], it[:], 1.0, t[:], ALU.add, ALU.mult))
                    V.tensor_copy(it[:], t[:]).then_inc(ready, 1)
                    dve.wait_ge(act_own, 2 + 3 * n + 3)
                    st.then(V.tensor_tensor(xc[:], xc[:], it[:], ALU.mult))
                    st.then(V.tensor_tensor_scan(out=t[:], data0=a[:], data1=xc[:], initial=0.0, op0=ALU.mult, op1=ALU.add))
                    dve.wait_ge(gelued, n + 1)
                    V.tensor_tensor(g[n % 2][:], g[n % 2][:], t[:], ALU.mult).then_inc(done, 1)

            @block.tensor
            def _(pe):
                for n in range(4):
                    pe.wait_ge(convd, n + 1)
                    if n:
                        pe.wait_ge(gated, 4 * n)
                    for c in range(4):
                        w = wa if c < 2 else wi
                        nc.tensor.matmul(ps[c][:], w[:, n, :], xcs[n % 2][:, c % 2 * BANK:(c % 2 + 1) * BANK], start=True, stop=True).then_inc(summed, 1)

            @block.scalar
            def _(act):
                S = nc.scalar
                act.wait_ge(got, 112)
                act.wait_ge(own, 3)
                S.activation(sp8[:], sp8[:], ACT.Exp).then_inc(act_own, 1)
                act.wait_ge(act_own, 1)
                S.activation(sp8[:], sp8[:], ACT.Ln, bias=1.0).then_inc(act_own, 1)

                def gates(n):
                    for c in range(4):
                        act.wait_ge(summed, 4 * n + c + 1)
                        dst, b = (rs[n % 2], ba) if c < 2 else (its[n % 2], bi)
                        S.activation(dst[:, c % 2 * BANK:(c % 2 + 1) * BANK], ps[c][:], ACT.Sigmoid, bias=b[:, n:n + 1]).then_inc(gated, 1)

                gates(0)
                for n in range(4):
                    r, it = rs[n % 2], its[n % 2]
                    act.wait_ge(ready, 2 * n + 1)
                    S.activation(a[:], r[:], ACT.Exp).then_inc(act_own, 1)
                    S.activation(t[:], r[:], ACT.Tanh, scale=-1.0).then_inc(act_own, 1)
                    act.wait_ge(x_in[n % 2], 32 * (n // 2 + 1))
                    S.activation(g[n % 2][:], g[n % 2][:], ACT.Gelu_apprx_tanh).then_inc(gelued, 1)
                    act.wait_ge(ready, 2 * n + 2)
                    S.activation(it[:], it[:], ACT.Sqrt).then_inc(act_own, 1)
                    if n < 3:
                        gates(n + 1)
                    act.wait_ge(done, n + 1)
                    act.dma_start(R["y"][12 + n], g[n % 2][:]).then_inc(stored[n % 2], 16)
                for j in range(2):
                    act.wait_ge(stored[j], 32)


SH, SHD, SDN = 8, 64, 64
NCK = SEQ // P


def ssd_conv(nc, A, R, xt, bt, bch, cz, C):
    with Stage(nc, "sc") as s:
        x = [s.sb(f"x{j}", [P, 3 + SEQ]) for j in range(2)]
        xo, cur = s.sb("xo", [P, 6, SEQ]), s.sb("cur", [P, 5, P])
        cw, cb = s.sb("cw", [P, 6, 4]), s.sb("cb", [P, 6])
        ps = s.ps("ps", [P, 2 * BANK])
        got, x_in, own, convd, silu, cut, turned, moved, padded = (s.sem("got"), s.sems("x_in", 2), *(s.sem(n) for n in (
            "own", "convd", "silu", "cut", "turned", "moved", "padded")))
        with nc.Block() as block:
            @block.sync
            def _(sp):
                sp.dma_start(cw[:], A["ssd_conv_w"]).then_inc(got, 16)
                sp.dma_start(cb[:], A["ssd_conv_b"]).then_inc(got, 16)
                for n in range(6):
                    if n >= 2:
                        sp.wait_ge(convd, n - 1)
                    sp.dma_start(x[n % 2][:, 3:], R["u"][U_XBC + n]).then_inc(x_in[n % 2], 16)

            @block.vector
            def _(dve):
                V, st = nc.vector, Steps(dve, own)
                for j in range(2):
                    st.then(V.memset(x[j][:, 0:3], 0.0))
                st.then(V.memset(cz[:], 0.0))
                dve.wait_ge(got, 32)
                for n in range(6):
                    dve.wait_ge(x_in[n % 2], 16 * (n // 2 + 1))
                    conv_causal(V, st, xo[:, n, :], x[n % 2], lambda i: cw[:, n, i:i + 1])
                    V.tensor_copy(cb[:, n:n + 1], cb[:, n:n + 1]).then_inc(convd, 1)
                with dve.Fori(0, NCK) as i:
                    dve.wait_ge(silu, 6)
                    dve.wait_ge(turned, i)
                    V.tensor_copy(cur[:], xo[:, 0:5, bass.ds(i * P, P)]).then_inc(cut, 1)
                V.tensor_copy(bch[:], xo[:, 4, :]).then_inc(padded, 1)
                for g in range(2):
                    V.tensor_copy(cz[g * 64:g * 64 + 64, g, :], xo[g * 64:g * 64 + 64, 5, :]).then_inc(padded, 1)
                dve.wait_ge(padded, 3)

            @block.scalar
            def _(act):
                act.wait_ge(got, 32)
                for n in range(6):
                    act.wait_ge(convd, n + 1)
                    nc.scalar.activation(xo[:, n, :], xo[:, n, :], ACT.Silu, bias=cb[:, n:n + 1]).then_inc(silu, 1)
                with act.Fori(0, NCK) as i:
                    act.wait_ge(turned, i + 1)
                    nc.scalar.activation(xt[:, bass.ds(i, 1), :], ps[:, 0:BANK].unsqueeze(1), ACT.Copy).then_inc(moved, 1)
                    nc.scalar.activation(bt[:, bass.ds(i, 1), :], ps[:, BANK:BANK + P].unsqueeze(1), ACT.Copy).then_inc(moved, 1)

            @block.tensor
            def _(pe):
                with pe.Fori(0, NCK) as i:
                    pe.wait_ge(cut, i + 1)
                    pe.wait_ge(moved, i * 2)
                    for n in range(5):
                        mm = nc.tensor.transpose(ps[:, n * P:(n + 1) * P], cur[:, n, :], C["ident"][:])
                    mm.then_inc(turned, 1)


def ssd_decays(nc, A, R, dt, a, acs, tot, eacs, back, incl, C):
    with Stage(nc, "sa") as s:
        al, bi, u = s.sb("al", [P, SH]), s.sb("bi", [P, SH]), s.sb("u", [P, NCK, SH])
        dtr = s.sb("dtr", [SH, SEQ])
        ps, pt, pd = s.ps("ps"), s.ps("pt"), s.ps("pd")
        turned = s.sem("turned")
        got, own, ready, exped, summed = (s.sem(n) for n in ("got", "own", "ready", "exped", "summed"))
        with nc.Block() as block:
            @block.sync
            def _(sp):
                sp.dma_start(dtr[:], R["u"][U_KR, NOPE + ROPE:NOPE + ROPE + SH, :]).then_inc(got, 16)
                sp.dma_start(al[:], A["ssd_a_log"].broadcast_to([P, SH])).then_inc(got, 16)
                sp.dma_start(bi[:], A["ssd_dt_bias"].broadcast_to([P, SH])).then_inc(got, 16)

            @block.vector
            def _(dve):
                V, st = nc.vector, Steps(dve, own)
                over = lambda x: x[:].unsqueeze(1).broadcast_to([P, NCK, SH])
                dve.wait_ge(got, 48)
                st.then(V.tensor_tensor(incl[:], C["earlier"][:], C["ident"][:], ALU.add))
                dve.wait_ge(turned, 1)
                st.then(V.tensor_tensor(dt[:], pd[:, 0:NCK * SH].rearrange("p (c h) -> p c h", h=SH), over(bi), ALU.add))
                V.scalar_tensor_tensor(u[:], dt[:], -1.0, dt[:], ALU.mult, ALU.min).then_inc(ready, 1)
                dve.wait_ge(exped, 3)
                st.then(V.scalar_tensor_tensor(dt[:], dt[:], 0.0, u[:], ALU.max, ALU.add))
                st.then(V.scalar_tensor_tensor(a[:], dt[:], -1.0, over(al), ALU.mult, ALU.mult))
                V.tensor_copy(al[:], al[:]).then_inc(ready, 1)
                dve.wait_ge(summed, 2)
                flat = lambda x: x[:].rearrange("p c h -> p (c h)")
                st.then(V.tensor_copy(flat(acs), ps[:, 0:NCK * SH]))
                st.then(V.tensor_copy(flat(tot), pt[:, 0:NCK * SH]))
                V.tensor_tensor(back[:], tot[:], acs[:], ALU.subtract).then_inc(ready, 1)

            @block.tensor
            def _(pe):
                pe.wait_ge(got, 48)
                for c in range(NCK):
                    mm = nc.tensor.transpose(pd[:, c * SH:(c + 1) * SH], dtr[:, c * P:(c + 1) * P], C["ident"][0:SH, 0:SH])
                mm.then_inc(turned, 1)
                pe.wait_ge(ready, 2)
                nc.tensor.matmul(ps[:, 0:NCK * SH], incl[:], a[:].rearrange("p c h -> p (c h)"), start=True, stop=True).then_inc(summed, 1)
                nc.tensor.matmul(pt[:, 0:NCK * SH], C["ones"][:], a[:].rearrange("p c h -> p (c h)"), start=True, stop=True).then_inc(summed, 1)

            @block.scalar
            def _(act):
                S = nc.scalar
                act.wait_ge(got, 48)
                S.activation(al[:], al[:], ACT.Exp).then_inc(exped, 1)
                act.wait_ge(ready, 1)
                S.activation(u[:], u[:], ACT.Exp).then_inc(exped, 1)
                act.wait_ge(exped, 2)
                S.activation(u[:], u[:], ACT.Ln, bias=1.0).then_inc(exped, 1)
                act.wait_ge(ready, 3)
                S.activation(eacs[:], acs[:], ACT.Exp).then_inc(exped, 1)
                S.activation(back[:], back[:], ACT.Exp).then_inc(exped, 1)
                S.activation(tot[:], tot[:], ACT.Exp).then_inc(exped, 1)


def ssd(nc, A, R, C):
    with Stage(nc, "sd") as s:
        xt, y = s.sb("xt", [P, NCK, SH * SHD]), s.sb("y", [P, NCK, SH * SHD])
        bt, bch, cz = s.sb("bt", [P, NCK, P]), s.sb("bch", [P, SEQ]), s.sb("cz", [P, 2, SEQ])
        dt, a, acs, tot, eacs, back = (s.sb(n, [P, NCK, SH]) for n in ("dt", "a", "acs", "tot", "eacs", "back"))
        incl = s.sb("incl", [P, P])
        ssd_conv(nc, A, R, xt, bt, bch, cz, C)
        ssd_decays(nc, A, R, dt, a, acs, tot, eacs, back, incl, C)
        with Stage(nc, "ss") as q:
            abc, L, M = q.sb("abc", [P, SH, P]), q.sb("L", [P, SH, P]), q.sb("M", [P, SH, P])
            bc, btc, cc = q.sb("bc", [P, P]), q.sb("btc", [P, P]), q.sb("cc", [P, 2, P])
            xdt, xb, S, t, dsk = (q.sb(n, [P, SH * SHD]) for n in ("xdt", "xb", "S", "t", "dsk"))
            d8 = q.sb("d8", [P, SH])
            rows, cb, yd, yo, new = q.ps("rows", [P, 2 * BANK]), q.ps("cb"), q.ps("yd"), q.ps("yo"), q.ps("new")
            got, own, cut, rowed, ready, exped, masked, summed, xb_done = (q.sem(n) for n in (
                "got", "own", "cut", "rowed", "ready", "exped", "masked", "summed", "xb_done"))
            heads = lambda x: x.rearrange("p (h d) -> p h d", h=SH)
            wide = lambda x: x.rearrange("p c h -> p (c h)").unsqueeze(2).broadcast_to([P, SH, SHD])
            with nc.Block() as block:
                @block.sync
                def _(sp):
                    sp.dma_start(d8[:], A["ssd_d"].broadcast_to([P, SH])).then_inc(got, 16)

                @block.vector
                def _(dve):
                    V = nc.vector
                    dve.wait_ge(got, 16)
                    V.tensor_copy(heads(dsk[:]), d8[:].unsqueeze(2).broadcast_to([P, SH, SHD])).then_inc(own, 1)
                    V.memset(S[:], 0.0).then_inc(own, 1)
                    dve.wait_ge(own, 2)
                    with dve.Fori(0, NCK) as i:
                        st = Steps(dve, own, i * 8 + 2)
                        at = lambda x: x[:, bass.ds(i, 1), :]
                        x_i = heads(at(xt).rearrange("p a n -> p (a n)"))
                        y_i = at(y).rearrange("p a n -> p (a n)")
                        st.then(V.tensor_tensor(heads(xdt[:]), x_i, wide(at(dt)), ALU.mult))
                        V.tensor_tensor(heads(xb[:]), heads(xdt[:]), wide(at(back)), ALU.mult).then_inc(xb_done, 1)
                        dve.wait_ge(rowed, i * 2 + 1)
                        st.then(V.tensor_tensor(L[:], heads(rows[:]), at(acs).rearrange("p c h -> p (c h)").unsqueeze(2).broadcast_to([P, SH, P]), ALU.subtract))
                        V.tensor_tensor(L[:], L[:], C["cut"][:, 0:1, :].broadcast_to([P, SH, P]), ALU.min).then_inc(ready, 1)
                        st.then(V.tensor_tensor(t[:], at(xt).rearrange("p a n -> p (a n)"), dsk[:], ALU.mult))
                        dve.wait_ge(exped, i + 1)
                        dve.wait_ge(rowed, i * 2 + 2)
                        for g in range(2):
                            V.tensor_tensor(M[:, 4 * g:4 * g + 4, :], L[:, 4 * g:4 * g + 4, :],
                                            cb[:, g * P:(g + 1) * P].unsqueeze(1).broadcast_to([P, 4, P]), ALU.mult).then_inc(masked, 1)
                        dve.wait_ge(summed, i * 3 + 1)
                        st.then(V.tensor_tensor(heads(y_i), heads(yo[:]), wide(at(eacs)), ALU.mult))
                        st.then(V.tensor_tensor(y_i, y_i, t[:], ALU.add))
                        st.then(V.tensor_tensor(heads(S[:]), heads(S[:]), wide(at(tot)), ALU.mult))
                        dve.wait_ge(summed, i * 3 + 2)
                        st.then(V.tensor_tensor(S[:], S[:], new[:], ALU.add))
                        dve.wait_ge(summed, i * 3 + 3)
                        st.then(V.tensor_tensor(y_i, y_i, yd[:], ALU.add))

                @block.tensor
                def _(pe):
                    mmul = nc.tensor.matmul
                    with pe.Fori(0, NCK) as i:
                        pe.wait_ge(cut, i * 4 + 4)
                        pe.wait_ge(masked, i * 2)
                        for h in range(SH):
                            mm = mmul(rows[:, h * P:(h + 1) * P], abc[:, h, :], incl[:], start=True, stop=True)
                        mm.then_inc(rowed, 1)
                        for g in range(2):
                            mm = mmul(cb[:, g * P:(g + 1) * P], bc[:], cc[:, g, :], start=True, stop=True)
                        mm.then_inc(rowed, 1)
                        pe.wait_ge(own, i * 8 + 2)
                        for g in range(2):
                            mm = mmul(yo[:, g * 256:(g + 1) * 256], cc[:, g, :], S[:, g * 256:(g + 1) * 256], start=True, stop=True)
                        mm.then_inc(summed, 1)
                        pe.wait_ge(xb_done, i + 1)
                        mmul(new[:], btc[:], xb[:], start=True, stop=True).then_inc(summed, 1)
                        pe.wait_ge(masked, i * 2 + 2)
                        for h in range(SH):
                            mm = mmul(yd[:, h * SHD:(h + 1) * SHD], M[:, h, :], xdt[:, h * SHD:(h + 1) * SHD], start=True, stop=True)
                        mm.then_inc(summed, 1)

                @block.scalar
                def _(act):
                    with act.Fori(0, NCK) as i:
                        at = lambda x: x[:, bass.ds(i, 1), :].rearrange("p a n -> p (a n)")
                        act.wait_ge(summed, i * 3)
                        for dst, src in ((abc, at(a).unsqueeze(2).broadcast_to([P, SH, P])), (bc, bch[:, bass.ds(i * P, P)]),
                                         (cc, cz[:, :, bass.ds(i * P, P)]), (btc, at(bt))):
                            nc.scalar.activation(dst[:], src, ACT.Copy).then_inc(cut, 1)
                        act.wait_ge(ready, i + 1)
                        nc.scalar.activation(L[:], L[:], ACT.Exp).then_inc(exped, 1)
        with Stage(nc, "sg") as q:
            z, ms = q.sb("z", [P, NCK, SH * SHD]), q.sb("ms", [P, NCK])
            got, own, silu, rooted = (q.sem(n) for n in ("got", "own", "silu", "rooted"))
            with nc.Block() as block:
                @block.sync
                def _(sp):
                    sp.dma_start(z[:], R["z2"][0].rearrange("(c p) n -> p c n", p=P)).then_inc(got, 16)

                @block.scalar
                def _(act):
                    act.wait_ge(got, 16)
                    nc.scalar.activation(z[:], z[:], ACT.Silu).then_inc(silu, 1)
                    act.wait_ge(own, 4)
                    nc.scalar.activation(ms[:], ms[:], ACT.Sqrt).then_inc(rooted, 1)

                @block.vector
                def _(dve):
                    V, st = nc.vector, Steps(dve, own)
                    dve.wait_ge(silu, 1)
                    st.then(V.tensor_tensor(y[:], y[:], z[:], ALU.mult))
                    st.then(V.tensor_tensor(z[:], y[:], y[:], ALU.mult))
                    st.then(V.reduce_sum(ms[:], z[:], AX.X))
                    st.then(V.tensor_scalar(ms[:], ms[:], 1.0 / (SH * SHD), EPS, ALU.mult, ALU.add))
                    dve.wait_ge(rooted, 1)
                    st.then(V.reciprocal(ms[:], ms[:]))
                    st.then(V.tensor_tensor(y[:], y[:], ms[:].unsqueeze(2).broadcast_to([P, NCK, SH * SHD]), ALU.mult))
        to_channels(nc, "sdo", y, NCK, 4, R["y"][8:12], A["ssd_norm"], C)


def gated_products(nc, name, w, kb, h, y, turns, acc):
    with Stage(nc, name) as s:
        W = Weights(nc, s, w, (KD + kb) * P, KD * turns)
        sg, t = [s.sb(f"sg{j}", [P, SEQ]) for j in range(2)], s.sb("t", [P, SEQ])
        yr, yh, yl = s.sb("yr", [P, kb, SEQ]), s.sb("yh", [P, kb, SEQ], F32R), s.sb("yl", [P, kb, SEQ], F32R)
        ps = [s.ps(f"g{j}", [P, 2 * BANK]) for j in range(2)]
        py = [s.ps(f"y{j}", [P, 2 * BANK]) for j in range(2)]
        summed, gated, taken, own = s.sem("summed"), s.sem("gated"), s.sems("taken", 2), s.sem("own")
        y_in, y_high, y_split = s.sem("y_in"), s.sem("y_high"), s.sem("y_split")
        with nc.Block() as block:
            @block.sync
            def _(sp):
                W.load(sp)

            @block.gpsimd
            def _(pool):
                W.halve(pool)

            @block.tensor
            def _(pe):
                for b in range(turns):
                    with pe.Fori(0, KD // 2) as i:
                        for j in range(2):
                            pe.wait_ge(W.split[j], i + b * KD // 2 + 1)
                            pe.wait_ge(taken[j], i + b * KD // 2)
                            for c in range(2):
                                cut = slice(c * BANK, (c + 1) * BANK)
                                for k in range(KD):
                                    mm = product3(nc, ps[j][:, cut], W.tile(j, k), (h[0][:, k, cut], h[1][:, k, cut]), k == 0, k == KD - 1)
                            mm.then_inc(summed, 1)
                            pe.wait_ge(y_split, (b + 1) * kb)
                            for c in range(2):
                                cut = slice(c * BANK, (c + 1) * BANK)
                                for k in range(kb):
                                    mm = product3(nc, py[j][:, cut], W.tile(j, KD + k), (yh[:, k, cut], yl[:, k, cut]), k == 0, k == kb - 1)
                            mm.then_inc(W.used[j], 1)

            @block.scalar
            def _(act):
                act.dma_start(yr[:], y(0)).then_inc(y_in, 16)
                for b in range(turns):
                    act.wait_ge(y_in, (b + 1) * 16)
                    if b:
                        act.wait_ge(W.used[1], b * KD // 2)
                    for k in range(kb):
                        nc.scalar.activation(yh[:, k], yr[:, k], ACT.Copy).then_inc(y_high, 1)
                    with act.Fori(0, KD // 2) as i:
                        for j in range(2):
                            act.wait_ge(summed, i * 2 + b * KD + j + 1)
                            act.wait_ge(taken[j], i + b * KD // 2)
                            nc.scalar.activation(sg[j][:], ps[j][:], ACT.Sigmoid).then_inc(gated, 1)
                    if b + 1 < turns:
                        act.wait_ge(y_split, (b + 1) * kb)
                        act.dma_start(yr[:], y(b + 1)).then_inc(y_in, 16)

            @block.vector
            def _(dve):
                for b in range(turns):
                    for k in range(kb):
                        dve.wait_ge(y_high, b * kb + k + 1)
                        nc.vector.tensor_tensor(yl[:, k], yr[:, k], yh[:, k].bitcast(F32), ALU.subtract).then_inc(y_split, 1)
                    with dve.Fori(0, KD // 2) as i:
                        for j in range(2):
                            n = i * 2 + j
                            dve.wait_ge(W.used[j], i + b * KD // 2 + 1)
                            dve.wait_ge(gated, n + b * KD + 1)
                            dve.wait_ge(own, n + b * KD)
                            nc.vector.tensor_tensor(t[:], sg[j][:], py[j][:], ALU.mult).then_inc(taken[j], 1)
                            dve.wait_ge(taken[j], i + b * KD // 2 + 1)
                            a = acc[:, bass.ds(n, 1), :].rearrange("p a t -> p (a t)")
                            nc.vector.tensor_tensor(a, a, t[:], ALU.add).then_inc(own, 1)


def second_block(nc, A, R, C, out):
    tiles_of = lambda r: r.rearrange("k p t -> p k t")
    with Stage(nc, "b2") as s:
        gains = s.sb("gains", [P, 4, KD])
        high, rest = s.sb("high", [P, KD, SEQ], F32R), s.sb("rest", [P, KD, SEQ], F32R)
        pair = lambda k, a, m: (high[:, k, a:a + m], rest[:, k, a:a + m])
        with Stage(nc, "in5") as f:
            x = f.sb("x", [P, KD, SEQ])
            load(nc, "l5", [(gains[:, n, :], A[g]) for n, g in enumerate(("g_mix", "g_mlp", "g_ple", "g_final"))] + [(x[:], tiles_of(R["xa"]))])
            norm_split(nc, "n5", x, SEQ, high, rest, lambda k: gains[:, 0, k:k + 1], None, C["ones"])
        gemm(nc, "u1", A["w_in2"], KD, N_U, pair, SEQ, lambda ns, out, ps, n, a, m, side: ns.activation(out, ps, ACT.Copy), out_dram=R["u"])
        gemm_tokens(nc, "u2", A["w_in_z"], 1, 512, high, rest, 0, NCK, R["z2"])
        mla(nc, A, R, C)
        pool_mixer(nc, A, R, C)
        ssd(nc, A, R, C)
        rglru(nc, A, R, C)
        with Stage(nc, "out5") as f:
            x = f.sb("x", [P, KD, SEQ])
            branches(nc, A, R, x, high, rest)
            split(nc, "sm", x, high, rest, KD)
            gemm(nc, "wo2", A["w_out2"], KD, KD, pair, SEQ,
                 lambda ns, out, ps, n, a, w, side: ns.tensor_tensor(x[:, bass.ds(n, 1), a:a + w], ps.unsqueeze(1), side.unsqueeze(1), ALU.add),
                 evac_on="vector", side_dram=R["xa"])
            norm_split(nc, "n6", x, SEQ, high, rest, lambda k: gains[:, 1, k:k + 1], None, C["ones"])
            feed_forward(nc, A, pair, x)
            norm_split(nc, "n7", x, SEQ, high, rest, lambda k: gains[:, 2, k:k + 1], None, C["ones"])
            gated_products(nc, "ple", A["w_ple"], 2, (high, rest), lambda b: A["pT"], 1, x)
            norm_channels(nc, "n8", x, SEQ, x, lambda k: gains[:, 3, k:k + 1], None, C["ones"])
            load(nc, "store", [(out, x[:])])


def branches(nc, A, R, merged, high, rest):
    with Stage(nc, "branch") as g:
        zeroed = g.sem("zeroed")
        with nc.Block() as block:
            @block.vector
            def _(dve):
                nc.vector.memset(merged[:], 0.0).then_inc(zeroed, 1)
                dve.wait_ge(zeroed, 1)
    gated_products(nc, "br", A["w_merge"], 4, (high, rest), lambda b: R["y"][4 * b:4 * b + 4].rearrange("k p t -> p k t"), 4, merged)


def feed_forward(nc, A, pair, x):
    with Stage(nc, "ff") as s:
        W = Weights(nc, s, A["w_ff"], D, 8 * KD)
        hidh, hidl = s.sb("hidh", [P, KD, SEQ], F32R), s.sb("hidl", [P, KD, SEQ], F32R)
        t = [s.sb(f"t{j}", [P, 1, SEQ]) for j in range(2)]
        ps = [s.ps(f"p{j}", [P, 2 * BANK]) for j in range(2)]
        taken, squared, rounded, left = s.sems("taken", 2), s.sem("squared"), s.sem("hid_rounded"), s.sems("left", 2)
        half = KD // 2
        with nc.Block() as block:
            @block.sync
            def _(sp):
                W.load(sp)

            @block.gpsimd
            def _(pool):
                W.halve(pool)

            @block.tensor
            def _(pe):
                def tiles_of(q, first, rhs):
                    with pe.Fori(0, half) as i:
                        for j in range(2):
                            pe.wait_ge(W.split[j], i + (q * KD + first + 1))
                            pe.wait_ge(taken[j], i + (q * KD + first))
                            for c in range(2):
                                for k in range(KD):
                                    mm = product3(nc, ps[j][:, c * BANK:(c + 1) * BANK], W.tile(j, k), rhs(k, c * BANK, BANK), k == 0, k == KD - 1)
                            mm.then_inc(W.used[j], 1)

                for q in range(4):
                    tiles_of(q, 0, pair)
                    for j in range(2):
                        pe.wait_ge(left[j], (q + 1) * half)
                    tiles_of(q, half, lambda k, a, m: (hidh[:, k, a:a + m], hidl[:, k, a:a + m]))

            @block.scalar
            def _(act):
                for q in range(4):
                    with act.Fori(0, half) as i:
                        for j in range(2):
                            n = i * 2 + j
                            act.wait_ge(W.used[j], i + (q * KD + 1))
                            act.wait_ge(left[j], i + q * half)
                            nc.scalar.activation(t[j][:], ps[j][:].unsqueeze(1), ACT.Relu).then_inc(taken[j], 1)
                            act.wait_ge(squared, n + q * KD + 1)
                            nc.scalar.activation(hidh[:, bass.ds(n, 1), :], t[j][:], ACT.Copy).then_inc(rounded, 1)

            @block.vector
            def _(dve):
                for q in range(4):
                    with dve.Fori(0, half) as i:
                        for j in range(2):
                            n = i * 2 + j
                            dve.wait_ge(taken[j], i + (q * KD + 1))
                            nc.vector.tensor_tensor(t[j][:], t[j][:], t[j][:], ALU.mult).then_inc(squared, 1)
                            dve.wait_ge(rounded, n + q * KD + 1)
                            nc.vector.tensor_tensor(hidl[:, bass.ds(n, 1), :], t[j][:], hidh[:, bass.ds(n, 1), :].bitcast(F32), ALU.subtract).then_inc(left[j], 1)
                    with dve.Fori(0, half) as i:
                        for j in range(2):
                            dve.wait_ge(W.used[j], i + (q * KD + half + 1))
                            onto = x[:, bass.ds(i * 2 + j, 1), :]
                            nc.vector.tensor_tensor(onto, onto, ps[j][:].unsqueeze(1), ALU.add).then_inc(taken[j], 1)


SCRATCH = dict(z_cm=(CM1, P, TOT), z_v=(2, TOT, 512), z_g=(2, SEQ, 512), mqk=(8, P, TOT),
               x1=(KD, P, SEQ), h2rows=(SEQ, D), yrows=(NBLK * SLOT, D),
               u=(N_U, P, SEQ), y=(16, P, SEQ), z2=(1, SEQ, MH * VH), xa=(KD, P, SEQ), xb=(KD, P, SEQ))


def program(nc, A, out):
    R = {k: nc.dram_tensor(k, shape, F32, kind="Internal").ap() for k, shape in SCRATCH.items()}
    R["slots"] = nc.dram_tensor("slots", ((NBLK + 1) * SLOT, 16), I32, kind="Internal").ap()
    with Stage(nc, "all") as s:
        C = {k: s.sb(k, shape, dt) for k, shape, dt in (
            ("keep", [P, 2, P], I32), ("cut", [P, 2, P], F32), ("cutq", [P, P], F32), ("ident", [P, P], F32),
            ("earlier", [P, P], F32))}
        load(nc, "consts", [(t[:], A[k]) for k, t in C.items()])
        C["ones"] = s.sb("ones", [P, P])
        filled = s.sem("filled")
        with nc.Block() as block:
            @block.vector
            def _(dve):
                nc.vector.memset(C["ones"][:], 1.0).then_inc(filled, 1)
                dve.wait_ge(filled, 1)
        first_block(nc, A, R, C)
        second_block(nc, A, R, C, out)


def tiles(w):
    k, n = w.shape
    return np.ascontiguousarray(w.reshape(k // P, P, n // P, P).transpose(2, 1, 0, 3)).reshape(n // P, P, k)


def slabs(w, width):
    k, n = w.shape
    return np.ascontiguousarray(w.reshape(k // P, P, n // width, width).transpose(2, 1, 0, 3)).reshape(n // width, P, -1)


def columns(v):
    return np.ascontiguousarray(v.reshape(-1, P).T)


def lay_out(I):
    A = {}
    A["xT"] = I["x"][0].T.reshape(KD, P, SEQ).transpose(1, 0, 2)
    A["ctxT"] = I["ctx"][0].T.reshape(KD, P, CTX).transpose(1, 0, 2)
    A["c2"] = np.stack([I["c"][0], I["c_ctx"]], -1).reshape(KD, P, 2).transpose(1, 0, 2)
    A["ada_w"] = slabs(I["ada_w"][0], BANK)
    A["ada_b"] = columns(I["ada_b"][0])
    A["norm1_g"] = columns(I["norm1_g"][0])
    w = I["w_in"][0]
    q, k, v, g, lr, mqk, mv, mo, mi, mf = np.split(w, np.cumsum([256, 256, 512, 512, 32, 1024, 512, 512, 8]), axis=1)
    small = np.zeros((D, 2 * P), w.dtype)
    small[:, 0:16], small[:, 32:48], small[:, 64:72], small[:, 96:104] = lr[:, :16], lr[:, 16:], mi, mf
    A["w_in_cm"] = tiles(np.concatenate([q, k, mqk, small], 1))
    A["w_in_v"] = slabs(np.concatenate([v, mv], 1), 512)
    A["w_in_g"] = slabs(np.concatenate([g, mo], 1), 512)
    A["conv_w"] = I["ml_conv_w"][0].reshape(9, 8, P).transpose(2, 1, 0)
    A["conv_b"] = columns(I["ml_conv_b"][0])
    A["conv_post"] = np.repeat(np.array([1.0] * 4 + [ML_D ** -0.5] * 4, np.float32)[None], P, 0)
    up = np.zeros((P, 2, P), np.float32)
    for d in range(2):
        up[32 * d:32 * d + 16] = I["gla_up_w"][0][d].reshape(16, 2, P)
    A["gla_up_w"] = up
    A["gla_up_b"] = I["gla_up_b"][0].reshape(4, P).T
    sm = np.ones((2, TOT), np.float32)
    sm[0, ::CH] = 0
    sm[1, CH - 1::CH] = 0
    A["scan_mask"] = sm
    gate = np.zeros((2, 64, 1), np.float32)
    for d in range(2):
        gate[0, 32 * d:32 * d + 4, 0], gate[1, 32 * d:32 * d + 4, 0] = I["ml_i_b"][0][d], I["ml_f_b"][0][d]
    A["ml_i_b"], A["ml_f_b"] = gate
    t = np.arange(P)
    keep = np.stack([t[:, None] <= t[None], t[:, None] >= t[None]], 1)
    A["keep"] = keep.astype(np.int32)
    A["cut"] = np.where(keep, 0.0, NEG).astype(np.float32)
    A["cutq"] = A["cut"][:, 1]
    A["ident"] = np.eye(P, dtype=np.float32)
    pick = np.zeros((64, 8, P), np.float32)
    for d in range(2):
        for n in range(4):
            pick[32 * d + n, 4 * d + n] = 1
    A["pick"] = pick
    A["earlier"] = (t[:, None] < t[None]).astype(np.float32)
    A["mix_g"] = columns(np.concatenate([I["gla_norm_g"][0], I["ml_norm_g"][0]]))
    A["w_out"] = tiles(I["w_out"][0])
    A["norm2_g"], A["final_g"] = columns(I["norm2_g"][0]), columns(I["final_norm_g"])
    A["router_w"] = np.concatenate([I["router_group_w"][0], I["router_expert_w"][0]], 1).reshape(KD, P, NG + NE).transpose(1, 0, 2)
    A["router_b"] = np.concatenate([I["router_group_b"][0], I["router_expert_b"][0]])[None]
    A["expert_ids"] = np.arange(NE, dtype=np.float32)[None]
    A["block_ids"] = np.arange(NBLK + 2, dtype=np.float32)[None]
    up = I["expert_w_in"][0].reshape(NE, 4, 2, P, 2, DE).transpose(0, 4, 1, 3, 2, 5).reshape(NE, 8, P, D)
    A["expert_w"] = np.concatenate([up, I["expert_w_out"][0].reshape(NE, 4, P, D)], 1).reshape(NE * 12, P, D)
    lay_out_second(I, A)
    return A


def lay_out_second(I, A):
    J = {k[:-2]: v for k, v in I.items() if k.endswith("_2")}
    w = J["w_in"][0]
    cq, ckv, kr, po, z, xbc, dt, lg, lx, gates = np.split(w, np.cumsum([384, 256, 32, 512, 512, 768, 8, 512, 512]), axis=1)
    last = np.zeros((D, P), w.dtype)
    last[:, NOPE:NOPE + ROPE], last[:, NOPE + ROPE:NOPE + ROPE + SH] = kr, dt
    A["w_in2"] = tiles(np.concatenate([cq, ckv, po, xbc, lg, lx, last], 1))
    A["w_in_z"] = slabs(z, 512)
    for k in ("g_mix", "g_mlp", "g_ple", "q_norm", "kv_norm", "pool_scale", "ssd_conv_b", "ssd_norm",
              "lru_conv_b", "lru_b_a", "lru_b_i", "lru_lambda"):
        A[k] = columns(J[k][0])
    A["g_final"] = columns(J["g_final"])
    A["positions"] = J["positions"]
    half = ROPE // 2
    inv = (np.float32(1.0) / np.power(np.float32(10000.0), np.arange(0, ROPE, 2, dtype=np.float32) / np.float32(ROPE))).astype(np.float32)
    A["rope_inv"] = np.zeros((P, 1), np.float32)
    A["rope_inv"][NOPE:NOPE + half, 0] = A["rope_inv"][NOPE + half:NOPE + ROPE, 0] = inv
    swap = np.zeros((P, P), np.float32)
    for n in range(half):
        swap[NOPE + half + n, NOPE + n], swap[NOPE + n, NOPE + half + n] = -1, 1
    A["swap"] = swap
    uq = np.zeros((QL, MH, P), w.dtype)
    uq[:, :, 0:NOPE + ROPE] = J["w_uq"][0].reshape(QL, MH, NOPE + ROPE)
    A["w_uq"] = tiles(uq.reshape(QL, MH * P))
    ukv = J["w_ukv"][0].reshape(KVL, MH, NOPE + VH)
    uk = np.zeros((KVL, MH, P), w.dtype)
    uk[:, :, 0:NOPE] = ukv[:, :, 0:NOPE]
    A["w_uk"] = tiles(uk.reshape(KVL, MH * P))
    A["w_uv"] = ukv[:, :, NOPE:].reshape(2, P, MH * VH).transpose(1, 0, 2)
    t = np.arange(SEQ)
    A["pool_inv"] = np.stack([np.float32(1.0) / np.minimum(t + 1, n).astype(np.float32) for n in (2, 4, 8, 16)])
    A["w_pool"] = J["w_pool"][0].transpose(1, 0, 2)
    A["ssd_conv_w"] = J["ssd_conv_w"][0].reshape(4, 6, P).transpose(2, 1, 0)
    for k in ("ssd_a_log", "ssd_dt_bias", "ssd_d"):
        A[k] = J[k]
    for k in ("lru_w_a", "lru_w_i"):
        blocks = np.zeros((P, 4, P), w.dtype)
        for n in range(8):
            r = slice(n % 2 * 64, n % 2 * 64 + 64)
            blocks[r, n // 2, r] = J[k][0][n]
        A[k] = blocks
    A["lru_conv_w"] = J["lru_conv_w"][0].reshape(4, 4, P).transpose(2, 1, 0)
    gate = tiles(gates).reshape(4, KD, P, D)
    branch = np.stack([tiles(J["w_branch"][0][n]) for n in range(4)])
    A["w_merge"] = np.concatenate([gate, branch], -1).reshape(4 * KD, P, -1)
    A["w_out2"] = tiles(J["w_out"][0])
    A["w_ff"] = np.concatenate([tiles(w) for q in range(4) for w in (np.split(J["w_ff1"][0], 4, 1)[q], np.split(J["w_ff2"][0], 4)[q])])
    A["w_ple"] = np.concatenate([tiles(J["w_ple_gate"][0]), tiles(J["w_ple"][0])], -1)
    A["pT"] = J["p"][0, 0].T.reshape(2, P, SEQ).transpose(1, 0, 2)




def kernel(**inputs):
    import concourse.bacc as bacc
    from concourse.bass_utils import run_bass_kernel_spmd

    nc = bacc.Bacc("TRN2", target_bir_lowering=False, num_devices=1)
    arrays = {"in_" + k: np.ascontiguousarray(v) for k, v in lay_out({k: np.asarray(v) for k, v in inputs.items()}).items()}
    A = {k[3:]: nc.dram_tensor(k, v.shape, mybir.dt.from_np(v.dtype), kind="ExternalInput").ap() for k, v in arrays.items()}
    out = nc.dram_tensor("out", (P, KD, SEQ), F32, kind="ExternalOutput").ap()
    program(nc, A, out)
    r = run_bass_kernel_spmd(nc, [arrays], core_ids=[0])
    return r.results[0]["out"].transpose(1, 0, 2).reshape(1, D, SEQ).transpose(0, 2, 1)
```
